# Optimizing a Trainium2 kernel written in Bass

```python
import jax, jax.numpy as jnp
from jax import lax
import numpy as np
import math

D_MODEL = 1024
BATCH = 1
SEQ = 512
DEPTH = 1

GRID_W = 64
CTX_LEN = 256
N_HEADS = 16
Q_RANK = 256
KV_RANK = 128
NOPE_DIM = 64
ROPE_DIM = 32
V_DIM = 64
ROPE_THETA = 10000.0
Q_BLOCK = 128
ATTN_SCALE = (NOPE_DIM + ROPE_DIM) ** -0.5
CONV_CH = D_MODEL
CONV_WIDTH = 31
CONV_HALF = CONV_WIDTH // 2
P_HEADS = 8
N_KEYS = 128
N_EXPERTS = N_KEYS * N_KEYS
P_DK = 256
P_TOPK = 16
P_CHUNK = 128
EPS = 1e-6

OFF_Q = 0
OFF_KV = Q_RANK
OFF_CONV = Q_RANK + KV_RANK + ROPE_DIM
OFF_GATE = OFF_CONV + 2 * CONV_CH
N_IN = OFF_GATE + 2 * D_MODEL


def rms_norm(x, g):
    xf = x.astype(jnp.float32)
    y = xf * lax.rsqrt(jnp.mean(xf * xf, axis=-1, keepdims=True) + EPS)
    return (y * g.astype(jnp.float32)).astype(x.dtype)

def layer_norm(x, g, b):
    xf = x.astype(jnp.float32)
    mu = jnp.mean(xf, axis=-1, keepdims=True)
    var = jnp.mean(jnp.square(xf - mu), axis=-1, keepdims=True)
    y = (xf - mu) * lax.rsqrt(var + EPS) * g.astype(jnp.float32) + b.astype(jnp.float32)
    return y.astype(x.dtype)

def modulate(h, shift, scale):
    return h * (1 + scale) + shift

def axial_rope_tables(n_tok):
    rows = n_tok // GRID_W
    r = jnp.repeat(jnp.arange(rows, dtype=jnp.int32), GRID_W)
    col = jnp.tile(jnp.arange(GRID_W, dtype=jnp.int32), rows)
    n_freq = ROPE_DIM // 4
    freq = ROPE_THETA ** (-jnp.arange(n_freq, dtype=jnp.float32) / n_freq)
    ang = jnp.stack([r[:, None] * freq, col[:, None] * freq], axis=1)
    return jnp.cos(ang), jnp.sin(ang)

def apply_rope(x, cos, sin):
    shp = x.shape
    xr = x.reshape(shp[:-1] + (2, 2, ROPE_DIM // 4)).astype(jnp.float32)
    extra = x.ndim - 3
    c = cos.reshape(cos.shape[:1] + (1,) * extra + cos.shape[1:])
    s = sin.reshape(sin.shape[:1] + (1,) * extra + sin.shape[1:])
    x1, x2 = xr[..., 0, :], xr[..., 1, :]
    out = jnp.stack([x1 * c - x2 * s, x2 * c + x1 * s], axis=-2)
    return out.reshape(shp).astype(x.dtype)

def mla_queries(cq, q_norm_g, w_uq):
    b, n, _ = cq.shape
    q = (rms_norm(cq, q_norm_g) @ w_uq).reshape(b, n, N_HEADS, NOPE_DIM + ROPE_DIM)
    return q[..., :NOPE_DIM], q[..., NOPE_DIM:]

def mla_keys(kvr, kv_norm_g, w_ukv):
    b, n, _ = kvr.shape
    c_kv = rms_norm(kvr[..., :KV_RANK], kv_norm_g)
    kv = (c_kv @ w_ukv).reshape(b, n, N_HEADS, NOPE_DIM + V_DIM)
    return kv[..., :NOPE_DIM], kvr[..., KV_RANK:], kv[..., NOPE_DIM:]

def attend(qn, qr, kn, kr, v):
    s = jnp.einsum('bqhd,bkhd->bhqk', qn, kn) + jnp.einsum('bqhd,bkd->bhqk', qr, kr)
    p = jax.nn.softmax(s.astype(jnp.float32) * ATTN_SCALE, axis=-1).astype(v.dtype)
    return jnp.einsum('bhqk,bkhd->bqhd', p, v)

def attend_blocked(qn, qr, kn, kr, v):
    b, n = qn.shape[:2]
    nb = n // Q_BLOCK
    blk = lambda t: jnp.moveaxis(t.reshape((b, nb, Q_BLOCK) + t.shape[2:]), 1, 0)
    out = lax.map(lambda qs: attend(qs[0], qs[1], kn, kr, v), (blk(qn), blk(qr)))
    return jnp.moveaxis(out, 0, 1).reshape(b, n, N_HEADS, V_DIM)

def conformer_conv(u, conv_w, conv_b, ln_g, ln_b, w_pw):
    a, g = jnp.split(u, 2, axis=-1)
    y = a * jax.nn.sigmoid(g)
    y = lax.conv_general_dilated(y, conv_w[:, None, :], window_strides=(1,),
                                 padding=[(CONV_HALF, CONV_HALF)],
                                 dimension_numbers=('NWC', 'WIO', 'NWC'),
                                 feature_group_count=CONV_CH) + conv_b
    y = jax.nn.silu(layer_norm(y, ln_g, ln_b))
    return y @ w_pw

def merge_branches(u, attn_heads, conv_w, conv_b, ln_g, ln_b, w_pw, w_o_mla, w_out):
    b, n = attn_heads.shape[:2]
    y_a = attn_heads.reshape(b, n, N_HEADS * V_DIM) @ w_o_mla
    y_c = conformer_conv(u[..., OFF_CONV:OFF_GATE], conv_w, conv_b, ln_g, ln_b, w_pw)
    g = jax.nn.sigmoid(u[..., OFF_GATE:])
    return (g[..., :D_MODEL] * y_a + g[..., D_MODEL:] * y_c) @ w_out

def peer_ffn(h, w_pq, sub_keys, u_tab, v_tab):
    shp = h.shape
    toks = h.reshape(-1, P_CHUNK, D_MODEL)

    def chunk(xc):
        q = (xc @ w_pq).reshape(P_CHUNK, P_HEADS, 2, P_DK // 2)
        s = jnp.einsum('thpd,hpkd->thpk', q, sub_keys)
        s_top, i_top = lax.top_k(s, P_TOPK)
        cand = s_top[..., 0, :, None] + s_top[..., 1, None, :]
        best, ci = lax.top_k(cand.reshape(P_CHUNK, P_HEADS, P_TOPK * P_TOPK), P_TOPK)
        e1 = jnp.take_along_axis(i_top[..., 0, :], ci // P_TOPK, axis=-1)
        e2 = jnp.take_along_axis(i_top[..., 1, :], ci % P_TOPK, axis=-1)
        expert = e1 * N_KEYS + e2
        gate = jax.nn.softmax(best.astype(jnp.float32), axis=-1).astype(xc.dtype)
        act = jax.nn.gelu(jnp.einsum('thkd,td->thk', u_tab[expert], xc), approximate=False)
        return jnp.einsum('thk,thkd->td', gate * act, v_tab[expert])

    return lax.map(chunk, toks).reshape(shp)

def first_inputs(seed: int = 0) -> dict:
    key = jax.random.key(seed)
    ks = jax.random.split(key, 30)
    nrm = lambda k, s, sc: jax.random.normal(k, s, jnp.float32) * sc
    D = D_MODEL
    return {
        "x": nrm(ks[0], (BATCH, SEQ, D), 1.0),
        "c": nrm(ks[1], (BATCH, D), 1.0),
        "ctx": nrm(ks[2], (BATCH, CTX_LEN, D), 1.0),
        "c_ctx": nrm(ks[3], (D,), 1.0),
        "w_mod": nrm(ks[4], (DEPTH, D, 6 * D), 0.5 * D ** -0.5),
        "b_mod": nrm(ks[5], (DEPTH, 6 * D), 0.01),
        "norm1_g": 1.0 + nrm(ks[6], (DEPTH, D), 0.02),
        "norm2_g": 1.0 + nrm(ks[7], (DEPTH, D), 0.02),
        "w_in": nrm(ks[8], (DEPTH, D, N_IN), D ** -0.5),
        "q_norm_g": 1.0 + nrm(ks[9], (DEPTH, Q_RANK), 0.02),
        "w_uq": nrm(ks[10], (DEPTH, Q_RANK, N_HEADS * (NOPE_DIM + ROPE_DIM)), Q_RANK ** -0.5),
        "kv_norm_g": 1.0 + nrm(ks[11], (DEPTH, KV_RANK), 0.02),
        "w_ukv": nrm(ks[12], (DEPTH, KV_RANK, N_HEADS * (NOPE_DIM + V_DIM)), KV_RANK ** -0.5),
        "w_o_mla": nrm(ks[13], (DEPTH, N_HEADS * V_DIM, D), (N_HEADS * V_DIM) ** -0.5),
        "conv_w": nrm(ks[14], (DEPTH, CONV_WIDTH, CONV_CH), CONV_WIDTH ** -0.5),
        "conv_b": nrm(ks[15], (DEPTH, CONV_CH), 0.01),
        "conv_ln_g": 1.0 + nrm(ks[16], (DEPTH, CONV_CH), 0.02),
        "conv_ln_b": nrm(ks[17], (DEPTH, CONV_CH), 0.01),
        "w_pw": nrm(ks[18], (DEPTH, CONV_CH, D), CONV_CH ** -0.5),
        "w_out": nrm(ks[19], (DEPTH, D, D), D ** -0.5),
        "w_pq": nrm(ks[20], (DEPTH, D, P_HEADS * P_DK), D ** -0.5),
        "sub_keys": nrm(ks[21], (DEPTH, P_HEADS, 2, N_KEYS, P_DK // 2), (P_DK // 2) ** -0.5),
        "u_experts": nrm(ks[22], (DEPTH, N_EXPERTS, D), D ** -0.5),
        "v_experts": nrm(ks[23], (DEPTH, N_EXPERTS, D), 1.0),
        "final_g": 1.0 + nrm(ks[24], (D,), 0.02),
    }

def first_block(x, c, ctx, c_ctx, w_mod, b_mod, norm1_g, norm2_g, w_in, q_norm_g, w_uq,
              kv_norm_g, w_ukv, w_o_mla, conv_w, conv_b, conv_ln_g, conv_ln_b, w_pw,
              w_out, w_pq, sub_keys, u_experts, v_experts, final_g):
    n_lat = x.shape[1]
    cos, sin = axial_rope_tables(n_lat)
    for l in range(DEPTH):
        last = l == DEPTH - 1
        mod_lat = (jax.nn.silu(c) @ w_mod[l] + b_mod[l])[:, None, :]
        mod_ctx = jax.nn.silu(c_ctx) @ w_mod[l] + b_mod[l]
        sh1, sc1, g1, sh2, sc2, g2 = jnp.split(mod_lat, 6, axis=-1)
        csh1, csc1, cg1, csh2, csc2, cg2 = jnp.split(mod_ctx, 6, axis=-1)

        h = modulate(rms_norm(x, norm1_g[l]), sh1, sc1)
        u = h @ w_in[l]
        qn, qr = mla_queries(u[..., OFF_Q:OFF_KV], q_norm_g[l], w_uq[l])
        qr = apply_rope(qr, cos, sin)
        kn_l, kr_l, v_l = mla_keys(u[..., OFF_KV:OFF_CONV], kv_norm_g[l], w_ukv[l])
        kr_l = apply_rope(kr_l, cos, sin)

        hc = modulate(rms_norm(ctx, norm1_g[l]), csh1, csc1)
        if last:
            uc = hc @ w_in[l][:, OFF_KV:OFF_CONV]
            kvr_c = uc
        else:
            uc = hc @ w_in[l]
            kvr_c = uc[..., OFF_KV:OFF_CONV]
        kn_c, kr_c, v_c = mla_keys(kvr_c, kv_norm_g[l], w_ukv[l])

        kn = jnp.concatenate([kn_l, kn_c], axis=1)
        kr = jnp.concatenate([kr_l, kr_c], axis=1)
        vv = jnp.concatenate([v_l, v_c], axis=1)
        attn_lat = attend_blocked(qn, qr, kn, kr, vv)
        x = x + g1 * merge_branches(u, attn_lat, conv_w[l], conv_b[l], conv_ln_g[l],
                                    conv_ln_b[l], w_pw[l], w_o_mla[l], w_out[l])
        if not last:
            qn_c, qr_c = mla_queries(uc[..., OFF_Q:OFF_KV], q_norm_g[l], w_uq[l])
            attn_c = attend(qn_c, qr_c, kn_c, kr_c, v_c)
            ctx = ctx + cg1 * merge_branches(uc, attn_c, conv_w[l], conv_b[l], conv_ln_g[l],
                                             conv_ln_b[l], w_pw[l], w_o_mla[l], w_out[l])

        h2 = modulate(rms_norm(x, norm2_g[l]), sh2, sc2)
        x = x + g2 * peer_ffn(h2, w_pq[l], sub_keys[l], u_experts[l], v_experts[l])
        if not last:
            hc2 = modulate(rms_norm(ctx, norm2_g[l]), csh2, csc2)
            ctx = ctx + cg2 * peer_ffn(hc2, w_pq[l], sub_keys[l], u_experts[l], v_experts[l])
    return rms_norm(x, final_g)


DEPTH_2 = 2

N_MIXERS = 2
N_A = (DEPTH_2 + 1) // 2
N_B = DEPTH_2 // 2
A_HEADS = 16
A_QK_DIM = 64
A_V_DIM = 64
A_KV_RANK = 256
IDX_HEADS = 8
IDX_DIM = 64
TOPK_MAX = 256
A_SPLITS = [A_HEADS * A_QK_DIM,
            A_HEADS * A_QK_DIM + A_KV_RANK,
            A_HEADS * A_QK_DIM + A_KV_RANK + IDX_HEADS * IDX_DIM,
            A_HEADS * A_QK_DIM + A_KV_RANK + IDX_HEADS * IDX_DIM + IDX_DIM]
A_IN = A_SPLITS[-1] + IDX_HEADS
B_HEADS = 8
B_HEAD_DIM = 64
B_QK = 2 * B_HEADS * B_HEAD_DIM
B_IN = 3 * B_QK
REL_BUCKETS = 32
REL_MAX_DIST = 128
BIAS_HEADS = A_HEADS
D_FF = 4 * D_MODEL
LN_EPS = 1e-5
NEG = -1e30
DN_ALPHA = (2 * DEPTH_2) ** 0.25
DN_BETA = (8 * DEPTH_2) ** -0.25


def _layer_norm(x, g, b):
    xf = x.astype(jnp.float32)
    mu = jnp.mean(xf, -1, keepdims=True)
    var = jnp.mean(jnp.square(xf - mu), -1, keepdims=True)
    return ((xf - mu) * lax.rsqrt(var + LN_EPS)).astype(x.dtype) * g + b

def _rms_norm(x, g):
    xf = x.astype(jnp.float32)
    return (xf * lax.rsqrt(jnp.mean(xf * xf, -1, keepdims=True) + LN_EPS)).astype(x.dtype) * g

def _rel_bucket(dist):
    n = jnp.maximum(dist, 0)
    max_exact = REL_BUCKETS // 2
    nf = jnp.maximum(n, 1).astype(jnp.float32)
    large = max_exact + (jnp.log(nf / max_exact) / math.log(REL_MAX_DIST / max_exact)
                         * (REL_BUCKETS - max_exact)).astype(jnp.int32)
    large = jnp.minimum(large, REL_BUCKETS - 1)
    return jnp.where(n < max_exact, n, large)

def _to_blocks(a):
    B, S = a.shape[:2]
    return jnp.moveaxis(a.reshape(B, S // Q_BLOCK, Q_BLOCK, *a.shape[2:]), 1, 0)

def _from_blocks(a):
    nb, B, Q = a.shape[:3]
    return jnp.moveaxis(a, 0, 1).reshape(B, nb * Q, *a.shape[3:])

def _dsa_mixer(h, w_in, kv_norm, w_uk, w_uv, w_o, rel_bias):
    B, S, _ = h.shape
    topk = min(TOPK_MAX, S // 4)
    proj = h @ w_in
    q, ckv, iq, ik, iw = jnp.split(proj, A_SPLITS, axis=-1)
    q = q.reshape(B, S, A_HEADS, A_QK_DIM)
    ckv = _rms_norm(ckv, kv_norm)
    iq = iq.reshape(B, S, IDX_HEADS, IDX_DIM)
    iw = iw * (IDX_HEADS ** -0.5 * IDX_DIM ** -0.5)
    pos = jnp.arange(S, dtype=jnp.int32)

    def block(args):
        qb, iqb, iwb, tpos = args
        idx_logits = jnp.einsum('bqhd,bsd->bhqs', iqb, ik).astype(jnp.float32)
        score = jnp.einsum('bhqs,bqh->bqs', jax.nn.relu(idx_logits), iwb.astype(jnp.float32))
        causal = pos[None, :] <= tpos[:, None]
        score = jnp.where(causal[None], score, -jnp.inf)
        _, sel = lax.top_k(score, topk)
        valid = sel <= tpos[None, :, None]
        kv_sel = jax.vmap(lambda cb, ib: cb[ib])(ckv, sel)
        q_lat = jnp.einsum('bqhd,hdr->bqhr', qb, w_uk) * (A_QK_DIM ** -0.5)
        logits = jnp.einsum('bqhr,bqkr->bhqk', q_lat, kv_sel).astype(jnp.float32)
        bias = rel_bias[_rel_bucket(tpos[None, :, None] - sel)]
        logits = logits + jnp.transpose(bias, (0, 3, 1, 2))
        logits = jnp.where(valid[:, None], logits, NEG)
        p = jax.nn.softmax(logits, axis=-1).astype(h.dtype)
        o_lat = jnp.einsum('bhqk,bqkr->bqhr', p, kv_sel)
        return jnp.einsum('bqhr,hrd->bqhd', o_lat, w_uv)

    o = lax.map(block, (_to_blocks(q), _to_blocks(iq), _to_blocks(iw),
                        pos.reshape(S // Q_BLOCK, Q_BLOCK)))
    o = _from_blocks(o)
    return o.reshape(B, S, A_HEADS * A_V_DIM) @ w_o

def _diff_mixer(h, w_in, lam, subln_g, w_o, rel_bias, layer_idx):
    B, S, _ = h.shape
    lam_init = 0.8 - 0.6 * math.exp(-0.3 * layer_idx)
    proj = h @ w_in
    q, k, v = jnp.split(proj, 3, axis=-1)
    q = q.reshape(B, S, B_HEADS, 2, B_HEAD_DIM) * (B_HEAD_DIM ** -0.5)
    k = k.reshape(B, S, B_HEADS, 2, B_HEAD_DIM)
    v = v.reshape(B, S, B_HEADS, 2 * B_HEAD_DIM)
    lam_f = lam.astype(jnp.float32)
    lam_full = (jnp.exp(jnp.sum(lam_f[0] * lam_f[1])) - jnp.exp(jnp.sum(lam_f[2] * lam_f[3]))
                + lam_init)
    pos = jnp.arange(S, dtype=jnp.int32)

    def block(args):
        qb, tpos = args
        logits = jnp.einsum('bqhmd,bshmd->bhmqs', qb, k).astype(jnp.float32)
        bias = rel_bias[_rel_bucket(tpos[:, None] - pos[None, :])]
        bias = jnp.transpose(bias.reshape(Q_BLOCK, S, B_HEADS, 2), (2, 3, 0, 1))
        causal = pos[None, :] <= tpos[:, None]
        logits = jnp.where(causal, logits + bias, NEG)
        p = jax.nn.softmax(logits, axis=-1)
        a = p[:, :, 0] - lam_full * p[:, :, 1]
        return jnp.einsum('bhqs,bshe->bqhe', a.astype(h.dtype), v)

    o = _from_blocks(lax.map(block, (_to_blocks(q), pos.reshape(S // Q_BLOCK, Q_BLOCK))))
    o = _rms_norm(o, subln_g) * (1.0 - lam_init)
    return o.reshape(B, S, B_HEADS * 2 * B_HEAD_DIM) @ w_o

def _sqrelu_mlp(h, w1, w2):
    return jnp.square(jax.nn.relu(h @ w1)) @ w2

def second_inputs(seed: int = 0) -> dict:
    key = jax.random.key(seed)
    ks = jax.random.split(key, 20)
    nrm = lambda k, shape, s: jax.random.normal(k, shape, jnp.float32) * s
    D = D_MODEL
    b_w_in = nrm(ks[10], (N_B, D, B_IN), D ** -0.5)
    b_w_in = b_w_in.at[..., 2 * B_QK:].multiply(DN_BETA)
    return {
        'x': nrm(ks[0], (BATCH, SEQ, D), 1.0),
        'c': nrm(ks[1], (BATCH, D), 1.0),
        'rel_bias': nrm(ks[2], (REL_BUCKETS, BIAS_HEADS), 0.5),
        'ada_w': nrm(ks[3], (DEPTH_2, D, 6 * D), 0.1 * D ** -0.5),
        'ada_b': nrm(ks[4], (DEPTH_2, 6 * D), 0.01),
        'ln_g': 1.0 + nrm(ks[5], (DEPTH_2, 2, D), 0.02),
        'ln_b': nrm(ks[6], (DEPTH_2, 2, D), 0.02),
        'a_w_in': nrm(ks[7], (N_A, D, A_IN), D ** -0.5),
        'a_kv_norm': 1.0 + nrm(ks[8], (N_A, A_KV_RANK), 0.02),
        'a_w_uk': nrm(ks[9], (N_A, A_HEADS, A_QK_DIM, A_KV_RANK), A_KV_RANK ** -0.5),
        'a_w_uv': nrm(ks[11], (N_A, A_HEADS, A_KV_RANK, A_V_DIM), DN_BETA * A_KV_RANK ** -0.5),
        'a_w_o': nrm(ks[12], (N_A, A_HEADS * A_V_DIM, D), DN_BETA * (A_HEADS * A_V_DIM) ** -0.5),
        'b_w_in': b_w_in,
        'b_lambda': nrm(ks[13], (N_B, 4, B_HEAD_DIM), 0.1),
        'b_subln': 1.0 + nrm(ks[14], (N_B, 2 * B_HEAD_DIM), 0.02),
        'b_w_o': nrm(ks[15], (N_B, B_QK, D), DN_BETA * B_QK ** -0.5),
        'mlp_w1': nrm(ks[16], (DEPTH_2, D, D_FF), D ** -0.5),
        'mlp_w2': nrm(ks[17], (DEPTH_2, D_FF, D), DN_BETA * D_FF ** -0.5),
    }

def second_block(x, c, rel_bias, ada_w, ada_b, ln_g, ln_b,
              a_w_in, a_kv_norm, a_w_uk, a_w_uv, a_w_o,
              b_w_in, b_lambda, b_subln, b_w_o,
              mlp_w1, mlp_w2):
    mod = jnp.einsum('bd,lde->lbe', jax.nn.silu(c), ada_w) + ada_b[:, None]
    for i in range(DEPTH_2):
        sh_t, sc_t, g_t, sh_c, sc_c, g_c = [m[:, None] for m in jnp.split(mod[i], 6, axis=-1)]
        h = x * (1.0 + sc_t) + sh_t
        j = i // N_MIXERS
        if i % N_MIXERS == 0:
            y = _dsa_mixer(h, a_w_in[j], a_kv_norm[j], a_w_uk[j], a_w_uv[j], a_w_o[j], rel_bias)
        else:
            y = _diff_mixer(h, b_w_in[j], b_lambda[j], b_subln[j], b_w_o[j], rel_bias, i)
        x = _layer_norm(DN_ALPHA * x + (1.0 + g_t) * y, ln_g[i, 0], ln_b[i, 0])
        h = x * (1.0 + sc_c) + sh_c
        y = _sqrelu_mlp(h, mlp_w1[i], mlp_w2[i])
        x = _layer_norm(DN_ALPHA * x + (1.0 + g_c) * y, ln_g[i, 1], ln_b[i, 1])
    return x


def setup_inputs(seed=0):
    out = dict(first_inputs(seed))
    for name, value in second_inputs(seed + 1).items():
        if name != "x":
            out[name + "_2"] = value
    return out


def reference(
    x, c, ctx, c_ctx, w_mod, b_mod, norm1_g, norm2_g, w_in, q_norm_g, w_uq, kv_norm_g, w_ukv,
    w_o_mla, conv_w, conv_b, conv_ln_g, conv_ln_b, w_pw, w_out, w_pq, sub_keys, u_experts,
    v_experts, final_g, c_2, rel_bias_2, ada_w_2, ada_b_2, ln_g_2, ln_b_2, a_w_in_2,
    a_kv_norm_2, a_w_uk_2, a_w_uv_2, a_w_o_2, b_w_in_2, b_lambda_2, b_subln_2, b_w_o_2,
    mlp_w1_2, mlp_w2_2,
):
    x = first_block(
        x, c, ctx, c_ctx, w_mod, b_mod, norm1_g, norm2_g, w_in, q_norm_g, w_uq, kv_norm_g,
        w_ukv, w_o_mla, conv_w, conv_b, conv_ln_g, conv_ln_b, w_pw, w_out, w_pq, sub_keys,
        u_experts, v_experts, final_g,
    )
    return second_block(
        x, c_2, rel_bias_2, ada_w_2, ada_b_2, ln_g_2, ln_b_2, a_w_in_2, a_kv_norm_2, a_w_uk_2,
        a_w_uv_2, a_w_o_2, b_w_in_2, b_lambda_2, b_subln_2, b_w_o_2, mlp_w1_2, mlp_w2_2,
    )


_drawn_inputs = setup_inputs


def setup_inputs(seed=0):
    import zlib

    import numpy as np

    out = dict(_drawn_inputs(seed))
    spreads = {}
    factors = {'ctx': 3.555,
     'norm1_g': 5.769,
     'q_norm_g': 8.0,
     'kv_norm_g': 8.0,
     'conv_b': 6.969,
     'conv_ln_g': 5.741,
     'conv_ln_b': 8.0,
     'ada_b_2': 3.517,
     'a_kv_norm_2': 8.0,
     'b_subln_2': 8.0}
    for name, (base, spread) in spreads.items():
        noise = np.random.default_rng([zlib.crc32(name.encode()), seed]).standard_normal(out[name].shape)
        drawn = base * np.exp(spread * noise) if base else spread * noise
        out[name] = __import__('jax').numpy.asarray(drawn.astype(out[name].dtype))
    for name, factor in factors.items():
        out[name] = (out[name] * factor).astype(out[name].dtype)
    return out
```

```python
from contextlib import ExitStack

import numpy as np
import concourse.bass as bass
from concourse import mybir

F32 = mybir.dt.float32
F32R = mybir.dt.float32r
U32 = mybir.dt.uint32
ACT = mybir.ActivationFunctionType
ALU = mybir.AluOpType
AX = mybir.AxisListType

P = 128
D = 1024
KC = D // P
T = 512
TC = 256
TB = T // P
KEYS = T + TC
HEADS = 16
PAIRS = HEADS // 2
NOPE, ROPE, VD = 64, 32, 64
QK = NOPE + ROPE
CONV_W = 31
HALF_W = CONV_W // 2
PEER_H, TOPK, NK = 8, 16, 128
IDX_H = 8
SEL = 128
FF = 4096
EPS1, EPS2 = 1e-6, 1e-5
NEG = -1e30
LOWEST = -3.0e38
TAKEN = -1.0e38
SCALE1 = float(QK) ** -0.5
SCALE2 = 64.0 ** -0.5
IW_SCALE = float(IDX_H) ** -0.5 * 64.0 ** -0.5
ALPHA = 4.0 ** 0.25
LAM_INIT = 0.8 - 0.6 * float(np.exp(-0.3))
BUCKETS = 32
GRID_W = 64

RING = 4
AHEAD = 3

R_IN = 0
R_CONV = 1
R_GATE = R_CONV + 4
R_MLA = R_GATE + 4
R_WO = R_MLA + 2
R_PW = R_WO + 2
R_OUT = R_PW + 2
R_PQ = R_OUT + 2
R_UV = R_PQ + 4
R_DSA_IN = R_UV + 64
R_DSA = R_DSA_IN + 2
R_AWO = R_DSA + 4
R_MLP1 = R_AWO + 2
R_DIFF = R_MLP1 + 16
R_BWO = R_DIFF + 6
R_MLP2 = R_BWO + 2
ROUNDS = R_MLP2 + 16
CHUNK_ROUNDS = NK // RING

MOD_UP = 16
MODS = 48 + 96

_cols = {}
_at = 0
for _name, _n in [("c", 8 * 4), ("b_mod", 48), ("ada_b", 96), ("norm1_g", 8), ("norm2_g", 8),
                  ("q_norm_g", 2), ("kv_norm_g", 1), ("conv_w", 8 * CONV_W), ("conv_b", 8),
                  ("conv_ln_g", 8), ("conv_ln_b", 8), ("final_g", 8), ("ln_g", 32), ("ln_b", 32),
                  ("a_kv_norm", 2), ("b_subln", 1)]:
    _cols[_name] = _at
    _at += _n
PACK = _at
BIAS_Z = 640


def build(nc, w_all, w_mods, x_t, ctx_t, pack, trig, sub_keys, rel_bias, bias_hot, b_lambda, out, stop=99):
    gates_dram = nc.dram_tensor("gates_scratch", [16, P, T], F32).ap()
    peer_gate_dram = nc.dram_tensor("peer_gate_scratch", [16, P, P * 32], F32).ap()
    bias_row_dram = nc.dram_tensor("bias_row_scratch", [HEADS, P, BIAS_Z], F32)
    bias_rows = bias_row_dram.ap()

    with ExitStack() as ctx:
        def sem(name):
            return ctx.enter_context(nc.semaphore(name))

        base = (nc.sbuf_base + 127) // 128 * 128

        def at(kb, name, shape, dt=F32):
            return nc.alloc_sbuf_tensor_at(name, shape, dt, offset=base + int(kb * 1024))

        raw = [at(4 * j, f"raw{j}", [P, 8, P]) for j in range(RING)]
        w_hi = [at(16 + 4 * j, f"w_hi{j}", [P, 8, P], F32R) for j in range(RING)]
        w_lo = [at(32 + 4 * j, f"w_lo{j}", [P, 8, P], F32R) for j in range(RING)]
        mod_raw = [at(48 + 4 * j, f"mod_raw{j}", [P, 8, P]) for j in range(2)]
        X = at(56, "X", [P, KC, T])
        RH = at(72, "RH", [P, KC, T], F32R)
        RL = at(88, "RL", [P, KC, T], F32R)
        sq = [at(104 + 2 * j, f"sq{j}", [P, T]) for j in range(2)]
        root = at(108, "root", [P, T])
        rinv = at(110, "rinv", [P, T])
        t_sb = [at(112 + 2 * j, f"t_sb{j}", [P, T]) for j in range(2)]
        f_sb = [at(116 + 2 * j, f"f_sb{j}", [P, T]) for j in range(2)]
        pk = at(120, "pk", [P, PACK])
        ident = at(122.5, "ident", [P, P])
        ones = at(123, "ones", [P, P])
        MOD = at(123.5, "MOD", [P, 48, 2])
        MOD2 = at(123.875, "MOD2", [P, 96])
        gain = at(124.25, "gain", [P, 8, 2])
        eps = at(124.375, "eps", [P, 2])
        nmax = at(124.4375, "nmax", [P, 2])
        psum_row = at(124.5, "psum_row", [P, 2])
        rrow = at(124.5625, "rrow", [P, 2])
        lam = at(124.625, "lam", [P, 8])
        cvec = at(124.6875, "cvec", [P, 8, 4])
        iota = at(125, "iota", [P, P])
        S = 125.5

        ypad = at(S, "ypad", [P, KC, T + 2 * HALF_W])
        KT = [at(S + 17 + 3 * m, f"KT{m}", [P, KEYS]) for m in range(2)]
        CQH = at(S + 23, "CQH", [P, 2, T], F32R)
        CQL = at(S + 27, "CQL", [P, 2, T], F32R)
        CKH = at(S + 31, "CKH", [P, KEYS], F32R)
        CKL = at(S + 34, "CKL", [P, KEYS], F32R)
        trig_sb = at(S + 37, "trig_sb", [P, T])
        CX = at(S + 39, "CX", [P, KC, TC])
        CH = at(S + 47, "CH", [P, KC, TC], F32R)
        CL = at(S + 55, "CL", [P, KC, TC], F32R)
        cqT = at(S + 63, "cqT", [P, 2, T])
        ckvT = at(S + 67, "ckvT", [P, KEYS])
        sig = [at(S + 70 + 2 * j, f"sig{j}", [P, T]) for j in range(2)]
        QT = [at(S + 39 + 2 * m, f"QT{m}", [P, T]) for m in range(2)]
        VT = at(S + 43, "VT", [P, KEYS])
        Vk = at(S + 46, "Vk", [P, 6, P])
        Pm = [at(S + 49 + 3 * j, f"Pm{j}", [P, KEYS]) for j in range(2)]
        PT = at(S + 55, "PT", [P, 6, T])
        Mg = at(S + 17, "Mg", [P, KC, T])
        gate_sb = at(S + 33, "gate_sb", [P, KC, T])
        VH = at(S + 49, "VH", [P, KC, T], F32R)
        VL = at(S + 65, "VL", [P, KC, T], F32R)
        SK = at(S, "SK", [P, 16, P])
        qs = [at(S + 8 + 2 * j, f"qs{j}", [P, T]) for j in range(2)]
        left = at(S + 12, "left", [P, TB, NK])
        cand = at(S + 14, "cand", [P, TB, 256])
        cand2 = at(S + 18, "cand2", [P, TB, 256])
        hit = at(S + 22, "hit", [P, TB, 256])
        top_v = [at(S + 26 + m / 4, f"top_v{m}", [P, TB, TOPK]) for m in range(2)]
        top_i = [at(S + 26.5 + m / 4, f"top_i{m}", [P, TB, TOPK], U32) for m in range(2)]
        top_f = [at(S + 27 + m / 4, f"top_f{m}", [P, TB, TOPK]) for m in range(2)]
        best = at(S + 27.5, "best", [P, TB, TOPK])
        best_i = at(S + 27.75, "best_i", [P, TB, TOPK], U32)
        half_i = [at(S + 28 + m / 4, f"half_i{m}", [P, TB, TOPK], U32) for m in range(2)]
        half_f = [at(S + 28.5 + m / 4, f"half_f{m}", [P, TB, TOPK]) for m in range(2)]
        zsum = at(S + 29, "zsum", [P, TB * PEER_H])
        zmax = at(S + 29.25, "zmax", [P, TB * PEER_H])
        E = [at(S + 76 + 2 * m, f"E{m}", [P, TB, PEER_H, TOPK]) for m in range(3)]
        Gs = [at(S + 16 * j, f"Gs{j}", [P, P, 32]) for j in range(2)]
        A1 = [at(S + 54 + 4 * j, f"A1_{j}", [P, 8, P]) for j in range(2)]
        B1 = [at(S + 62 + 4 * j, f"B1_{j}", [P, 8, P]) for j in range(2)]
        ET = [at(S + 70 + 2 * m, f"ET{m}", [P, T]) for m in range(3)]
        Y = at(S, "Y", [P, KC, T])
        GL = [at(S + 16 + 8 * j, f"GL{j}", [P, 16, P]) for j in range(2)]
        WH = [at(S + 32 + 8 * j, f"WH{j}", [P, RING, T], F32R) for j in range(2)]
        WL = [at(S + 48 + 8 * j, f"WL{j}", [P, RING, T], F32R) for j in range(2)]
        ge = [at(S + 64 + 2 * j, f"ge{j}", [P, T]) for j in range(2)]
        wf = [at(S + 68 + 2 * j, f"wf{j}", [P, T]) for j in range(2)]
        KVH = at(S, "KVH", [P, 2, T], F32R)
        KVL = at(S + 4, "KVL", [P, 2, T], F32R)
        M = [None] + [at(S + 8 + 2 * b, f"M{b + 1}", [P, T]) for b in range(3)]
        kvT = at(S + 14, "kvT", [P, 2, T])
        iqT = at(S + 18, "iqT", [P, 4, T])
        ikT = at(S + 26, "ikT", [P, T])
        iwT = at(S + 28, "iwT", [P, T])
        IW = at(S + 30, "IW", [P, TB, IDX_H])
        top8 = at(S + 30.25, "top8", [P, 4, 8])
        score = [None] + [at(S + 31 + 2 * b, f"score{b + 1}", [P, T]) for b in range(3)]
        hotz = at(S + 40, "hotz", [BUCKETS + 1, BIAS_Z])
        relb = at(S + 43, "relb", [BUCKETS + 1, HEADS])
        lb_sb = at(S + 34, "lb_sb", [P, 256])
        brow = at(S + 44, "brow", [HEADS, BIAS_Z])
        Tb = [at(S + 14 + 2 * j, f"Tb{j}", [P, T]) for j in range(4)]
        q2 = at(S + 22, "q2", [P, T])
        k2 = at(S + 24, "k2", [P, T])
        vT2 = at(S + 26, "vT2", [P, T])
        v2 = at(S + 28, "v2", [P, TB, P])
        ss = [at(S + 30 + 2 * j, f"ss{j}", [P, T]) for j in range(2)]
        P2 = [at(S + 34 + 2 * j, f"P2_{j}", [P, T]) for j in range(2)]
        PT2 = at(S + 38, "PT2", [P, TB, T])
        OH = at(S + 46, "OH", [P, KC, T], F32R)
        OL = at(S + 62, "OL", [P, KC, T], F32R)
        HH = at(S, "HH", [P, 16, T], F32R)
        HL = at(S + 32, "HL", [P, 16, T], F32R)
        Y2 = at(S + 64, "Y2", [P, KC, T])

        ps = ctx.enter_context(nc.psum_tensor("ps", [P, 8, T], F32))
        psf = ps[:].rearrange("p b t -> p (b t)")

        def bank(b, n=T):
            return psf[:, b * T:b * T + n]

        def col(name, k=0, n=1):
            c = _cols[name] + k
            return pk[:, c:c + n]

        consts_in = sem("consts_in")
        x_in, ctx_in = sem("x_in"), sem("ctx_in")
        landed = [sem(f"landed{j}") for j in range(RING)]
        hi_done, lo_done, unit_done = sem("hi_done"), sem("lo_done"), sem("unit_done")
        mod_landed = [sem(f"mod_landed{j}") for j in range(2)]
        mod_used, mod_evac = sem("mod_used"), sem("mod_evac")
        consts_made, cvec_done = sem("consts_made"), sem("cvec_done")
        met = {n: sem(f"met_{n}") for n in ("pe", "act", "dve")}
        sq_done, sq_used, sums_done, root_done, rinv_done = (
            sem("sq_done"), sem("sq_used"), sem("sums_done"), sem("root_done"), sem("rinv_done"))
        norm_t, norm_f, norm_lo = sem("norm_t"), sem("norm_f"), sem("norm_lo")
        centred = sem("centred")
        in_evac_a, in_evac_d = sem("in_evac_a"), sem("in_evac_d")
        sig_done, glu_done = sem("sig_done"), sem("glu_done")
        gate_free, gate_done = sem("gate_free"), sem("gate_done")
        gate_out = [sem(f"gate_out{j}") for j in range(2)]
        gen_done, q_evac, k_evac, v_evac, vt_done, v_ready = (
            sem("gen_done"), sem("q_evac"), sem("k_evac"), sem("v_evac"), sem("vt_done"), sem("v_ready"))
        s_done, max_done, exp_done, p_done, tp_done, tp_evac, pv_done, o_hi, o_lo = (
            sem("s_done"), sem("max_done"), sem("exp_done"), sem("p_done"), sem("tp_done"),
            sem("tp_evac"), sem("pv_done"), sem("o_hi"), sem("o_lo"))
        tap_done = sem("tap_done")
        wo_evac, pw_evac, out_evac, m_hi = sem("wo_evac"), sem("pw_evac"), sem("out_evac"), sem("m_hi")
        gate_in = sem("gate_in")
        q_ready, sc_done, sc_used = sem("q_ready"), sem("sc_done"), sem("sc_used")
        z_ready, z_exp = sem("z_ready"), sem("z_exp")
        e_tp, hot_done, g_mm, g_evac = sem("e_tp"), sem("hot_done"), sem("g_mm"), sem("g_evac")
        g_out = [sem(f"g_out{j}") for j in range(2)]
        gl_in = [sem(f"gl_in{j}") for j in range(2)]
        ge_done, w_done, wh_done, wl_done, acc_mm, acc_done = (
            sem("ge_done"), sem("w_done"), sem("wh_done"), sem("wl_done"), sem("acc_mm"), sem("acc_done"))
        ix_evac, iw_tp, iw_evac, ix_mm, ix_relu, ix_add = (
            sem("ix_evac"), sem("iw_tp"), sem("iw_evac"), sem("ix_mm"), sem("ix_relu"), sem("ix_add"))
        ix_scored, ix_masked = sem("ix_scored"), sem("ix_masked")
        bias_mm, bias_ev, bias_out = sem("bias_mm"), sem("bias_ev"), sem("bias_out")
        awo_evac, bwo_evac = sem("awo_evac"), sem("bwo_evac")
        lam_in, lam_exp = sem("lam_in"), sem("lam_exp")
        iota_made, keys_in, bias_tables, relb_made = (
            sem("iota_made"), sem("keys_in"), sem("bias_tables"), sem("relb_made"))
        out_done = sem("out_done")
        att = [{n: sem(f"{n}_{a}") for n in ("k_mm", "q_ev", "k_ev", "v_ev", "vt", "vr",
                                              "s", "mx", "ex", "pd", "tp", "te", "pv", "oh", "ol",
                                              "osq", "oss", "ort")}
               for a in ("dsa", "diff")]
        bias_in4 = [[sem(f"bias_in_{a}{j}") for j in range(4)] for a in range(2)]
        mlp = [{n: sem(f"{n}_mlp{a}") for n in ("free", "sq", "hh", "hl", "acc")}
               for a in range(2)]

        block = ctx.enter_context(nc.Block())

        class Tally(dict):

            def __missing__(self, k):
                return 0

        def meet(e, who, tally):
            tally["meet"] += 1
            e.drain().then_inc(met[who], 1)
            for n in met:
                if n != who:
                    e.wait_ge(met[n], tally["meet"])

        def split_hi(act, r, j):
            act.wait_ge(landed[j], 16 * r + 16)
            if not (isinstance(r, int) and r == 0):
                act.wait_ge(unit_done, RING * r + j + 1 - RING)
            nc.scalar.activation(w_hi[j][:], raw[j][:], ACT.Copy).then_inc(hi_done, 1)

        def split_lo(dve, r, j):
            dve.wait_ge(hi_done, RING * r + j + 1)
            nc.vector.tensor_tensor(w_lo[j][:], raw[j][:], w_hi[j][:].bitcast(F32),
                                    ALU.subtract).then_inc(lo_done, 1)

        def ahead(r, j):
            return (r, j + AHEAD) if j + AHEAD < RING else (r + 1, j + AHEAD - RING)

        def hi_ahead(act, r, j):
            split_hi(act, *ahead(r, j))

        def lo_ahead(dve, r, j):
            split_lo(dve, *ahead(r, j))

        def product(slot, weight_tiles, out_ap, rhs_pairs, start=True, stop=True):
            last = None
            n = len(weight_tiles)
            for x, (k, (rh, rl)) in enumerate(zip(weight_tiles, rhs_pairs)):
                nc.tensor.matmul(out_ap, w_hi[slot][:, k, :], rh, start=start and x == 0, stop=False)
                nc.tensor.matmul(out_ap, w_hi[slot][:, k, :], rl, start=False, stop=False)
                last = nc.tensor.matmul(out_ap, w_lo[slot][:, k, :], rh, start=False,
                                        stop=stop and x == n - 1)
            return last

        def slab(h, l, lo=0, n=8):
            return [(h[:, k, :], l[:, k, :]) for k in range(lo, lo + n)]

        def pe_unit(pe, r, j, b, pairs, start=True, stop=True):
            pe.wait_ge(lo_done, RING * r + j + 1)
            return product(j, range(8), bank(b), pairs, start, stop)

        def pe_mod(pe, loads, m2, out_ap, which):
            pe.wait_ge(mod_landed[m2], 16 * loads)
            for k in range(8):
                mm = nc.tensor.matmul(out_ap, mod_raw[m2][:, k, :], cvec[:, k, which:which + 2],
                                      start=(k == 0), stop=(k == 7))
            mm.then_inc(mod_used, 1)

        def act_squares(act, tl, src, n, w, ready=None):
            for k in range(n):
                if ready is not None:
                    ready(k)
                if tl["sq"] >= 2:
                    act.wait_ge(sq_used, tl["sq"] - 1)
                nc.scalar.activation(sq[tl["sq"] % 2][:, 0:w], src(k), ACT.Square).then_inc(sq_done, 1)
                tl["sq"] += 1

        def pe_sums(pe, tl, n, w, b=4):
            if tl["root"]:
                pe.wait_ge(root_done, tl["root"])
            tl["root"] += 1
            for k in range(n):
                pe.wait_ge(sq_done, tl["sq"] + 1)
                nc.tensor.matmul(bank(b, w), ones[:], sq[tl["sq"] % 2][:, 0:w], start=(k == 0),
                                 stop=(k == n - 1)).then_inc(sq_used, 1)
                tl["sq"] += 1

        def act_root(act, tl, n, w, e, b=4):
            act.wait_ge(sq_used, tl["sq"])
            if tl["root"]:
                act.wait_ge(rinv_done, tl["root"])
            nc.scalar.activation(root[:, 0:w], bank(b, w), ACT.Sqrt, bias=eps[:, e:e + 1],
                                 scale=1.0 / (n * P)).then_inc(root_done, 1)
            tl["root"] += 1

        def dve_rinv(dve, tl, w):
            tl["root"] += 1
            dve.wait_ge(root_done, tl["root"])
            nc.vector.reciprocal(rinv[:, 0:w], root[:, 0:w]).then_inc(rinv_done, 1)
            dve.drain()

        def dve_scaled(dve, tl, src, n, w, hi=None, lo=None):
            def low(k):
                dve.wait_ge(norm_f, tl["f"] + k + 1)
                nc.vector.tensor_tensor(lo(k), f_sb[(tl["f"] + k) % 2][:, 0:w], hi(k).bitcast(F32),
                                        ALU.subtract).then_inc(norm_lo, 1)
            for k in range(n):
                g = tl["f"] + k
                if g >= 2:
                    dve.wait_ge(norm_f, g - 1)
                nc.vector.tensor_tensor(t_sb[g % 2][:, 0:w], src(k), rinv[:, 0:w],
                                        ALU.mult).then_inc(norm_t, 1)
                if hi is not None and k:
                    low(k - 1)
            if hi is not None:
                low(n - 1)
                tl["lo"] += n
            tl["f"] += n
            tl["t"] += n

        def act_affine(act, tl, n, w, func, a, b, hi=None, dst=None):
            for k in range(n):
                g = tl["f"]
                act.wait_ge(norm_t, tl["t"] + 1)
                if hi is not None:
                    if tl["lo"] >= 2:
                        act.wait_ge(norm_lo, tl["lo"] - 1)
                    nc.scalar.activation(hi(k), t_sb[g % 2][:, 0:w], func, bias=b(k), scale=a(k))
                    nc.scalar.activation(f_sb[g % 2][:, 0:w], t_sb[g % 2][:, 0:w], func, bias=b(k),
                                         scale=a(k)).then_inc(norm_f, 1)
                    tl["lo"] += 1
                else:
                    nc.scalar.activation(dst(k), t_sb[g % 2][:, 0:w], func, bias=b(k),
                                         scale=a(k)).then_inc(norm_f, 1)
                tl["f"] += 1
                tl["t"] += 1

        def act_direct(act, tl, src, n, a, b, hi):
            for k in range(n):
                g = tl["f"]
                if tl["lo"] >= 2:
                    act.wait_ge(norm_lo, tl["lo"] - 1)
                nc.scalar.activation(hi(k), src(k), ACT.Identity, bias=b(k), scale=a(k))
                nc.scalar.activation(f_sb[g % 2][:], src(k), ACT.Identity, bias=b(k),
                                     scale=a(k)).then_inc(norm_f, 1)
                tl["f"] += 1
                tl["lo"] += 1

        def dve_direct(dve, tl, n, hi, lo):
            for k in range(n):
                dve.wait_ge(norm_f, tl["f"] + 1)
                nc.vector.tensor_tensor(lo(k), f_sb[tl["f"] % 2][:], hi(k).bitcast(F32),
                                        ALU.subtract).then_inc(norm_lo, 1)
                tl["f"] += 1
                tl["lo"] += 1

        def pe_means(pe, tl, src):
            for k in range(KC):
                mm = nc.tensor.matmul(bank(5), ones[:], src(k), start=(k == 0), stop=(k == KC - 1))
            mm.then_inc(sums_done, 1)
            tl["mean"] += 1

        def dve_centre(dve, tl, src):
            tl["mean"] += 1
            dve.wait_ge(sums_done, tl["mean"])
            nc.vector.tensor_scalar(rinv[:], bank(5), 1.0 / D, None, ALU.mult)
            dve.drain()
            for k in range(KC):
                nc.vector.tensor_tensor(src(k), src(k), rinv[:], ALU.subtract).then_inc(centred, 1)
            dve.drain()

        def act_centred(act, tl):
            def ready(k):
                tl["cen"] += 1
                act.wait_ge(centred, tl["cen"])
            return ready

        xk = lambda k: X[:, k, :]
        rhk = lambda k: RH[:, k, :]
        rlk = lambda k: RL[:, k, :]

        def pe_dense8(pe, r0, evac, pairs):
            for n in range(8):
                if n >= 4:
                    pe.wait_ge(evac, n - 3)
                pe_unit(pe, r0 + n // 4, n % 4, n % 4, pairs).then_inc(unit_done, 1)

        @block.sync
        def _(sp):
            sp.dma_start(pk[:], pack).then_inc(consts_in, 16)
            sp.dma_start(trig_sb[:], trig).then_inc(consts_in, 16)
            sp.dma_start(X[:], x_t).then_inc(x_in, 16)
            sp.dma_start(CX[:], ctx_t).then_inc(ctx_in, 16)
            for j in range(RING):
                sp.dma_start(raw[j][:].rearrange("p a b -> p (a b)"), w_all[j]).then_inc(landed[j], 16)
            n_rounds = ROUNDS if stop >= 99 else {1: 1, 2: R_MLA, 3: R_WO, 4: R_PQ, 5: R_UV, 6: R_UV, 7: R_DSA_IN, 8: R_DSA, 9: R_MLP1, 10: R_DIFF}[stop]
            with sp.Fori(1, n_rounds + 1) as r:
                for j in range(RING):
                    sp.wait_ge(lo_done, RING * r + j + 1 - RING)
                    sp.dma_start(raw[j][:].rearrange("p a b -> p (a b)"),
                                 w_all[r * RING + j]).then_inc(landed[j], 16)
            if stop >= 99:
                sp.wait_ge(met["act"], 24)
                sp.dma_start(out, X[:]).then_inc(out_done, 16)
                sp.wait_ge(out_done, 16)


        @block.gpsimd
        def _(pool):
            g = nc.gpsimd
            g.memset(ones[:], 1.0)
            g.memset(ident[:], 0.0)
            g.memset(eps[:, 0:1], EPS1)
            g.memset(eps[:, 1:2], EPS2)
            g.memset(ypad[:], 0.0)
            g.iota(iota[:], pattern=[[1, P]], base=0, channel_multiplier=0,
                   allow_small_or_imprecise_dtypes=True).then_inc(iota_made, 1)
            pool.drain()
            g.affine_select(out=ident[:], in_=ident[:], compare_op=ALU.not_equal, fill=1.0, base=0,
                            pattern=[[-1, P]], channel_multiplier=1).then_inc(consts_made, 1)
            for j in range(2):
                pool.dma_start(mod_raw[j][:].rearrange("p a b -> p (a b)"),
                               w_mods[j]).then_inc(mod_landed[j], 16)
            with pool.Fori(1, {1: 8, 2: 8, 3: 24, 4: 24}.get(stop, MODS // 2)) as r:
                for j in range(2):
                    pool.wait_ge(mod_used, 2 * r + j - 1)
                    pool.dma_start(mod_raw[j][:].rearrange("p a b -> p (a b)"),
                                   w_mods[r * 2 + j]).then_inc(mod_landed[j], 16)
            if stop < 6:
                return
            with pool.Fori(0, 8) as i:
                for b in range(2):
                    pool.wait_ge(g_evac, 16 * i + 8 * b + 8)
                    pool.dma_start(peer_gate_dram[i * 2 + b],
                                   Gs[b][:].rearrange("p e t -> p (e t)")).then_inc(g_out[b], 16)
            for b in range(2):
                pool.wait_ge(g_out[b], 16 * 8)
            gd = peer_gate_dram.rearrange("b p (r x) -> p b r x", x=P)
            pool.wait_ge(met["dve"], 10)
            for b in range(2):
                pool.dma_start(GL[b][:], gd[:, :, b, :]).then_inc(gl_in[b], 16)
            with pool.Fori(1, CHUNK_ROUNDS // 2) as i:
                for b in range(2):
                    pool.wait_ge(w_done, 8 * i + 4 * b - 4)
                    pool.dma_start(GL[b][:], gd[:, :, i * 2 + b, :]).then_inc(gl_in[b], 16)
            if stop < 8:
                return
            for b in range(1, TB):
                pool.wait_ge(ix_scored, b)
                blk = score[b][:, b * P:(b + 1) * P]
                g.affine_select(out=blk, in_=blk, compare_op=ALU.is_ge, fill=LOWEST, base=0,
                                pattern=[[-1, P]], channel_multiplier=1).then_inc(ix_masked, 1)
            pool.wait_ge(bias_out, 16)
            for a in range(2):
                if a == 1 and stop < 11:
                    return
                pool.wait_ge(met["dve"], (14, 19)[a])
                for p in range(PAIRS):
                    for m in range(2):
                        if p >= 2:
                            pool.wait_ge(att[a]["mx"], 8 * (p - 1))
                        src = bass.AP(bias_row_dram, (2 * p + m) * P * BIAS_Z + P - 1,
                                      [[BIAS_Z - 1, P], [1, T]])
                        pool.dma_start(Tb[2 * (p % 2) + m][:], src).then_inc(
                            bias_in4[a][2 * (p % 2) + m], 16)

        def order(a):
            return [(m, b) for m in range(2) for b in range(TB)] if a == 0 else \
                   [(m, b) for b in range(TB) for m in range(2)]

        def act_residual_norm(act, tl, r0, layer, which):
            for n in range(8):
                hi_ahead(act, r0 + n // 4, n % 4)
            act_post(act, tl, layer, which)

        def act_post(act, tl, layer, which):
            sc = nc.scalar
            meet(act, "act", tl)
            act_squares(act, tl, xk, KC, T, act_centred(act, tl))
            act_root(act, tl, KC, T, 1)
            c = (layer * 2 + which) * 8
            act_affine(act, tl, KC, T, ACT.Identity, lambda k: col("ln_g", c + k),
                       lambda k: col("ln_b", c + k), dst=xk)
            act.drain()
            if (layer, which) != (1, 1):
                s = 48 * layer + 24 if which == 0 else 48
                act_direct(act, tl, xk, KC, lambda k: gain[:, k, 0:1],
                           lambda k: MOD2[:, s + k:s + k + 1], rhk)
            meet(act, "act", tl)

        def act_attention(act, tl, a):
            sc, A = nc.scalar, att[a]
            r0, units = ((R_DSA, 2), (R_DIFF, 3))[a]
            body = 4 // units if a == 0 else 4
            with act.Fori(0, PAIRS // body) as i:
                for pp in range(body):
                    p = i * body + pp
                    tiles = order(a)
                    for x in range(units):
                        u = units * pp + x
                        hi_ahead(act, r0 + i * (units * body // 4) + u // 4, u % 4)
                    rnd = lambda x: RING * (r0 + i * (units * body // 4)) + units * pp + x
                    act.wait_ge(unit_done, rnd(1))
                    act.wait_ge(A["s"], 8 * p)
                    sc.activation(q2[:], bank(7), ACT.Copy, scale=SCALE2).then_inc(A["q_ev"], 1)
                    act.wait_ge(A["k_mm"], p + 1) if a == 0 else act.wait_ge(unit_done, rnd(2))
                    sc.activation(k2[:], bank(0), ACT.Copy).then_inc(A["k_ev"], 1)
                    act.wait_ge(unit_done, rnd(units))
                    act.wait_ge(A["vt"], p)
                    sc.activation(vT2[:], bank(2), ACT.Copy).then_inc(A["v_ev"], 1)
                    act.wait_ge(A["vt"], p + 1)
                    act.wait_ge(A["pv"], (2, 1)[a] * p)
                    sc.activation(v2[:].rearrange("p c k -> p (c k)"), bank(4), ACT.Copy).then_inc(A["vr"], 1)

                    turns = (8, 4)[a]

                    def turned(x):
                        b = x % 4
                        act.wait_ge(A["tp"], turns * p + x + 1)
                        if b == 0:
                            act.wait_ge(A["pv"], (2, 1)[a] * p + x // 4)
                        sc.activation(PT2[:, 0:b + 1, b * P:(b + 1) * P],
                                      bank(4 + x % 2, (b + 1) * P).rearrange("p (c k) -> p c k", k=P),
                                      ACT.Copy).then_inc(A["te"], 1)

                    for n, (m, b) in enumerate(tiles):
                        w = (b + 1) * P
                        act.wait_ge(A["mx"], 8 * p + n + 1)
                        if a == 0:
                            act.wait_ge(A["tp"], 8 * p + max(n - 1, 0))
                        else:
                            act.wait_ge(A["tp"], 4 * p + n // 2)
                        sc.activation(P2[n % 2][:, 0:w], ss[n % 2][:, 0:w], ACT.Exp,
                                      bias=nmax[:, n % 2:n % 2 + 1],
                                      accum_out=psum_row[:, n % 2:n % 2 + 1]).then_inc(A["ex"], 1)
                        if a == 0 and n:
                            turned(n - 1)
                        if a == 1 and n % 2 == 0 and n:
                            turned(n // 2 - 1)
                    turned(turns - 1)
                    act.wait_ge(A["pv"], (2, 1)[a] * (p + 1))
                    if a == 0:
                        sc.activation(OH[:, p, :], bank(6), ACT.Copy).then_inc(A["oh"], 1)
                    else:
                        sc.activation(sq[0][:], bank(6), ACT.Square).then_inc(A["osq"], 1)
                        act.wait_ge(A["oss"], p + 1)
                        sc.activation(root[:], bank(7), ACT.Sqrt, bias=eps[:, 1:2],
                                      scale=1.0 / P).then_inc(A["ort"], 1)
                        act.wait_ge(A["oh"], p + 1)
                        act.wait_ge(A["ol"], p)
                        sc.activation(OH[:, p, :], t_sb[0][:], ACT.Copy, scale=lam[:, 5:6])
                        sc.activation(f_sb[0][:], t_sb[0][:], ACT.Copy, scale=lam[:, 5:6]).then_inc(A["ort"], 1)

        def act_mlp(act, tl, a, r0):
            sc, L = nc.scalar, mlp[a]
            act.drain().then_inc(L["free"], RING)
            with act.Fori(0, 2) as i:
                for n in range(16):
                    r, j = r0 + i * 8 + n // 4, n % 4
                    hi_ahead(act, r, j)
                    act.wait_ge(unit_done, RING * r + j + 1)
                    act.wait_ge(L["sq"], 16 * i + max(n - 1, 0))
                    sc.activation(t_sb[n % 2][:], bank(j), ACT.Relu).then_inc(L["free"], 1)
                    act.wait_ge(L["sq"], 16 * i + n + 1)
                    sc.activation(HH[:, n, :], f_sb[n % 2][:], ACT.Copy).then_inc(L["hh"], 1)
                for n in range(16):
                    hi_ahead(act, r0 + i * 8 + 4 + n // 4, n % 4)

        @block.scalar
        def _(act):
            tl = Tally()
            sc = nc.scalar
            act.wait_ge(consts_in, 32)
            sc.activation(cvec[:].rearrange("p a b -> p (a b)"), col("c", 0, 32), ACT.Silu).then_inc(cvec_done, 1)
            for j in range(AHEAD):
                split_hi(act, 0, j)
            act.wait_ge(consts_made, 1)
            act.wait_ge(x_in, 16)
            act_squares(act, tl, xk, KC, T)
            act_root(act, tl, KC, T, 0)
            meet(act, "act", tl)
            act_affine(act, tl, KC, T, ACT.Identity, lambda k: gain[:, k, 0:1],
                       lambda k: MOD[:, k, 0:1], hi=rhk)
            act.wait_ge(ctx_in, 16)
            act_squares(act, tl, lambda k: CX[:, k, :], KC, TC)
            act_root(act, tl, KC, TC, 0)
            act_affine(act, tl, KC, TC, ACT.Identity, lambda k: gain[:, k, 1:2],
                       lambda k: MOD[:, k, 1:2], hi=lambda k: CH[:, k, :])
            meet(act, "act", tl)
            if stop < 2:
                return
            for j in range(RING):
                hi_ahead(act, R_IN, j)
                if j < 2:
                    act.wait_ge(unit_done, j + 1)
                    sc.activation(cqT[:, j, :], bank(j), ACT.Copy).then_inc(in_evac_a, 1)
            with act.Fori(0, 4) as i:
                for j in range(RING):
                    hi_ahead(act, R_CONV + i, j)
                    if j % 2:
                        act.wait_ge(unit_done, RING * (R_CONV + i) + j + 1)
                        act.wait_ge(glu_done, 2 * i)
                        sc.activation(sig[j // 2][:], bank(j), ACT.Sigmoid).then_inc(sig_done, 1)
            act.wait_ge(glu_done, 8)
            act.drain().then_inc(gate_free, RING)
            with act.Fori(0, 4) as i:
                for j in range(RING):
                    hi_ahead(act, R_GATE + i, j)
                    act.wait_ge(unit_done, RING * (R_GATE + i) + j + 1)
                    act.wait_ge(gate_out[j % 2], 32 * i + 16 * (j // 2))
                    sc.activation(sig[j % 2][:], bank(j), ACT.Sigmoid).then_inc(gate_free, 1)
                    act.wait_ge(gate_free, RING * i + j + 1 + RING)
                    act.dma_start(gates_dram[i * 4 + j], sig[j % 2][:]).then_inc(gate_out[j % 2], 16)
            act_squares(act, tl, lambda k: cqT[:, k, :], 2, T)
            act_root(act, tl, 2, T, 0)
            act_affine(act, tl, 2, T, ACT.Identity, lambda k: col("q_norm_g", k),
                       lambda k: 0.0, hi=lambda k: CQH[:, k, :])
            for lo, w in ((0, T), (T, TC)):
                act_squares(act, tl, lambda k: ckvT[:, lo:lo + w], 1, w)
                act_root(act, tl, 1, w, 0)
                act_affine(act, tl, 1, w, ACT.Identity, lambda k: col("kv_norm_g"), lambda k: 0.0,
                           hi=lambda k: CKH[:, lo:lo + w])
            for j in range(2):
                act.wait_ge(gate_out[j], 16 * 8)
            meet(act, "act", tl)
            if stop < 3:
                return
            with act.Fori(0, 2) as i:
                for pp in range(4):
                    p = i * 4 + pp
                    hi_ahead(act, R_MLA + i, pp)
                    act.wait_ge(gen_done, 4 * p + 2)
                    act.wait_ge(s_done, 8 * p)
                    sc.activation(KT[0][0:NOPE, :], psf[0:NOPE, 0:KEYS], ACT.Copy)
                    sc.activation(KT[1][0:NOPE, :], psf[NOPE:P, 0:KEYS], ACT.Copy).then_inc(k_evac, 1)
                    act.wait_ge(gen_done, 4 * p + 3)
                    act.wait_ge(vt_done, p)
                    sc.activation(VT[:], bank(2, KEYS), ACT.Copy).then_inc(v_evac, 1)
                    act.wait_ge(vt_done, p + 1)
                    act.wait_ge(pv_done, 2 * p)
                    sc.activation(Vk[:].rearrange("p c k -> p (c k)"), bank(4, KEYS),
                                  ACT.Copy).then_inc(v_ready, 1)

                    def turned(n):
                        act.wait_ge(tp_done, 8 * p + n + 1)
                        if n == 0 or n == 4:
                            act.wait_ge(pv_done, 2 * p + n // 4)
                        sc.activation(PT[:, :, (n % 4) * P:(n % 4 + 1) * P],
                                      bank(4, KEYS).rearrange("p (c k) -> p c k", c=6),
                                      ACT.Copy).then_inc(tp_evac, 1)

                    for n in range(8):
                        act.wait_ge(max_done, 8 * p + n + 1)
                        act.wait_ge(tp_done, 8 * p + max(n - 1, 0))
                        sc.activation(Pm[n % 2][:], bank(2 * (n % 2), KEYS), ACT.Exp,
                                      bias=nmax[:, n % 2:n % 2 + 1],
                                      accum_out=psum_row[:, n % 2:n % 2 + 1]).then_inc(exp_done, 1)
                        if n:
                            turned(n - 1)
                    turned(7)
                    act.wait_ge(pv_done, 2 * p + 2)
                    sc.activation(RH[:, p, :], bank(6), ACT.Copy).then_inc(o_hi, 1)
            meet(act, "act", tl)
            if stop < 4:
                return
            act.dma_start(gate_sb[:], gates_dram[0:8].rearrange("k p t -> p k t")).then_inc(gate_in, 16)
            for n in range(8):
                hi_ahead(act, R_WO + n // 4, n % 4)
            act_squares(act, tl, lambda k: ypad[:, k, 0:T], KC, T, act_centred(act, tl))
            act_root(act, tl, KC, T, 0)
            act.wait_ge(wo_evac, 8)
            act.dma_start(gate_sb[:], gates_dram[8:16].rearrange("k p t -> p k t")).then_inc(gate_in, 16)
            act_affine(act, tl, KC, T, ACT.Silu, lambda k: col("conv_ln_g", k),
                       lambda k: col("conv_ln_b", k), hi=lambda k: VH[:, k, :])
            meet(act, "act", tl)
            for n in range(8):
                hi_ahead(act, R_PW + n // 4, n % 4)
                act.wait_ge(pw_evac, n + 1)
                sc.activation(RH[:, n, :], Mg[:, n, :], ACT.Copy).then_inc(m_hi, 1)
            meet(act, "act", tl)
            for n in range(8):
                hi_ahead(act, R_OUT + n // 4, n % 4)
            meet(act, "act", tl)
            act_squares(act, tl, xk, KC, T)
            act_root(act, tl, KC, T, 0)
            act_affine(act, tl, KC, T, ACT.Identity, lambda k: gain[:, k, 0:1],
                       lambda k: MOD[:, 24 + k, 0:1], hi=rhk)
            meet(act, "act", tl)
            if stop < 5:
                return
            act.dma_start(SK[:], sub_keys).then_inc(keys_in, 16)
            with act.Fori(0, 4) as i:
                for j in range(RING):
                    hi_ahead(act, R_PQ + i, j)
                    act.wait_ge(unit_done, RING * (R_PQ + i) + j + 1)
                    act.wait_ge(sc_done, 4 * i + max(j - 1, 0))
                    sc.activation(qs[j % 2][:], bank(j), ACT.Copy).then_inc(q_ready, 1)
            act.wait_ge(z_ready, 1)
            ev = E[2][:].rearrange("p a b c -> p (a b c)")
            sc.activation(ev, ev, ACT.Exp).then_inc(z_exp, 1)
            meet(act, "act", tl)
            if stop < 6:
                return
            for m in range(3):
                act.wait_ge(e_tp, m + 1)
                sc.activation(ET[m][:], bank(m), ACT.Copy)
            act.drain().then_inc(e_tp, 1)
            with act.Fori(0, 8) as i:
                for b in range(2):
                    act.wait_ge(g_out[b], 16 * i)
                    for s in range(8):
                        act.wait_ge(g_mm, 16 * i + 8 * b + s + 1)
                        sc.activation(Gs[b][:, :, 4 * s:4 * s + 4],
                                      bank(s % 4).rearrange("p (t e) -> p e t", t=4),
                                      ACT.Copy).then_inc(g_evac, 1)
            meet(act, "act", tl)
            if stop < 7:
                return
            def act_up(r, par, n):
                for c in range(RING):
                    hi_ahead(act, r, c)
                    act.wait_ge(unit_done, RING * r + c + 1)
                    sc.activation(ge[c % 2][:], bank(c), ACT.Gelu).then_inc(ge_done, 1)
                    act.wait_ge(w_done, RING * n + c + 1)
                    sc.activation(WH[par][:, c, :], wf[c % 2][:], ACT.Copy).then_inc(wh_done, 1)

            def act_down(r):
                split_hi(act, r, 3)
                split_hi(act, r + 1, 0)
                split_hi(act, r + 1, 1)
                split_hi(act, r + 1, 2)

            act_up(R_UV, 0, 0)
            with act.Fori(0, 15) as i:
                for b in range(2):
                    act_up(R_UV + 1 + i * 4 + 2 * b, 1 - b, i * 2 + 1 + b)
                    act_down(R_UV + 2 + i * 4 + 2 * b)
            act_up(R_UV + 61, 1, 31)
            act_down(R_UV + 62)
            act_down(R_UV + 63)
            meet(act, "act", tl)
            act_squares(act, tl, xk, KC, T)
            act_root(act, tl, KC, T, 0)
            act_affine(act, tl, KC, T, ACT.Identity, lambda k: col("final_g", k), lambda k: 0.0, dst=xk)
            act.drain()
            act_direct(act, tl, xk, KC, lambda k: gain[:, k, 0:1], lambda k: MOD2[:, k:k + 1], rhk)
            meet(act, "act", tl)
            if stop < 8:
                return
            act.dma_start(hotz[:], bias_hot).then_inc(bias_tables, 16)
            act.dma_start(relb[0:BUCKETS, :], rel_bias).then_inc(bias_tables, 16)
            for n in range(8):
                hi_ahead(act, R_DSA_IN + n // 4, n % 4)
                act.wait_ge(unit_done, RING * R_DSA_IN + n + 1)
                dst = kvT[:, n, :] if n < 2 else iqT[:, n - 2, :] if n < 6 else ikT[:] if n == 6 else None
                if dst is not None:
                    sc.activation(dst, bank(n), ACT.Copy).then_inc(ix_evac, 1)
                else:
                    sc.activation(iwT[0:IDX_H, :], psf[0:IDX_H, n * T:(n + 1) * T], ACT.Copy,
                                  scale=IW_SCALE).then_inc(ix_evac, 1)
            act.drain()
            act_squares(act, tl, lambda k: kvT[:, k, :], 2, T)
            act_root(act, tl, 2, T, 1)
            act_affine(act, tl, 2, T, ACT.Identity, lambda k: col("a_kv_norm", k), lambda k: 0.0,
                       hi=lambda k: KVH[:, k, :])
            act.wait_ge(bias_mm, 1)
            sc.activation(brow[:], psf[0:HEADS, 6 * T:6 * T + BIAS_Z], ACT.Copy).then_inc(bias_ev, 1)
            act.wait_ge(bias_ev, 1)
            act.dma_start(bias_rows, brow[:].unsqueeze(1).to_broadcast([HEADS, P, BIAS_Z])).then_inc(bias_out, 16)
            meet(act, "act", tl)
            for b in range(1, TB):
                for h in range(IDX_H):
                    n = (b - 1) * IDX_H + h
                    act.wait_ge(ix_mm, n + 1)
                    if n >= 2:
                        act.wait_ge(ix_add, n - 1)
                    w = (b + 1) * P
                    sc.activation(sq[n % 2][:, 0:w], bank(n % 4, w), ACT.Relu).then_inc(ix_relu, 1)
            act.wait_ge(bias_out, 16)
            meet(act, "act", tl)
            if stop < 9:
                return
            act_attention(act, tl, 0)
            meet(act, "act", tl)
            act_residual_norm(act, tl, R_AWO, 0, 0)
            if stop < 10:
                return
            act_mlp(act, tl, 0, R_MLP1)
            act_post(act, tl, 0, 1)
            if stop < 11:
                return
            act.dma_start(lb_sb[:], bass.AP(b_lambda.tensor, 0, [[0, P], [1, 256]])).then_inc(lam_in, 16)
            act.wait_ge(lam_exp, 1)
            sc.activation(lam[:, 2:4], lam[:, 0:2], ACT.Exp).then_inc(lam_exp, 1)
            act_attention(act, tl, 1)
            meet(act, "act", tl)
            act_residual_norm(act, tl, R_BWO, 1, 0)
            act_mlp(act, tl, 1, R_MLP2)
            act_post(act, tl, 1, 1)

        def dve_retrieve(dve, tl):
            v = nc.vector
            dve.wait_ge(iota_made, 1)
            io16 = iota[:, 0:TOPK].unsqueeze(1).to_broadcast([P, TOPK, TOPK])
            with dve.Fori(0, 4) as i:
                for j in range(RING):
                    lo_ahead(dve, R_PQ + i, j)
                    m = j % 2
                    dve.wait_ge(sc_done, RING * i + j + 1)
                    v.memset(nmax[:, 0:1], 0.0)
                    src = ps[:, 4 + m, :].rearrange("p (b k) -> p b k", b=TB)
                    for b in range(TB):
                        v.max(top_v[m][:, b, 0:8], src[:, b, :])
                    dve.drain()
                    for b in range(TB):
                        v.max_index(top_i[m][:, b, 0:8], top_v[m][:, b, 0:8], src[:, b, :])
                        v.match_replace(left[:, b, :], top_v[m][:, b, 0:8], src[:, b, :], LOWEST)
                    dve.drain().then_inc(sc_used, 1)
                    for b in range(TB):
                        v.max(top_v[m][:, b, 8:16], left[:, b, :])
                    dve.drain()
                    for b in range(TB):
                        v.max_index(top_i[m][:, b, 8:16], top_v[m][:, b, 8:16], left[:, b, :])
                    dve.drain()
                    v.tensor_copy(top_f[m][:], top_i[m][:])
                    if m == 0:
                        continue
                    h = i * 2 + j // 2
                    for b in range(TB):
                        v.tensor_tensor(cand[:, b, :].rearrange("p (x y) -> p x y", x=TOPK),
                                        top_v[0][:, b, :].unsqueeze(2).to_broadcast([P, TOPK, TOPK]),
                                        top_v[1][:, b, :].unsqueeze(1).to_broadcast([P, TOPK, TOPK]), ALU.add)
                    dve.drain()
                    for b in range(TB):
                        v.max(best[:, b, 0:8], cand[:, b, :])
                    dve.drain()
                    for b in range(TB):
                        v.max_index(best_i[:, b, 0:8], best[:, b, 0:8], cand[:, b, :])
                        v.match_replace(cand2[:, b, :], best[:, b, 0:8], cand[:, b, :], LOWEST)
                    dve.drain()
                    for b in range(TB):
                        v.max(best[:, b, 8:16], cand2[:, b, :])
                    dve.drain()
                    for b in range(TB):
                        v.max_index(best_i[:, b, 8:16], best[:, b, 8:16], cand2[:, b, :])
                    dve.drain()
                    v.tensor_single_scalar(half_i[0][:], best_i[:], 4, ALU.logical_shift_right)
                    v.tensor_single_scalar(half_i[1][:], best_i[:], TOPK - 1, ALU.bitwise_and)
                    v.tensor_copy(E[2][:, :, h, :], best[:])
                    dve.drain()
                    for x in range(2):
                        v.tensor_copy(half_f[x][:], half_i[x][:])
                    dve.drain()
                    for x in range(2):
                        for b in range(TB):
                            v.tensor_tensor(hit[:, b, :].rearrange("p (x y) -> p x y", x=TOPK),
                                            half_f[x][:, b, :].unsqueeze(2).to_broadcast([P, TOPK, TOPK]),
                                            io16, ALU.is_equal)
                        dve.drain()
                        for b in range(TB):
                            hb = hit[:, b, :].rearrange("p (x y) -> p x y", x=TOPK)
                            v.tensor_tensor(hb, hb, top_f[x][:, b, :].unsqueeze(1).to_broadcast([P, TOPK, TOPK]),
                                            ALU.mult)
                        dve.drain()
                        v.tensor_reduce(E[x][:, :, h, :], hit[:].rearrange("p b (x y) -> p b x y", x=TOPK),
                                        AX.X, ALU.add)
                        dve.drain()
            bv = E[2][:].rearrange("p b h k -> p (b h) k")
            v.tensor_copy(zmax[:], bv[:, :, 0])
            dve.drain()
            v.tensor_tensor(bv, bv, zmax[:].unsqueeze(2).to_broadcast([P, TB * PEER_H, TOPK]), ALU.subtract)
            dve.drain().then_inc(z_ready, 1)
            dve.wait_ge(z_exp, 1)
            v.tensor_reduce(zsum[:], bv, AX.X, ALU.add)
            dve.drain()
            v.reciprocal(zsum[:], zsum[:])
            dve.drain()
            v.tensor_tensor(bv, bv, zsum[:].unsqueeze(2).to_broadcast([P, TB * PEER_H, TOPK]), ALU.mult)
            dve.wait_ge(mod_used, MODS)
            v.tensor_tensor(MOD2[:], bank(6, 96 * 2).rearrange("p (m c) -> p m c", c=2)[:, :, 0],
                            col("ada_b", 0, 96), ALU.add)

        def dve_residual_norm(dve, tl, r0, layer, which, evac):
            v = nc.vector
            g0 = 48 * layer + 16
            v.tensor_scalar(gain[:, :, 1], MOD2[:, g0:g0 + 8], 1.0, None, ALU.add)
            dve.drain()
            for n in range(8):
                lo_ahead(dve, r0 + n // 4, n % 4)
                dve.wait_ge(unit_done, RING * r0 + n + 1)
                v.tensor_scalar(f_sb[0][:], bank(n % 4), gain[:, n, 1:2], None, ALU.mult).then_inc(evac, 1)
                dve.drain()
                v.scalar_tensor_tensor(X[:, n, :], X[:, n, :], ALPHA, f_sb[0][:], ALU.mult, ALU.add)
                dve.drain()
            dve_post(dve, tl, layer, which)

        def dve_post(dve, tl, layer, which):
            v = nc.vector
            last = (layer, which) == (1, 1)
            if which == 1:
                g0 = 48 * layer + 40
                v.tensor_scalar(gain[:, :, 1], MOD2[:, g0:g0 + 8], 1.0, None, ALU.add)
                dve.drain()
                for k in range(KC):
                    v.tensor_scalar(Y2[:, k, :], Y2[:, k, :], gain[:, k, 1:2], None, ALU.mult)
                dve.drain()
                for k in range(KC):
                    v.scalar_tensor_tensor(X[:, k, :], X[:, k, :], ALPHA, Y2[:, k, :], ALU.mult, ALU.add)
            if not last:
                s0 = 48 * layer + 32 if which == 0 else 48 + 8
                v.tensor_scalar(gain[:, :, 0], MOD2[:, s0:s0 + 8], 1.0, None, ALU.add)
            meet(dve, "dve", tl)
            dve_centre(dve, tl, xk)
            dve_rinv(dve, tl, T)
            dve_scaled(dve, tl, xk, KC, T)
            if not last:
                dve_direct(dve, tl, KC, rhk, rlk)
            meet(dve, "dve", tl)

        def dve_attention(dve, tl, a):
            v, A = nc.vector, att[a]
            r0, units = ((R_DSA, 2), (R_DIFF, 3))[a]
            body = 2 if a == 0 else 4
            turns = (8, 4)[a]
            with dve.Fori(0, PAIRS // body) as i:
                for pp in range(body):
                    p = i * body + pp
                    for x in range(units):
                        u = units * pp + x
                        lo_ahead(dve, r0 + i * (units * body // 4) + u // 4, u % 4)

                    def normalised(n):
                        m, b = order(a)[n]
                        w = (b + 1) * P
                        c = slice(n % 2, n % 2 + 1)
                        dve.wait_ge(A["ex"], 8 * p + n + 1)
                        v.reciprocal(rrow[:, c], psum_row[:, c])
                        dve.drain()
                        if a == 0:
                            v.tensor_scalar(P2[n % 2][:, 0:w], P2[n % 2][:, 0:w], rrow[:, c], None,
                                            ALU.mult).then_inc(A["pd"], 1)
                        elif m == 1:
                            v.tensor_scalar(P2[1][:, 0:w], P2[1][:, 0:w], rrow[:, 1:2], lam[:, 4:5],
                                            ALU.mult, ALU.mult)
                            dve.drain()
                            v.scalar_tensor_tensor(P2[0][:, 0:w], P2[0][:, 0:w], rrow[:, 0:1],
                                                   P2[1][:, 0:w], ALU.mult, ALU.subtract).then_inc(A["pd"], 1)

                    for n, (m, b) in enumerate(order(a)):
                        w = (b + 1) * P
                        if b == 0:
                            dve.wait_ge(bias_in4[a][2 * (pp % 2) + m], 16 * (body // 2) * i + 16 * (pp // 2) + 16)
                        dve.wait_ge(A["s"], 8 * p + n + 1)
                        tb = Tb[2 * (pp % 2) + m][:, (TB - 1 - b) * P:TB * P]
                        s = ss[n % 2][:, 0:w]
                        v.tensor_tensor(s, bank(2 * (n % 2), w), tb, ALU.add)
                        dve.drain()
                        if a == 0 and b:
                            v.tensor_tensor(s, s, M[b][:, 0:w], ALU.add)
                            dve.drain()
                        v.tensor_reduce(nmax[:, n % 2:n % 2 + 1], s, AX.X, ALU.max,
                                        negate=True).then_inc(A["mx"], 1)
                        if n:
                            normalised(n - 1)
                    normalised(7)
                    if a == 0:
                        dve.wait_ge(A["oh"], p + 1)
                        v.tensor_tensor(OL[:, p, :], bank(6), OH[:, p, :].bitcast(F32),
                                        ALU.subtract).then_inc(A["ol"], 1)
                    else:
                        dve.wait_ge(A["ort"], 2 * p + 1)
                        v.reciprocal(rinv[:], root[:])
                        dve.drain()
                        v.tensor_tensor(t_sb[0][:], bank(6), rinv[:], ALU.mult).then_inc(A["oh"], 1)
                        dve.wait_ge(A["ort"], 2 * p + 2)
                        v.tensor_tensor(OL[:, p, :], f_sb[0][:], OH[:, p, :].bitcast(F32),
                                        ALU.subtract).then_inc(A["ol"], 1)

        def dve_mlp(dve, tl, a, r0):
            v, L = nc.vector, mlp[a]
            v.memset(Y2[:], 0.0)
            dve.drain()
            with dve.Fori(0, 2) as i:
                for n in range(16):
                    lo_ahead(dve, r0 + i * 8 + n // 4, n % 4)
                    dve.wait_ge(L["free"], RING + 16 * i + n + 1)
                    if n >= 2:
                        dve.wait_ge(L["hh"], 16 * i + n - 1)
                    v.tensor_tensor(f_sb[n % 2][:], t_sb[n % 2][:], t_sb[n % 2][:],
                                    ALU.mult).then_inc(L["sq"], 1)
                    dve.wait_ge(L["hh"], 16 * i + n + 1)
                    v.tensor_tensor(HL[:, n, :], f_sb[n % 2][:], HH[:, n, :].bitcast(F32),
                                    ALU.subtract).then_inc(L["hl"], 1)
                for n in range(16):
                    lo_ahead(dve, r0 + i * 8 + 4 + n // 4, n % 4)
                    if n % 2:
                        d = n // 2
                        dve.wait_ge(unit_done, RING * (r0 + i * 8 + 4 + n // 4) + n % 4 + 1)
                        v.tensor_tensor(Y2[:, d, :], Y2[:, d, :], bank(4 + d % 4), ALU.add).then_inc(L["acc"], 1)
            dve.drain()

        @block.vector
        def _(dve):
            tl = Tally()
            v = nc.vector
            for j in range(AHEAD):
                split_lo(dve, 0, j)
            dve.wait_ge(x_in, 16)
            dve.wait_ge(mod_used, MOD_UP)
            for c in range(2):
                v.tensor_tensor(MOD[:, 0:MOD_UP, c], bank(7, 2 * MOD_UP).rearrange("p (m c) -> p m c", c=2)[:, :, c],
                                col("b_mod", 0, MOD_UP), ALU.add)
            dve.drain()
            for c in range(2):
                v.scalar_tensor_tensor(gain[:, :, c], MOD[:, 8:16, c], 1.0, col("norm1_g", 0, 8),
                                       ALU.add, ALU.mult)
            dve_rinv(dve, tl, T)
            meet(dve, "dve", tl)
            dve_scaled(dve, tl, xk, KC, T, rhk, rlk)
            dve_rinv(dve, tl, TC)
            dve_scaled(dve, tl, lambda k: CX[:, k, :], KC, TC, lambda k: CH[:, k, :], lambda k: CL[:, k, :])
            meet(dve, "dve", tl)
            if stop < 2:
                return
            for j in range(RING):
                lo_ahead(dve, R_IN, j)
                if j == 2:
                    dve.wait_ge(unit_done, 3)
                    v.tensor_copy(ckvT[:, 0:T], bank(2))
                    v.tensor_copy(ckvT[:, T:KEYS], bank(5, TC))
                if j == 3:
                    dve.wait_ge(unit_done, 4)
                    v.tensor_tensor(t_sb[0][NOPE:QK], ps[NOPE:QK, 3, :], trig_sb[NOPE:QK], ALU.mult)
                    v.tensor_tensor(t_sb[1][NOPE:QK], ps[QK:P, 3, :], trig_sb[QK:P], ALU.mult)
                    dve.drain()
                    for m in range(2):
                        v.tensor_tensor(KT[m][NOPE:QK, 0:T], t_sb[0][NOPE:QK], t_sb[1][NOPE:QK], ALU.add)
                        v.tensor_copy(KT[m][NOPE:QK, T:KEYS], ps[NOPE:QK, 6, 0:TC])
                    dve.drain().then_inc(in_evac_d, 1)
            with dve.Fori(0, 4) as i:
                for j in range(RING):
                    lo_ahead(dve, R_CONV + i, j)
                    if j % 2:
                        dve.wait_ge(sig_done, 2 * i + j // 2 + 1)
                        v.tensor_tensor(ypad[:, i * 2 + j // 2, HALF_W:HALF_W + T], bank(j - 1),
                                        sig[j // 2][:], ALU.mult).then_inc(glu_done, 1)
            with dve.Fori(0, 4) as i:
                for j in range(RING):
                    lo_ahead(dve, R_GATE + i, j)
            dve_rinv(dve, tl, T)
            dve_scaled(dve, tl, lambda k: cqT[:, k, :], 2, T, lambda k: CQH[:, k, :], lambda k: CQL[:, k, :])
            for lo, w in ((0, T), (T, TC)):
                dve_rinv(dve, tl, w)
                dve_scaled(dve, tl, lambda k: ckvT[:, lo:lo + w], 1, w, lambda k: CKH[:, lo:lo + w],
                           lambda k: CKL[:, lo:lo + w])
            meet(dve, "dve", tl)
            if stop < 3:
                return
            with dve.Fori(0, 2) as i:
                for pp in range(4):
                    p = i * 4 + pp
                    lo_ahead(dve, R_MLA + i, pp)

                    def queries(m):
                        dve.wait_ge(gen_done, 4 * p + (1, 4)[m])
                        v.tensor_scalar(QT[m][0:NOPE], ps[0:NOPE, 7, :], SCALE1, None, ALU.mult)
                        v.scalar_tensor_tensor(t_sb[0][NOPE:QK], ps[NOPE:QK, 7, :], SCALE1,
                                               trig_sb[NOPE:QK], ALU.mult, ALU.mult)
                        v.scalar_tensor_tensor(t_sb[1][NOPE:QK], ps[QK:P, 7, :], SCALE1,
                                               trig_sb[QK:P], ALU.mult, ALU.mult)
                        dve.drain()
                        v.tensor_tensor(QT[m][NOPE:QK], t_sb[0][NOPE:QK], t_sb[1][NOPE:QK],
                                        ALU.add).then_inc(q_evac, 1)

                    def taps(lo, hi):
                        for t in range(lo, min(hi, CONV_W)):
                            w = pk[:, bass.ds(p * CONV_W + (_cols["conv_w"] + t), 1)]
                            y = ypad[:, p, t:t + T]
                            acc = f_sb[t % 2]
                            if t == 0:
                                dve.wait_ge(tap_done, 32 * p)
                                ins = v.tensor_scalar(acc[:], y, w, pk[:, bass.ds(p + _cols["conv_b"], 1)],
                                                      ALU.mult, ALU.add)
                            elif t == 1:
                                ins = v.tensor_scalar(acc[:], y, w, None, ALU.mult)
                            else:
                                dve.wait_ge(tap_done, 32 * p + t - 1)
                                ins = v.scalar_tensor_tensor(acc[:], y, w, acc[:], ALU.mult, ALU.add)
                            ins.then_inc(tap_done, 1)
                        if hi > CONV_W:
                            dve.wait_ge(tap_done, 32 * p + CONV_W)
                            v.tensor_tensor(ypad[:, p, 0:T], f_sb[0][:], f_sb[1][:],
                                            ALU.add).then_inc(tap_done, 1)

                    def normalised(n):
                        dve.wait_ge(exp_done, 8 * p + n + 1)
                        v.reciprocal(rrow[:, n % 2:n % 2 + 1], psum_row[:, n % 2:n % 2 + 1])
                        dve.drain()
                        v.tensor_scalar(Pm[n % 2][:], Pm[n % 2][:], rrow[:, n % 2:n % 2 + 1], None,
                                        ALU.mult).then_inc(p_done, 1)

                    dve.wait_ge(s_done, 8 * p)
                    queries(0)
                    queries(1)
                    for n in range(8):
                        dve.wait_ge(s_done, 8 * p + n + 1)
                        v.tensor_reduce(nmax[:, n % 2:n % 2 + 1], bank(2 * (n % 2), KEYS), AX.X, ALU.max,
                                        negate=True).then_inc(max_done, 1)
                        if n:
                            normalised(n - 1)
                        taps(4 * n, 4 * n + 4)
                    normalised(7)
                    dve.wait_ge(mod_used, MOD_UP + 4 * p + 4)
                    for c in range(2):
                        ins = v.tensor_tensor(MOD[:, bass.ds(4 * p + MOD_UP, 4), c],
                                              bank(7, 8).rearrange("p (m c) -> p m c", c=2)[:, :, c],
                                              pk[:, bass.ds(4 * p + (_cols["b_mod"] + MOD_UP), 4)], ALU.add)
                    ins.then_inc(mod_evac, 1)
                    dve.wait_ge(o_hi, p + 1)
                    v.tensor_tensor(RL[:, p, :], bank(6), RH[:, p, :].bitcast(F32), ALU.subtract).then_inc(o_lo, 1)
            meet(dve, "dve", tl)
            if stop < 4:
                return
            dve.wait_ge(gate_in, 16)
            for n in range(8):
                lo_ahead(dve, R_WO + n // 4, n % 4)
                dve.wait_ge(unit_done, RING * R_WO + n + 1)
                v.tensor_tensor(Mg[:, n, :], bank(n % 4), gate_sb[:, n, :], ALU.mult).then_inc(wo_evac, 1)
            yk = lambda k: ypad[:, k, 0:T]
            dve_centre(dve, tl, yk)
            dve_rinv(dve, tl, T)
            dve_scaled(dve, tl, yk, KC, T, lambda k: VH[:, k, :], lambda k: VL[:, k, :])
            meet(dve, "dve", tl)
            dve.wait_ge(gate_in, 32)
            for n in range(8):
                lo_ahead(dve, R_PW + n // 4, n % 4)
                dve.wait_ge(unit_done, RING * R_PW + n + 1)
                v.tensor_tensor(f_sb[0][:], bank(n % 4), gate_sb[:, n, :], ALU.mult)
                dve.drain()
                v.tensor_tensor(Mg[:, n, :], Mg[:, n, :], f_sb[0][:], ALU.add).then_inc(pw_evac, 1)
                dve.wait_ge(m_hi, n + 1)
                v.tensor_tensor(RL[:, n, :], Mg[:, n, :], RH[:, n, :].bitcast(F32), ALU.subtract)
            meet(dve, "dve", tl)
            for n in range(8):
                lo_ahead(dve, R_OUT + n // 4, n % 4)
                dve.wait_ge(unit_done, RING * R_OUT + n + 1)
                v.scalar_tensor_tensor(X[:, n, :], bank(n % 4), MOD[:, 16 + n, 0:1], X[:, n, :],
                                       ALU.mult, ALU.add).then_inc(out_evac, 1)
            v.scalar_tensor_tensor(gain[:, :, 0], MOD[:, 32:40, 0], 1.0, col("norm2_g", 0, 8), ALU.add, ALU.mult)
            meet(dve, "dve", tl)
            dve_rinv(dve, tl, T)
            dve_scaled(dve, tl, xk, KC, T, rhk, rlk)
            meet(dve, "dve", tl)
            if stop < 5:
                return
            dve_retrieve(dve, tl)
            meet(dve, "dve", tl)
            if stop < 6:
                return
            dve.wait_ge(e_tp, 4)
            iob = iota[:].unsqueeze(1).to_broadcast([P, 8, P])
            with dve.Fori(0, 16) as i:
                for s in range(4):
                    dve.wait_ge(g_mm, 8 * i + max(2 * s - 2, 0))
                    for x in range(8):
                        t = 8 * s + x
                        v.tensor_scalar(A1[s % 2][:, x, :], iota[:], ET[0][:, bass.ds(i * 32 + t, 1)],
                                        ET[2][:, bass.ds(i * 32 + t, 1)], ALU.is_equal, ALU.mult)
                    e2 = ET[1][:, bass.ds(i * 32 + 8 * s, 8)].unsqueeze(2).to_broadcast([P, 8, P])
                    v.tensor_tensor(B1[s % 2][:], e2, iob, ALU.is_equal).then_inc(hot_done, 1)
            meet(dve, "dve", tl)
            for b in range(2):
                dve.wait_ge(g_out[b], 16 * 8)
            v.memset(Y[:], 0.0)
            if stop < 7:
                return

            def dve_up(r, par, n, loads):
                dve.wait_ge(gl_in[par], 16 * loads)
                for c in range(RING):
                    lo_ahead(dve, r, c)
                    dve.wait_ge(ge_done, RING * n + c + 1)
                    gl = GL[par][:, :, 32 * c:32 * c + 32]
                    v.tensor_tensor(wf[c % 2][:].rearrange("p (b t) -> p b t", b=16),
                                    ge[c % 2][:].rearrange("p (b t) -> p b t", b=16), gl,
                                    ALU.mult).then_inc(w_done, 1)
                    dve.wait_ge(wh_done, RING * n + c + 1)
                    v.tensor_tensor(WL[par][:, c, :], wf[c % 2][:], WH[par][:, c, :].bitcast(F32),
                                    ALU.subtract).then_inc(wl_done, 1)

            def dve_down(r, n):
                split_lo(dve, r, 3)
                for h in range(2):
                    for d in range(8):
                        dve.wait_ge(acc_mm, 16 * n + 8 * h + d + 1)
                        dve.wait_ge(acc_done, 16 * n + h * (d + 1))
                        v.tensor_tensor(Y[:, d, :], Y[:, d, :], bank(4 + d % 4), ALU.add).then_inc(acc_done, 1)
                    if h == 0:
                        split_lo(dve, r + 1, 0)
                        split_lo(dve, r + 1, 1)
                split_lo(dve, r + 1, 2)

            dve_up(R_UV, 0, 0, 1)
            with dve.Fori(0, 15) as i:
                for b in range(2):
                    n = i * 2 + 1 + b
                    dve_up(R_UV + 1 + i * 4 + 2 * b, 1 - b, n, i + b + 1)
                    dve_down(R_UV + 2 + i * 4 + 2 * b, n - 1)
            dve_up(R_UV + 61, 1, 31, 16)
            dve_down(R_UV + 62, 30)
            dve_down(R_UV + 63, 31)
            dve.drain()
            for k in range(KC):
                v.scalar_tensor_tensor(X[:, k, :], Y[:, k, :], MOD[:, 40 + k, 0:1], X[:, k, :],
                                       ALU.mult, ALU.add)
            v.tensor_scalar(gain[:, :, 0], MOD2[:, 8:16], 1.0, None, ALU.add)
            meet(dve, "dve", tl)
            dve_rinv(dve, tl, T)
            dve_scaled(dve, tl, xk, KC, T)
            dve_direct(dve, tl, KC, rhk, rlk)
            meet(dve, "dve", tl)
            if stop < 8:
                return
            v.memset(relb[BUCKETS:BUCKETS + 1, :], NEG).then_inc(relb_made, 1)
            for n in range(8):
                lo_ahead(dve, R_DSA_IN + n // 4, n % 4)
            dve_rinv(dve, tl, T)
            dve_scaled(dve, tl, lambda k: kvT[:, k, :], 2, T, lambda k: KVH[:, k, :], lambda k: KVL[:, k, :])
            dve.wait_ge(iw_tp, 1)
            v.tensor_copy(IW[:].rearrange("p b h -> p (b h)"), bank(5, TB * IDX_H)).then_inc(iw_evac, 1)
            meet(dve, "dve", tl)
            for b in range(1, TB):
                w = (b + 1) * P
                for h in range(IDX_H):
                    n = (b - 1) * IDX_H + h
                    dve.wait_ge(ix_relu, n + 1)
                    if h == 0:
                        v.tensor_scalar(score[b][:, 0:w], sq[n % 2][:, 0:w], IW[:, b, h:h + 1], None,
                                        ALU.mult).then_inc(ix_add, 1)
                    else:
                        v.scalar_tensor_tensor(score[b][:, 0:w], sq[n % 2][:, 0:w], IW[:, b, h:h + 1],
                                               score[b][:, 0:w], ALU.mult, ALU.add).then_inc(ix_add, 1)
                    dve.wait_ge(ix_add, n + 1)
                dve.drain().then_inc(ix_scored, 1)
            dve.wait_ge(ix_masked, TB - 1)
            with dve.Fori(0, SEL // 8) as i:
                for b in range(1, TB):
                    v.max(top8[:, b, :], score[b][:, 0:(b + 1) * P])
                dve.drain()
                for b in range(1, TB):
                    v.match_replace(score[b][:, 0:(b + 1) * P], top8[:, b, :], score[b][:, 0:(b + 1) * P], TAKEN)
                dve.drain()
            for b in range(1, TB):
                v.tensor_scalar(M[b][:, 0:(b + 1) * P], score[b][:, 0:(b + 1) * P], TAKEN, NEG,
                                ALU.not_equal, ALU.mult)
            meet(dve, "dve", tl)
            if stop < 9:
                return
            dve_attention(dve, tl, 0)
            meet(dve, "dve", tl)
            dve_residual_norm(dve, tl, R_AWO, 0, 0, awo_evac)
            if stop < 10:
                return
            dve_mlp(dve, tl, 0, R_MLP1)
            dve_post(dve, tl, 0, 1)
            if stop < 11:
                return
            dve.wait_ge(lam_in, 16)
            for x in range(2):
                v.tensor_tensor(ss[0][:, 64 * x:64 * x + 64], lb_sb[:, 128 * x:128 * x + 64],
                                lb_sb[:, 128 * x + 64:128 * x + 128], ALU.mult)
            dve.drain()
            v.tensor_reduce(lam[:, 0:2], ss[0][:, 0:128].rearrange("p (a b) -> p a b", a=2), AX.X,
                            ALU.add).then_inc(lam_exp, 1)
            dve.wait_ge(lam_exp, 2)
            v.tensor_tensor(lam[:, 4:5], lam[:, 2:3], lam[:, 3:4], ALU.subtract)
            v.tensor_scalar(lam[:, 5:6], col("b_subln"), 1.0 - LAM_INIT, None, ALU.mult)
            dve.drain()
            v.tensor_scalar(lam[:, 4:5], lam[:, 4:5], LAM_INIT, None, ALU.add)
            dve.drain()
            dve_attention(dve, tl, 1)
            meet(dve, "dve", tl)
            dve_residual_norm(dve, tl, R_BWO, 1, 0, bwo_evac)
            dve_mlp(dve, tl, 1, R_MLP2)
            dve_post(dve, tl, 1, 1)

        def pe_post(pe, tl, layer, which):
            meet(pe, "pe", tl)
            pe_means(pe, tl, xk)
            pe_sums(pe, tl, KC, T)
            meet(pe, "pe", tl)

        def pe_attention(pe, tl, a):
            A, mm = att[a], nc.tensor.matmul
            r0, units = ((R_DSA, 2), (R_DIFF, 3))[a]
            body = 2 if a == 0 else 4
            turns, main = (8, 4)[a], slab(RH, RL)
            kv = slab(KVH, KVL, 0, 2)
            with pe.Fori(0, PAIRS // body) as i:
                for pp in range(body):
                    p = i * body + pp
                    rr = lambda x: r0 + i * (units * body // 4) + (units * pp + x) // 4
                    jj = lambda x: (units * pp + x) % 4
                    if a == 0:
                        pe.wait_ge(A["q_ev"], p)
                    else:
                        pe.wait_ge(A["ort"], 2 * p)
                    pe_unit(pe, rr(0), jj(0), 7, main).then_inc(unit_done, 1)
                    pe.wait_ge(A["mx"], 8 * p)
                    if a == 0:
                        pe.wait_ge(lo_done, RING * rr(1) + jj(1) + 1)
                        product(jj(1), (0, 1), bank(0), kv).then_inc(A["k_mm"], 1)
                        product(jj(1), (2, 3), bank(2), kv).then_inc(unit_done, 1)
                    else:
                        pe_unit(pe, rr(1), jj(1), 0, main).then_inc(unit_done, 1)
                        pe_unit(pe, rr(2), jj(2), 2, main).then_inc(unit_done, 1)
                    pe.wait_ge(A["v_ev"], p + 1)
                    pe.wait_ge(A["te"], turns * p)
                    for c in range(TB):
                        ins = nc.tensor.transpose(bank(4)[:, c * P:(c + 1) * P],
                                                  vT2[:, c * P:(c + 1) * P], ident[:])
                    ins.then_inc(A["vt"], 1)

                    def scores(n):
                        m, b = order(a)[n]
                        if n == 0:
                            pe.wait_ge(A["q_ev"], p + 1)
                            pe.wait_ge(A["k_ev"], p + 1)
                        if n >= 2:
                            pe.wait_ge(A["mx"], 8 * p + n - 1)
                        o, w = 64 * m, (b + 1) * P
                        mm(bank(2 * (n % 2), w), q2[o:o + 64, b * P:(b + 1) * P], k2[o:o + 64, 0:w],
                           start=True, stop=True).then_inc(A["s"], 1)

                    def turn(x, src):
                        b = x % 4
                        pe.wait_ge(A["pd"], turns * p + x + 1)
                        if x == 0:
                            pe.wait_ge(A["vr"], p + 1)
                        if x >= 2:
                            pe.wait_ge(A["te"], turns * p + x - 1)
                        for c in range(b + 1):
                            ins = nc.tensor.transpose(bank(4 + x % 2)[:, c * P:(c + 1) * P],
                                                      src[:, c * P:(c + 1) * P], ident[:])
                        ins.then_inc(A["tp"], 1)

                    def values(m):
                        pe.wait_ge(A["te"], turns * p + (4 * m + 4 if a == 0 else 4))
                        if m == 0:
                            pe.wait_ge(A["ol"] if a == 0 else A["oh"], p)
                            pe.wait_ge(A["vr"], p + 1)
                        rows = slice(64 * m, 64 * m + 64) if a == 0 else slice(0, P)
                        for c in range(TB):
                            ins = mm(ps[rows, 6, c * P:T], v2[:, c, rows], PT2[:, c, c * P:T],
                                     start=(c == 0), stop=(c == TB - 1))
                        ins.then_inc(A["pv"], 1)

                    for n in range(8):
                        scores(n)
                        if a == 0 and n:
                            turn(n - 1, P2[(n - 1) % 2])
                        if a == 0 and n == 5:
                            values(0)
                        if a == 1 and n % 2 == 0 and n:
                            turn(n // 2 - 1, P2[0])
                    if a == 0:
                        turn(7, P2[1])
                        values(1)
                    else:
                        turn(3, P2[0])
                        values(0)
                        pe.wait_ge(A["osq"], p + 1)
                        mm(bank(7), ones[:], sq[0][:], start=True, stop=True).then_inc(A["oss"], 1)

        def pe_mlp(pe, tl, a, r0):
            L, main = mlp[a], slab(RH, RL)
            with pe.Fori(0, 2) as i:
                for n in range(16):
                    pe.wait_ge(L["free"], 16 * i + n + 1)
                    pe_unit(pe, r0 + i * 8 + n // 4, n % 4, n % 4, main).then_inc(unit_done, 1)
                for n in range(16):
                    d, g = n // 2, n % 2
                    pe.wait_ge(L["hl"], 16 * i + 16) if n == 0 else None
                    if g == 0:
                        pe.wait_ge(L["acc"], 8 * i + max(d - 3, 0))
                    pe_unit(pe, r0 + i * 8 + 4 + n // 4, n % 4, 4 + d % 4, slab(HH, HL, 8 * g),
                            start=(g == 0), stop=(g == 1)).then_inc(unit_done, 1)

        @block.tensor
        def _(pe):
            tl = Tally()
            mm = nc.tensor.matmul
            pe.wait_ge(cvec_done, 1)
            for m in range(MOD_UP):
                pe_mod(pe, m // 2 + 1, m % 2, bank(7)[:, 2 * m:2 * m + 2], 0)
            pe.wait_ge(consts_made, 1)
            pe_sums(pe, tl, KC, T)
            meet(pe, "pe", tl)
            pe_sums(pe, tl, KC, TC)
            meet(pe, "pe", tl)
            if stop < 2:
                return
            main = slab(RH, RL)
            for j in range(RING):
                u = pe_unit(pe, R_IN, j, j, main)
                if j >= 2:
                    u = product(j, range(8), bank(3 + j, TC), slab(CH, CL))
                u.then_inc(unit_done, 1)
            pe.wait_ge(in_evac_a, 2)
            pe.wait_ge(in_evac_d, 1)
            with pe.Fori(0, 4) as i:
                for j in range(RING):
                    pe.wait_ge(glu_done, 2 * i)
                    pe_unit(pe, R_CONV + i, j, j, main).then_inc(unit_done, 1)
            with pe.Fori(0, 4) as i:
                for j in range(RING):
                    pe.wait_ge(gate_free, RING * i + j + 1)
                    pe_unit(pe, R_GATE + i, j, j, main).then_inc(unit_done, 1)
            pe_sums(pe, tl, 2, T)
            pe_sums(pe, tl, 1, T)
            pe_sums(pe, tl, 1, TC)
            meet(pe, "pe", tl)
            if stop < 3:
                return
            cq = slab(CQH, CQL, 0, 2)
            with pe.Fori(0, 2) as i:
                for pp in range(4):
                    p = i * 4 + pp
                    pe.wait_ge(lo_done, RING * (R_MLA + i) + pp + 1)
                    pe.wait_ge(mod_evac, p)
                    product(pp, (0, 1), bank(7), cq).then_inc(gen_done, 1)
                    pe.wait_ge(exp_done, 8 * p)
                    for x in range(2):
                        b = 2 * x
                        product(pp, (4 + x,), bank(b), [(CKH[:, 0:T], CKL[:, 0:T])])
                        product(pp, (4 + x,), bank(b + 1, TC),
                                [(CKH[:, T:KEYS], CKL[:, T:KEYS])]).then_inc(gen_done, 1)
                    pe.wait_ge(q_evac, 2 * p + 1)
                    product(pp, (2, 3), bank(7), cq).then_inc(gen_done, 1)
                    pe.wait_ge(v_evac, p + 1)
                    pe.wait_ge(tp_evac, 8 * p)
                    for c in range(6):
                        ins = nc.tensor.transpose(bank(4, KEYS)[:, c * P:(c + 1) * P],
                                                  VT[:, c * P:(c + 1) * P], ident[:])
                        if c == 0:
                            ins.then_inc(unit_done, 1)
                    ins.then_inc(vt_done, 1)

                    def scores(n):
                        m, b = n // 4, n % 4
                        if n == 0:
                            pe.wait_ge(k_evac, p + 1)
                            pe.wait_ge(q_evac, 2 * p + 1)
                        elif n == 4:
                            pe.wait_ge(q_evac, 2 * p + 2)
                        if n >= 2:
                            pe.wait_ge(exp_done, 8 * p + n - 1)
                        q = QT[m][0:QK, b * P:(b + 1) * P]
                        o = 2 * (n % 2)
                        mm(bank(o), q, KT[m][0:QK, 0:T], start=True, stop=True)
                        mm(bank(o + 1, TC), q, KT[m][0:QK, T:KEYS], start=True, stop=True).then_inc(s_done, 1)

                    def turn(n):
                        pe.wait_ge(p_done, 8 * p + n + 1)
                        if n == 0:
                            pe.wait_ge(v_ready, p + 1)
                        else:
                            pe.wait_ge(tp_evac, 8 * p + n)
                        for c in range(6):
                            ins = nc.tensor.transpose(bank(4, KEYS)[:, c * P:(c + 1) * P],
                                                      Pm[n % 2][:, c * P:(c + 1) * P], ident[:])
                        ins.then_inc(tp_done, 1)

                    def values(m):
                        pe.wait_ge(tp_evac, 8 * p + 4 * m + 4)
                        if m == 0:
                            pe.wait_ge(o_lo, p)
                        for c in range(6):
                            ins = mm(ps[VD * m:VD * m + VD, 6, :], Vk[:, c, VD * m:VD * m + VD],
                                     PT[:, c, :], start=(c == 0), stop=(c == 5))
                        ins.then_inc(pv_done, 1)

                    for n in range(8):
                        scores(n)
                        if n:
                            turn(n - 1)
                        if 1 <= n <= 4:
                            pe.wait_ge(q_evac, 2 * p + 2)
                            pe_mod(pe, MOD_UP // 2 + 2 * p + (n - 1) // 2 + 1, (n - 1) % 2,
                                   bank(7)[:, 2 * n - 2:2 * n], 0)
                        if n == 5:
                            values(0)
                    turn(7)
                    values(1)
            meet(pe, "pe", tl)
            if stop < 4:
                return
            pe_dense8(pe, R_WO, wo_evac, main)
            pe.wait_ge(wo_evac, 8)
            yk = lambda k: ypad[:, k, 0:T]
            pe_means(pe, tl, yk)
            pe_sums(pe, tl, KC, T)
            meet(pe, "pe", tl)
            pe_dense8(pe, R_PW, pw_evac, slab(VH, VL))
            meet(pe, "pe", tl)
            pe_dense8(pe, R_OUT, out_evac, main)
            meet(pe, "pe", tl)
            pe_sums(pe, tl, KC, T)
            meet(pe, "pe", tl)
            if stop < 5:
                return
            pe.wait_ge(keys_in, 16)
            with pe.Fori(0, 4) as i:
                for j in range(RING):
                    pe.wait_ge(q_ready, 4 * i + max(j - 3, 0))
                    pe_unit(pe, R_PQ + i, j, j, main).then_inc(unit_done, 1)
                    for x in range(6):
                        pe_mod(pe, 24 + 12 * i + 3 * j + x // 2 + 1, x % 2,
                               ps[:, 6, bass.ds(48 * i + 12 * j + 2 * x, 2)], 2)
                    pe.wait_ge(q_ready, 4 * i + j + 1)
                    pe.wait_ge(sc_used, 4 * i + max(j - 1, 0))
                    for b in range(TB):
                        ins = mm(bank(4 + j % 2)[:, b * P:(b + 1) * P], qs[j % 2][:, b * P:(b + 1) * P],
                                 SK[:, i * 4 + j, :], start=True, stop=True)
                    ins.then_inc(sc_done, 1)
            meet(pe, "pe", tl)
            if stop < 6:
                return
            for m in range(3):
                for b in range(TB):
                    ins = nc.tensor.transpose(bank(m)[:, b * P:(b + 1) * P],
                                              E[m][:, b].rearrange("p h k -> p (h k)"), ident[:])
                ins.then_inc(e_tp, 1)
            with pe.Fori(0, 16) as i:
                for s in range(8):
                    pe.wait_ge(hot_done, 4 * i + s // 2 + 1)
                    pe.wait_ge(g_evac, 8 * i + max(s - 3, 0))
                    for x in range(4):
                        k = 4 * (s % 2) + x
                        ins = mm(bank(s % 4)[:, x * P:(x + 1) * P], A1[s // 2 % 2][:, k, :],
                                 B1[s // 2 % 2][:, k, :], start=True, stop=True)
                    ins.then_inc(g_mm, 1)
            meet(pe, "pe", tl)
            if stop < 7:
                return

            def up(r, n):
                for c in range(RING):
                    pe.wait_ge(ge_done, RING * n + c - 3) if not isinstance(n, int) or n else None
                    pe_unit(pe, r, c, c, main).then_inc(unit_done, 1)

            def down(r, par, n):
                pe.wait_ge(wl_done, RING * n + RING)
                for h in range(2):
                    pe.wait_ge(lo_done, RING * r + 2 * h + 2)
                    for d in range(8):
                        x = 8 * h + d
                        if x >= 4:
                            pe.wait_ge(acc_done, 16 * n + x - 3)
                        else:
                            pe.wait_ge(acc_done, 16 * n)
                        for c in (2 * h, 2 * h + 1):
                            ins = product(c, (d,), bank(4 + d % 4), [(WH[par][:, c, :], WL[par][:, c, :])],
                                          start=(c == 2 * h), stop=(c == 2 * h + 1))
                        ins.then_inc(acc_mm, 1)
                    pe.drain().then_inc(unit_done, 2)

            up(R_UV, 0)
            with pe.Fori(0, 15) as i:
                for b in range(2):
                    up(R_UV + 1 + i * 4 + 2 * b, i * 2 + 1 + b)
                    down(R_UV + 2 + i * 4 + 2 * b, b, i * 2 + b)
            up(R_UV + 61, 31)
            down(R_UV + 62, 0, 30)
            down(R_UV + 63, 1, 31)
            meet(pe, "pe", tl)
            pe_sums(pe, tl, KC, T)
            meet(pe, "pe", tl)
            if stop < 8:
                return
            for n in range(8):
                pe_unit(pe, R_DSA_IN + n // 4, n % 4, n, main).then_inc(unit_done, 1)
            pe.wait_ge(ix_evac, 8)
            pe_sums(pe, tl, 2, T)
            for b in range(TB):
                ins = nc.tensor.transpose(bank(5)[:, b * IDX_H:(b + 1) * IDX_H],
                                          iwT[0:IDX_H, b * P:(b + 1) * P], ident[0:IDX_H, 0:IDX_H])
            ins.then_inc(iw_tp, 1)
            pe.wait_ge(bias_tables, 32)
            pe.wait_ge(relb_made, 1)
            mm(ps[0:HEADS, 6, :], relb[:], hotz[:, 0:T], start=True, stop=True)
            mm(ps[0:HEADS, 7, 0:BIAS_Z - T], relb[:], hotz[:, T:BIAS_Z], start=True,
               stop=True).then_inc(bias_mm, 1)
            meet(pe, "pe", tl)
            for b in range(1, TB):
                for h in range(IDX_H):
                    n = (b - 1) * IDX_H + h
                    if n >= 4:
                        pe.wait_ge(ix_relu, n - 3)
                    o = 64 * (h % 2)
                    mm(bank(n % 4, (b + 1) * P), iqT[o:o + 64, h // 2, b * P:(b + 1) * P],
                       ikT[o:o + 64, 0:(b + 1) * P], start=True, stop=True).then_inc(ix_mm, 1)
            meet(pe, "pe", tl)
            if stop < 9:
                return
            pe_attention(pe, tl, 0)
            meet(pe, "pe", tl)
            pe_dense8(pe, R_AWO, awo_evac, slab(OH, OL))
            pe_post(pe, tl, 0, 0)
            if stop < 10:
                return
            pe_mlp(pe, tl, 0, R_MLP1)
            pe_post(pe, tl, 0, 1)
            if stop < 11:
                return
            pe_attention(pe, tl, 1)
            meet(pe, "pe", tl)
            pe_dense8(pe, R_BWO, bwo_evac, slab(OH, OL))
            pe_post(pe, tl, 1, 0)
            pe_mlp(pe, tl, 1, R_MLP2)
            pe_post(pe, tl, 1, 1)

    return nc


def rope_tables():
    rows = T // GRID_W
    r = np.repeat(np.arange(rows), GRID_W)
    c = np.tile(np.arange(GRID_W), rows)
    n = ROPE // 4
    freq = np.float32(10000.0) ** (-np.arange(n, dtype=np.float32) / np.float32(n))
    table = np.zeros((P, T), np.float32)
    for d in range(ROPE):
        ang = (r if d < ROPE // 2 else c).astype(np.float32) * freq[d % n]
        table[NOPE + d] = np.cos(ang)
        table[QK + d] = np.sin(ang) * (-1.0 if d % (2 * n) < n else 1.0)
    return table


def bias_one_hot():
    d = T - 1 - np.arange(BIAS_Z)
    exact = BUCKETS // 2
    n = np.maximum(d, 0)
    large = exact + (np.log(np.maximum(n, 1).astype(np.float32) / np.float32(exact)).astype(np.float32)
                     / np.float32(np.log(128 / exact)) * np.float32(BUCKETS - exact)).astype(np.int32)
    b = np.where(n < exact, n, np.minimum(large, BUCKETS - 1))
    b = np.where(d < 0, BUCKETS, b)
    return (np.arange(BUCKETS + 1)[:, None] == b[None, :]).astype(np.float32)


def kernel(**inputs):
    import concourse.bacc as bacc
    from concourse.bass_utils import run_bass_kernel_spmd

    a = {k: np.asarray(v) for k, v in inputs.items()}

    def tiles(w):
        n = w.shape[1] // P
        return w.reshape(8, P, n, P).transpose(2, 1, 0, 3)

    def zeros(*shape):
        return np.zeros(shape, np.float32)

    w_in = a["w_in"][0]
    swap = np.arange(ROPE) ^ (ROPE // 4)
    kr = w_in[:, 384:384 + ROPE]
    stream = [tiles(w_in[:, 0:384]), tiles(np.concatenate([zeros(D, NOPE), kr, kr[:, swap]], 1))]
    conv = tiles(w_in[:, 416:416 + 2 * D])
    stream.append(np.stack([conv[0:8], conv[8:16]], 1).reshape(16, P, 8, P))
    stream.append(tiles(w_in[:, 416 + 2 * D:416 + 4 * D]))
    uq = a["w_uq"][0].reshape(2, P, HEADS, QK)
    uq = np.concatenate([uq, uq[..., NOPE:][..., swap]], -1)
    ukv = a["w_ukv"][0].reshape(P, PAIRS, 2, NOPE + VD)
    pair = [uq[:, :, 0::2].transpose(2, 1, 0, 3), uq[:, :, 1::2].transpose(2, 1, 0, 3),
            ukv[..., 0:NOPE].reshape(P, PAIRS, 1, P).transpose(1, 0, 2, 3),
            ukv[..., NOPE:].reshape(P, PAIRS, 1, P).transpose(1, 0, 2, 3), zeros(PAIRS, P, 2, P)]
    stream.append(np.concatenate(pair, 2))
    stream += [tiles(a[n][0]) for n in ("w_o_mla", "w_pw", "w_out", "w_pq")]
    up = a["u_experts"][0].reshape(P, P, 8, P).transpose(1, 3, 2, 0)
    down = a["v_experts"][0].reshape(P, P, 8, P).transpose(1, 0, 2, 3)
    up, down = (x.reshape(CHUNK_ROUNDS, RING, P, 8, P) for x in (up, down))
    stream.append(up[0])
    for n in range(1, CHUNK_ROUNDS):
        stream += [up[n], down[n - 1]]
    stream.append(down[-1])
    wa = a["a_w_in_2"][0]
    ik = wa[:, 1792:1856]
    stream.append(tiles(np.concatenate([wa[:, 1024:1792], ik, ik, wa[:, 1856:1864], zeros(D, P - 8)], 1)))
    uk = a["a_w_uk_2"][0].reshape(PAIRS, 2, 64, 2, P).transpose(0, 4, 3, 1, 2).reshape(PAIRS, P, 2, P)
    uv = a["a_w_uv_2"][0].reshape(PAIRS, 2, 2, P, 64).transpose(0, 3, 2, 1, 4).reshape(PAIRS, P, 2, P)
    ukuv = np.concatenate([uk, uv, zeros(PAIRS, P, 4, P)], 2)
    stream.append(np.stack([tiles(wa[:, 0:D]), ukuv], 1).reshape(16, P, 8, P))
    stream.append(tiles(a["a_w_o_2"][0]))

    def mlp_units(layer):
        w1, w2 = a["mlp_w1_2"][layer], a["mlp_w2_2"][layer]
        parts = []
        for half in range(2):
            h = slice(half * 2048, (half + 1) * 2048)
            parts.append(tiles(w1[:, h]))
            x = w2[h].reshape(2, 8, P, 8, P)
            parts.append(x.transpose(3, 0, 2, 1, 4).reshape(16, P, 8, P))
        return parts

    stream += mlp_units(0)
    wb = a["b_w_in_2"][0]
    stream.append(np.stack([tiles(wb[:, D * x:D * (x + 1)]) for x in range(3)], 1).reshape(24, P, 8, P))
    stream.append(tiles(a["b_w_o_2"][0]))
    stream += mlp_units(1)
    stream.append(zeros(RING, P, 8, P))
    w_all = np.concatenate(stream, 0).reshape(-1, P, 8 * P)
    assert w_all.shape[0] == RING * (ROUNDS + 1), w_all.shape

    w_mods = np.concatenate([tiles(a["w_mod"][0]), tiles(a["ada_w_2"][0]), tiles(a["ada_w_2"][1])], 0)
    w_mods = w_mods.reshape(MODS, P, 8 * P)

    def cols(v):
        return np.ascontiguousarray(v.reshape(-1, P).T)

    cs = [a["c"].reshape(8, P), a["c_ctx"].reshape(8, P), a["c_2"].reshape(8, P), a["c_2"].reshape(8, P)]
    parts = [np.stack(cs, -1).transpose(1, 0, 2).reshape(P, 32), cols(a["b_mod"]), cols(a["ada_b_2"]),
             cols(a["norm1_g"]), cols(a["norm2_g"]), cols(a["q_norm_g"]), cols(a["kv_norm_g"]),
             a["conv_w"][0].reshape(CONV_W, 8, P).transpose(2, 1, 0).reshape(P, 8 * CONV_W),
             cols(a["conv_b"]), cols(a["conv_ln_g"]), cols(a["conv_ln_b"]), cols(a["final_g"]),
             cols(a["ln_g_2"]), cols(a["ln_b_2"]), cols(a["a_kv_norm_2"]), cols(a["b_subln_2"])]
    pack = np.concatenate(parts, 1)
    arrays = {
        "w_all": w_all, "w_mods": w_mods,
        "x_t": a["x"][0].T.reshape(8, P, T).transpose(1, 0, 2),
        "ctx_t": a["ctx"][0].T.reshape(8, P, TC).transpose(1, 0, 2),
        "pack": pack, "trig": rope_tables(),
        "sub_keys_t": a["sub_keys"][0].reshape(16, NK, P).transpose(2, 0, 1),
        "rel_bias": a["rel_bias_2"], "bias_hot": bias_one_hot(),
        "b_lambda": a["b_lambda_2"].reshape(1, 256),
    }
    arrays = {k: np.ascontiguousarray(v) for k, v in arrays.items()}
    nc = bacc.Bacc("TRN2", target_bir_lowering=False, num_devices=1)
    aps = [nc.dram_tensor(k, v.shape, F32, kind="ExternalInput").ap() for k, v in arrays.items()]
    out = nc.dram_tensor("out_t", [P, KC, T], F32, kind="ExternalOutput").ap()
    build(nc, *aps, out)
    r = run_bass_kernel_spmd(nc, [arrays], core_ids=[0])
    got = np.asarray(r.results[0]["out_t"])
    return np.ascontiguousarray(got.transpose(1, 0, 2).reshape(D, T).T).reshape(1, T, D)
```

```python
from contextlib import ExitStack

import numpy as np
import concourse.bass as bass
from concourse import mybir

F32 = mybir.dt.float32
F32R = mybir.dt.float32r
U32 = mybir.dt.uint32
ACT = mybir.ActivationFunctionType
ALU = mybir.AluOpType
AX = mybir.AxisListType

P = 128
D = 1024
KC = D // P
T = 512
TC = 256
TB = T // P
KEYS = T + TC
HEADS = 16
PAIRS = HEADS // 2
NOPE, ROPE, VD = 64, 32, 64
QK = NOPE + ROPE
CONV_W = 31
HALF_W = CONV_W // 2
PEER_H, TOPK, NK = 8, 16, 128
IDX_H = 8
SEL = 128
FF = 4096
EPS1, EPS2 = 1e-6, 1e-5
NEG = -1e30
LOWEST = -3.0e38
TAKEN = -1.0e38
SCALE1 = float(QK) ** -0.5
SCALE2 = 64.0 ** -0.5
IW_SCALE = float(IDX_H) ** -0.5 * 64.0 ** -0.5
ALPHA = 4.0 ** 0.25
LAM_INIT = 0.8 - 0.6 * float(np.exp(-0.3))
BUCKETS = 32
GRID_W = 64

RING = 4
AHEAD = 3

R_IN = 0
R_CONV = 1
R_GATE = R_CONV + 4
R_MLA = R_GATE + 4
R_WO = R_MLA + 2
R_PW = R_WO + 2
R_OUT = R_PW + 2
R_PQ = R_OUT + 2
R_UV = R_PQ + 4
R_DSA_IN = R_UV + 64
R_DSA = R_DSA_IN + 2
R_AWO = R_DSA + 4
R_MLP1 = R_AWO + 2
R_DIFF = R_MLP1 + 16
R_BWO = R_DIFF + 6
R_MLP2 = R_BWO + 2
ROUNDS = R_MLP2 + 16
CHUNK_ROUNDS = NK // RING

MOD_UP = 16
MODS = 48 + 96

_cols = {}
_at = 0
for _name, _n in [("c", 8 * 4), ("b_mod", 48), ("ada_b", 96), ("norm1_g", 8), ("norm2_g", 8),
                  ("q_norm_g", 2), ("kv_norm_g", 1), ("conv_w", 8 * CONV_W), ("conv_b", 8),
                  ("conv_ln_g", 8), ("conv_ln_b", 8), ("final_g", 8), ("ln_g", 32), ("ln_b", 32),
                  ("a_kv_norm", 2), ("b_subln", 1)]:
    _cols[_name] = _at
    _at += _n
PACK = _at
BIAS_Z = 640


def build(nc, w_all, w_mods, x_t, ctx_t, pack, trig, sub_keys, rel_bias, bias_hot, b_lambda, out):
    gates_dram = nc.dram_tensor("gates_scratch", [16, P, T], F32).ap()
    peer_gate_dram = nc.dram_tensor("peer_gate_scratch", [16, P, P * 32], F32).ap()
    bias_row_dram = nc.dram_tensor("bias_row_scratch", [HEADS, P, BIAS_Z], F32)
    bias_rows = bias_row_dram.ap()

    with ExitStack() as ctx:
        def sem(name):
            return ctx.enter_context(nc.semaphore(name))

        base = (nc.sbuf_base + 127) // 128 * 128

        def at(kb, name, shape, dt=F32):
            return nc.alloc_sbuf_tensor_at(name, shape, dt, offset=base + int(kb * 1024))

        raw = [at(4 * j, f"raw{j}", [P, 8, P]) for j in range(RING)]
        w_hi = [at(16 + 4 * j, f"w_hi{j}", [P, 8, P], F32R) for j in range(RING)]
        w_lo = [at(32 + 4 * j, f"w_lo{j}", [P, 8, P], F32R) for j in range(RING)]
        mod_raw = [at(48 + 4 * j, f"mod_raw{j}", [P, 8, P]) for j in range(2)]
        mod_up = [at(kb, f"mod_up{j}", [P, 8, 8, P]) for j, kb in enumerate((16, 72))]
        X = at(56, "X", [P, KC, T])
        RH = at(72, "RH", [P, KC, T], F32R)
        RL = at(88, "RL", [P, KC, T], F32R)
        sq = [at(104 + 2 * j, f"sq{j}", [P, T]) for j in range(2)]
        root = at(108, "root", [P, T])
        rinv = at(110, "rinv", [P, T])
        t_sb = [at(112 + 2 * j, f"t_sb{j}", [P, T]) for j in range(2)]
        f_sb = [at(116 + 2 * j, f"f_sb{j}", [P, T]) for j in range(2)]
        pk = at(120, "pk", [P, PACK])
        ident = at(122.5, "ident", [P, P])
        ones = at(123, "ones", [P, P])
        MOD = at(123.5, "MOD", [P, 48, 2])
        MOD2 = at(123.875, "MOD2", [P, 96])
        gain = at(124.25, "gain", [P, 8, 2])
        eps = at(124.375, "eps", [P, 2])
        nmax = at(124.4375, "nmax", [P, 2])
        psum_row = at(124.5, "psum_row", [P, 2])
        rrow = at(124.5625, "rrow", [P, 2])
        lam = at(124.625, "lam", [P, 8])
        cvec = at(124.6875, "cvec", [P, 8, 4])
        shift = at(124.8125, "shift", [P, 8])
        iota = at(125, "iota", [P, P])
        S = 125.5

        ypad = at(S, "ypad", [P, KC, T + 2 * HALF_W])
        KT = [at(S + 17 + 3 * m, f"KT{m}", [P, KEYS]) for m in range(2)]
        CQH = at(S + 23, "CQH", [P, 2, T], F32R)
        CQL = at(S + 27, "CQL", [P, 2, T], F32R)
        CKH = at(S + 31, "CKH", [P, KEYS], F32R)
        CKL = at(S + 34, "CKL", [P, KEYS], F32R)
        trig_sb = at(S + 37, "trig_sb", [P, T])
        CX = at(S + 39, "CX", [P, KC, TC])
        CH = at(S + 47, "CH", [P, KC, TC], F32R)
        CL = at(S + 55, "CL", [P, KC, TC], F32R)
        cqT = at(S + 63, "cqT", [P, 2, T])
        ckvT = at(S + 67, "ckvT", [P, KEYS])
        sig = [at(S + 70 + 2 * j, f"sig{j}", [P, T]) for j in range(2)]
        QT = [at(S + 39 + 2 * m, f"QT{m}", [P, T]) for m in range(2)]
        VT = at(S + 43, "VT", [P, KEYS])
        Vk = at(S + 46, "Vk", [P, 6, P])
        Pm = [at(S + kb, f"Pm{j}", [P, KEYS]) for j, kb in enumerate((49, 52, 67))]
        PT = at(S + 55, "PT", [P, 6, T])
        Mg = at(S + 17, "Mg", [P, KC, T])
        gate_sb = at(S + 33, "gate_sb", [P, KC, T])
        VH = at(S + 49, "VH", [P, KC, T], F32R)
        VL = at(S + 65, "VL", [P, KC, T], F32R)
        SK = at(S, "SK", [P, 16, P])
        qs = [at(S + 8 + 2 * j, f"qs{j}", [P, T]) for j in range(2)]
        left = at(S + 12, "left", [P, TB, NK])
        cand = at(S + 14, "cand", [P, TB, 256])
        cand2 = at(S + 18, "cand2", [P, TB, 256])
        hit = at(S + 22, "hit", [P, TB, 256])
        top_v = [at(S + 26 + m / 4, f"top_v{m}", [P, TB, TOPK]) for m in range(2)]
        top_i = [at(S + 26.5 + m / 4, f"top_i{m}", [P, TB, TOPK], U32) for m in range(2)]
        top_f = [at(S + 27 + m / 4, f"top_f{m}", [P, TB, TOPK]) for m in range(2)]
        best = at(S + 27.5, "best", [P, TB, TOPK])
        best_i = at(S + 27.75, "best_i", [P, TB, TOPK], U32)
        half_i = [at(S + 28 + m / 4, f"half_i{m}", [P, TB, TOPK], U32) for m in range(2)]
        half_f = [at(S + 28.5 + m / 4, f"half_f{m}", [P, TB, TOPK]) for m in range(2)]
        zsum = at(S + 29, "zsum", [P, TB * PEER_H])
        zmax = at(S + 29.25, "zmax", [P, TB * PEER_H])
        E = [at(S + 76 + 2 * m, f"E{m}", [P, TB, PEER_H, TOPK]) for m in range(3)]
        mod_ring = mod_raw + [at(S + 32 + 4 * j, f"mod_ring{j}", [P, 8, P]) for j in range(4)]
        Gs = [at(S + 16 * j, f"Gs{j}", [P, P, 32]) for j in range(2)]
        A1 = [at(S + 54 + 4 * j, f"A1_{j}", [P, 8, P]) for j in range(2)]
        B1 = [at(S + 62 + 4 * j, f"B1_{j}", [P, 8, P]) for j in range(2)]
        ET = [at(S + 70 + 2 * m, f"ET{m}", [P, T]) for m in range(3)]
        Y = at(S, "Y", [P, KC, T])
        GL = [at(S + 16 + 8 * j, f"GL{j}", [P, 16, P]) for j in range(2)]
        WH = [at(S + 32 + 8 * j, f"WH{j}", [P, RING, T], F32R) for j in range(2)]
        WL = [at(S + 48 + 8 * j, f"WL{j}", [P, RING, T], F32R) for j in range(2)]
        ge = [at(S + 64 + 2 * j, f"ge{j}", [P, T]) for j in range(2)]
        wf = [at(S + 68 + 2 * j, f"wf{j}", [P, T]) for j in range(2)]
        KVH = at(S, "KVH", [P, 2, T], F32R)
        KVL = at(S + 4, "KVL", [P, 2, T], F32R)
        M = [None] + [at(S + 8 + 2 * b, f"M{b + 1}", [P, T]) for b in range(3)]
        kvT = at(S + 14, "kvT", [P, 2, T])
        iqT = at(S + 18, "iqT", [P, 4, T])
        ikT = at(S + 26, "ikT", [P, T])
        iwT = at(S + 28, "iwT", [P, T])
        IW = at(S + 30, "IW", [P, TB, IDX_H])
        top8 = at(S + 30.25, "top8", [P, 4, 8])
        score = [None] + [at(S + 31 + 2 * b, f"score{b + 1}", [P, T]) for b in range(3)]
        hotz = at(S + 40, "hotz", [BUCKETS + 1, BIAS_Z])
        relb = at(S + 43, "relb", [BUCKETS + 1, HEADS])
        lb_sb = at(S + 34, "lb_sb", [P, 256])
        brow = at(S + 44, "brow", [HEADS, BIAS_Z])
        Tb = [at(S + 14 + 2 * j, f"Tb{j}", [P, T]) for j in range(4)]
        q2 = at(S + 22, "q2", [P, T])
        k2 = at(S + 24, "k2", [P, T])
        vT2 = at(S + 26, "vT2", [P, T])
        v2 = at(S + 28, "v2", [P, TB, P])
        ss = [at(S + 30 + 2 * j, f"ss{j}", [P, T]) for j in range(2)]
        P2 = [at(S + kb, f"P2_{j}", [P, T]) for j, kb in enumerate((34, 36, 78, 80))]
        PT2 = at(S + 38, "PT2", [P, TB, T])
        OH = at(S + 46, "OH", [P, KC, T], F32R)
        OL = at(S + 62, "OL", [P, KC, T], F32R)
        HH = at(S, "HH", [P, 16, T], F32R)
        HL = at(S + 32, "HL", [P, 16, T], F32R)
        Y2 = at(S + 64, "Y2", [P, KC, T])

        ps = ctx.enter_context(nc.psum_tensor("ps", [P, 8, T], F32))
        psf = ps[:].rearrange("p b t -> p (b t)")

        def bank(b, n=T):
            return psf[:, b * T:b * T + n]

        def col(name, k=0, n=1):
            c = _cols[name] + k
            return pk[:, c:c + n]

        consts_in = sem("consts_in")
        x_in, ctx_in = sem("x_in"), sem("ctx_in")
        landed = [sem(f"landed{j}") for j in range(RING)]
        hi_done, lo_done, unit_done = sem("hi_done"), sem("lo_done"), sem("unit_done")
        mod_landed = [sem(f"mod_landed{j}") for j in range(2)]
        up_in = [sem(f"up_in{q}") for q in range(4)]
        ring_landed = mod_landed + up_in
        fills_before = [16, 16, 1, 1, 1, 1]
        mod_used, mod_evac = sem("mod_used"), sem("mod_evac")
        consts_made, cvec_done = sem("consts_made"), sem("cvec_done")
        met = {n: sem(f"met_{n}") for n in ("pe", "act", "dve")}
        sq_done, sq_used, sums_done, root_done, rinv_done = (
            sem("sq_done"), sem("sq_used"), sem("sums_done"), sem("root_done"), sem("rinv_done"))
        norm_t, norm_f, norm_lo = sem("norm_t"), sem("norm_f"), sem("norm_lo")
        centred = sem("centred")
        x_made = sem("x_made")
        in_evac_a, in_evac_d = sem("in_evac_a"), sem("in_evac_d")
        sig_done, glu_done = sem("sig_done"), sem("glu_done")
        gate_free = sem("gate_free")
        gate_out = [sem(f"gate_out{j}") for j in range(2)]
        gen_done, q_evac, k_evac, v_evac, vt_done, v_ready = (
            sem("gen_done"), sem("q_evac"), sem("k_evac"), sem("v_evac"), sem("vt_done"), sem("v_ready"))
        s_done, max_done, exp_done, p_done, tp_done, tp_evac, pv_done, o_hi, o_lo = (
            sem("s_done"), sem("max_done"), sem("exp_done"), sem("p_done"), sem("tp_done"),
            sem("tp_evac"), sem("pv_done"), sem("o_hi"), sem("o_lo"))
        tap_done = sem("tap_done")
        wo_evac, pw_evac, out_evac, m_hi = sem("wo_evac"), sem("pw_evac"), sem("out_evac"), sem("m_hi")
        gate_in = sem("gate_in")
        q_ready, sc_done, sc_used = sem("q_ready"), sem("sc_done"), sem("sc_used")
        z_ready, z_exp = sem("z_ready"), sem("z_exp")
        e_tp, hot_done, g_mm, g_evac = sem("e_tp"), sem("hot_done"), sem("g_mm"), sem("g_evac")
        g_out = [sem(f"g_out{j}") for j in range(2)]
        gl_in = [sem(f"gl_in{j}") for j in range(2)]
        ge_done, w_done, wh_done, wl_done, acc_mm, acc_done = (
            sem("ge_done"), sem("w_done"), sem("wh_done"), sem("wl_done"), sem("acc_mm"), sem("acc_done"))
        ix_evac, iw_tp, iw_evac, ix_mm, ix_relu, ix_add = (
            sem("ix_evac"), sem("iw_tp"), sem("iw_evac"), sem("ix_mm"), sem("ix_relu"), sem("ix_add"))
        ix_scored, ix_masked = sem("ix_scored"), sem("ix_masked")
        bias_mm, bias_ev, bias_out = sem("bias_mm"), sem("bias_ev"), sem("bias_out")
        awo_evac, bwo_evac = sem("awo_evac"), sem("bwo_evac")
        lam_in, lam_exp = sem("lam_in"), sem("lam_exp")
        iota_made, keys_in, bias_tables, relb_made = (
            sem("iota_made"), sem("keys_in"), sem("bias_tables"), sem("relb_made"))
        out_done = sem("out_done")
        shared = ("q_ev", "k_ev", "v_ev", "vt", "vr", "s", "mx", "ex", "pd", "tp", "te", "pv", "oh", "ol")
        att = [{n: sem(f"{n}_{a}") for n in shared + own}
               for a, own in (("dsa", ("k_mm",)), ("diff", ("osq", "oss", "rt", "ort")))]
        bias_in4 = [[sem(f"bias_in_{a}{j}") for j in range(4)] for a in range(2)]
        mlp = [{n: sem(f"{n}_mlp{a}") for n in ("free", "sq", "hh", "hl", "acc")}
               for a in range(2)]

        block = ctx.enter_context(nc.Block())

        class Tally(dict):

            def __missing__(self, k):
                return 0

        def meet(e, who, tally):
            tally["meet"] += 1
            e.drain().then_inc(met[who], 1)
            for n in met:
                if n != who:
                    e.wait_ge(met[n], tally["meet"])

        def split_hi(act, r, j):
            act.wait_ge(landed[j], 16 * r + 16)
            if not (isinstance(r, int) and r == 0):
                act.wait_ge(unit_done, RING * r + j + 1 - RING)
            nc.scalar.activation(w_hi[j][:], raw[j][:], ACT.Copy).then_inc(hi_done, 1)

        def split_lo(dve, r, j):
            dve.wait_ge(hi_done, RING * r + j + 1)
            nc.vector.tensor_tensor(w_lo[j][:], raw[j][:], w_hi[j][:].bitcast(F32),
                                    ALU.subtract).then_inc(lo_done, 1)

        def ahead(r, j):
            return (r, j + AHEAD) if j + AHEAD < RING else (r + 1, j + AHEAD - RING)

        def hi_ahead(act, r, j):
            split_hi(act, *ahead(r, j))

        def lo_ahead(dve, r, j):
            split_lo(dve, *ahead(r, j))

        def product(slot, weight_tiles, out_ap, rhs_pairs, start=True, stop=True):
            last = None
            n = len(weight_tiles)
            for x, (k, (rh, rl)) in enumerate(zip(weight_tiles, rhs_pairs)):
                nc.tensor.matmul(out_ap, w_hi[slot][:, k, :], rh, start=start and x == 0, stop=False)
                nc.tensor.matmul(out_ap, w_hi[slot][:, k, :], rl, start=False, stop=False)
                last = nc.tensor.matmul(out_ap, w_lo[slot][:, k, :], rh, start=False,
                                        stop=stop and x == n - 1)
            return last

        def slab(h, l, lo=0, n=8):
            return [(h[:, k, :], l[:, k, :]) for k in range(lo, lo + n)]

        def pe_unit(pe, r, j, b, pairs, start=True, stop=True):
            pe.wait_ge(lo_done, RING * r + j + 1)
            return product(j, range(8), bank(b), pairs, start, stop)

        def pe_mod(pe, loads, m2, out_ap, which, tile=None):
            if tile is None:
                if which == 2:
                    loads = loads + fills_before[m2]
                pe.wait_ge(ring_landed[m2], 16 * loads)
                tile = mod_ring[m2][:]
            for k in range(8):
                mm = nc.tensor.matmul(out_ap, tile[:, k, :], cvec[:, k, which:which + 2],
                                      start=(k == 0), stop=(k == 7))
            mm.then_inc(mod_used, 1)

        def act_squares(act, tl, src, n, w, ready=None):
            for k in range(n):
                if ready is not None:
                    ready(k)
                if tl["sq"] >= 2:
                    act.wait_ge(sq_used, tl["sq"] - 1)
                nc.scalar.activation(sq[tl["sq"] % 2][:, 0:w], src(k), ACT.Square).then_inc(sq_done, 1)
                tl["sq"] += 1

        def pe_sums(pe, tl, n, w, b=4):
            if tl["root"]:
                pe.wait_ge(root_done, tl["root"])
            tl["root"] += 1
            for k in range(n):
                pe.wait_ge(sq_done, tl["sq"] + 1)
                nc.tensor.matmul(bank(b, w), ones[:], sq[tl["sq"] % 2][:, 0:w], start=(k == 0),
                                 stop=(k == n - 1)).then_inc(sq_used, 1)
                tl["sq"] += 1

        def act_root(act, tl, n, w, e, b=4):
            act.wait_ge(sq_used, tl["sq"])
            if tl["root"]:
                act.wait_ge(rinv_done, tl["root"])
            nc.scalar.activation(root[:, 0:w], bank(b, w), ACT.Sqrt, bias=eps[:, e:e + 1],
                                 scale=1.0 / (n * P)).then_inc(root_done, 1)
            tl["root"] += 1

        def dve_rinv(dve, tl, w):
            tl["root"] += 1
            dve.wait_ge(root_done, tl["root"])
            nc.vector.reciprocal(rinv[:, 0:w], root[:, 0:w]).then_inc(rinv_done, 1)
            dve.drain()

        def dve_scaled(dve, tl, src, n, w, hi=None, lo=None):
            def low(k):
                dve.wait_ge(norm_f, tl["f"] + k + 1)
                nc.vector.tensor_tensor(lo(k), f_sb[(tl["f"] + k) % 2][:, 0:w], hi(k).bitcast(F32),
                                        ALU.subtract).then_inc(norm_lo, 1)
            for k in range(n):
                g = tl["f"] + k
                if g >= 2:
                    dve.wait_ge(norm_f, g - 1)
                nc.vector.tensor_tensor(t_sb[g % 2][:, 0:w], src(k), rinv[:, 0:w],
                                        ALU.mult).then_inc(norm_t, 1)
                if hi is not None and k:
                    low(k - 1)
            if hi is not None:
                low(n - 1)
                tl["lo"] += n
            tl["f"] += n
            tl["t"] += n

        def act_affine(act, tl, n, w, func, a, b, hi=None, dst=None):
            for k in range(n):
                g = tl["f"]
                act.wait_ge(norm_t, tl["t"] + 1)
                if hi is not None:
                    if tl["lo"] >= 2:
                        act.wait_ge(norm_lo, tl["lo"] - 1)
                    nc.scalar.activation(hi(k), t_sb[g % 2][:, 0:w], func, bias=b(k), scale=a(k))
                    nc.scalar.activation(f_sb[g % 2][:, 0:w], t_sb[g % 2][:, 0:w], func, bias=b(k),
                                         scale=a(k)).then_inc(norm_f, 1)
                    tl["lo"] += 1
                else:
                    nc.scalar.activation(dst(k), t_sb[g % 2][:, 0:w], func, bias=b(k),
                                         scale=a(k)).then_inc(norm_f, 1)
                tl["f"] += 1
                tl["t"] += 1

        def pe_means(pe, tl, src):
            for k in range(KC):
                pe_mean(pe, tl, src, k)

        def pe_mean(pe, tl, src, k, made=False):
            if made:
                tl["made"] += 1
                pe.wait_ge(x_made, tl["made"])
            mm = nc.tensor.matmul(bank(5), ones[:], src(k), start=(k == 0), stop=(k == KC - 1))
            if k == KC - 1:
                mm.then_inc(sums_done, 1)
                tl["mean"] += 1

        def dve_centre(dve, tl, src):
            tl["mean"] += 1
            dve.wait_ge(sums_done, tl["mean"])
            nc.vector.tensor_scalar(rinv[:], bank(5), 1.0 / D, None, ALU.mult)
            dve.drain()
            for k in range(KC):
                nc.vector.tensor_tensor(src(k), src(k), rinv[:], ALU.subtract).then_inc(centred, 1)
            dve.drain()

        def act_centred(act, tl):
            def ready(k):
                tl["cen"] += 1
                act.wait_ge(centred, tl["cen"])
            return ready

        xk = lambda k: X[:, k, :]
        rhk = lambda k: RH[:, k, :]
        rlk = lambda k: RL[:, k, :]

        def pe_dense8(pe, r0, evac, pairs, tl=None):
            for n in range(8):
                if n >= 4:
                    pe.wait_ge(evac, n - 3)
                pe_unit(pe, r0 + n // 4, n % 4, n % 4, pairs).then_inc(unit_done, 1)
                if tl is not None and n >= 2:
                    pe_mean(pe, tl, xk, n - 2, made=True)
            if tl is not None:
                pe_mean(pe, tl, xk, 6, made=True)
                pe_mean(pe, tl, xk, 7, made=True)

        @block.sync
        def _(sp):
            def weights(r, j):
                sp.wait_ge(lo_done, RING * r + j + 1 - RING)
                sp.dma_start(raw[j][:].rearrange("p a b -> p (a b)"),
                             w_all[r * RING + j]).then_inc(landed[j], 16)

            def modulation(m, slot):
                sp.wait_ge(mod_used, m - 1)
                sp.dma_start(mod_raw[slot][:].rearrange("p a b -> p (a b)"),
                             w_mods[m]).then_inc(mod_landed[slot], 16)

            def modulation6(m, slot):
                sp.wait_ge(mod_used, m - 5)
                sp.dma_start(mod_ring[slot][:].rearrange("p a b -> p (a b)"),
                             w_mods[m]).then_inc(ring_landed[slot], 16)

            sp.dma_start(pk[:], pack).then_inc(consts_in, 16)
            sp.dma_start(trig_sb[:], trig).then_inc(consts_in, 16)
            for q in range(4):
                sp.dma_start(mod_up[q // 2][:, 4 * (q % 2):4 * (q % 2) + 4].rearrange("p m a b -> p m (a b)"),
                             w_mods[4 * q:4 * q + 4].rearrange("m p x -> p m x")).then_inc(up_in[q], 16)
                if q == 0:
                    sp.dma_start(X[:], x_t).then_inc(x_in, 16)
            sp.dma_start(CX[:], ctx_t).then_inc(ctx_in, 16)
            for j in range(RING):
                sp.dma_start(raw[j][:].rearrange("p a b -> p (a b)"), w_all[j]).then_inc(landed[j], 16)
            with sp.Fori(1, R_MLA + 1) as r:
                for j in range(RING):
                    weights(r, j)
            with sp.Fori(0, 2) as i:
                for j in range(RING):
                    weights(R_MLA + 1 + i, j)
                    for x in range(4):
                        modulation(i * 16 + (MOD_UP + 4 * j + x), x % 2)
            with sp.Fori(R_WO + 1, R_PQ + 1) as r:
                for j in range(RING):
                    weights(r, j)
            with sp.Fori(0, 4) as i:
                for j in range(RING):
                    weights(R_PQ + 1 + i, j)
                    if j == 0:
                        sp.wait_ge(met["dve"], 7)
                    for x in range(3):
                        modulation6(i * 12 + (MOD_UP + 32 + 3 * j + x), (3 * j + x) % 6)
            with sp.Fori(0, 8) as i:
                for x in range(6):
                    modulation6(i * 6 + (MOD_UP + 80 + x), x)
            with sp.Fori(R_UV + 1, ROUNDS + 1) as r:
                for j in range(RING):
                    weights(r, j)
            sp.wait_ge(met["act"], 24)
            sp.dma_start(out, X[:]).then_inc(out_done, 16)
            sp.wait_ge(out_done, 16)


        @block.gpsimd
        def _(pool):
            g = nc.gpsimd
            g.memset(ones[:], 1.0)
            g.memset(ident[:], 0.0)
            g.memset(eps[:, 0:1], EPS1)
            g.memset(eps[:, 1:2], EPS2)
            g.memset(ypad[:], 0.0)
            g.iota(iota[:], pattern=[[1, P]], base=0, channel_multiplier=0,
                   allow_small_or_imprecise_dtypes=True).then_inc(iota_made, 1)
            pool.drain()
            g.affine_select(out=ident[:], in_=ident[:], compare_op=ALU.not_equal, fill=1.0, base=0,
                            pattern=[[-1, P]], channel_multiplier=1).then_inc(consts_made, 1)
            with pool.Fori(0, 8) as i:
                for b in range(2):
                    pool.wait_ge(g_evac, 16 * i + 8 * b + 8)
                    pool.dma_start(peer_gate_dram[i * 2 + b],
                                   Gs[b][:].rearrange("p e t -> p (e t)")).then_inc(g_out[b], 16)
            for b in range(2):
                pool.wait_ge(g_out[b], 16 * 8)
            gd = peer_gate_dram.rearrange("b p (r x) -> p b r x", x=P)
            pool.wait_ge(met["dve"], 10)
            for b in range(2):
                pool.dma_start(GL[b][:], gd[:, :, b, :]).then_inc(gl_in[b], 16)
            with pool.Fori(1, CHUNK_ROUNDS // 2) as i:
                for b in range(2):
                    pool.wait_ge(w_done, 8 * i + 4 * b - 4)
                    pool.dma_start(GL[b][:], gd[:, :, i * 2 + b, :]).then_inc(gl_in[b], 16)
            for b in range(1, TB):
                pool.wait_ge(ix_scored, b)
                blk = score[b][:, b * P:(b + 1) * P]
                g.affine_select(out=blk, in_=blk, compare_op=ALU.is_ge, fill=LOWEST, base=0,
                                pattern=[[-1, P]], channel_multiplier=1).then_inc(ix_masked, 1)
            pool.wait_ge(bias_out, 16)
            for a in range(2):
                pool.wait_ge(met["dve"], (14, 19)[a])
                for p in range(PAIRS):
                    for m in range(2):
                        if p >= 2:
                            pool.wait_ge(att[a]["mx"], 8 * (p - 1))
                        src = bass.AP(bias_row_dram, (2 * p + m) * P * BIAS_Z + P - 1,
                                      [[BIAS_Z - 1, P], [1, T]])
                        pool.dma_start(Tb[2 * (p % 2) + m][:], src).then_inc(
                            bias_in4[a][2 * (p % 2) + m], 16)

        def order(a):
            return [(m, b) for m in range(2) for b in range(TB)] if a == 0 else \
                   [(m, b) for b in range(TB) for m in range(2)]

        def act_residual_norm(act, tl, r0, layer, which):
            for n in range(8):
                hi_ahead(act, r0 + n // 4, n % 4)
            act_post(act, tl, layer, which)

        def act_post(act, tl, layer, which):
            sc = nc.scalar
            meet(act, "act", tl)
            act_squares(act, tl, xk, KC, T, act_centred(act, tl))
            act_root(act, tl, KC, T, 1)
            c = (layer * 2 + which) * 8
            if (layer, which) != (1, 1):
                act_affine(act, tl, KC, T, ACT.Identity, lambda k: gain[:, k, 0:1],
                           lambda k: shift[:, k:k + 1], hi=rhk)
            else:
                act_affine(act, tl, KC, T, ACT.Identity, lambda k: col("ln_g", c + k),
                           lambda k: col("ln_b", c + k), dst=xk)
                act.drain()
            meet(act, "act", tl)

        def act_attention(act, tl, a):
            sc, A = nc.scalar, att[a]
            r0, units = ((R_DSA, 2), (R_DIFF, 3))[a]
            body = 4 // units if a == 0 else 4
            with act.Fori(0, PAIRS // body) as i:
                for pp in range(body):
                    p = i * body + pp
                    tiles = order(a)
                    for x in range(units):
                        u = units * pp + x
                        hi_ahead(act, r0 + i * (units * body // 4) + u // 4, u % 4)
                    rnd = lambda x: RING * (r0 + i * (units * body // 4)) + units * pp + x
                    act.wait_ge(A["s"], 8 * p)
                    if a == 0:
                        act.wait_ge(unit_done, rnd(1))
                        sc.activation(q2[:], bank(7), ACT.Copy, scale=SCALE2).then_inc(A["q_ev"], 1)
                    act.wait_ge(A["k_mm"], p + 1) if a == 0 else act.wait_ge(unit_done, rnd(1))
                    sc.activation(k2[:], bank(0), ACT.Copy).then_inc(A["k_ev"], 1)
                    act.wait_ge(unit_done, rnd(2))
                    act.wait_ge(A["vt"], p)
                    sc.activation(vT2[:], bank(2), ACT.Copy).then_inc(A["v_ev"], 1)
                    if a == 1:
                        act.wait_ge(unit_done, rnd(3))
                        sc.activation(q2[:], bank(7), ACT.Copy, scale=SCALE2).then_inc(A["q_ev"], 1)
                    act.wait_ge(A["vt"], p + 1)
                    act.wait_ge(A["pv"], (2, 1)[a] * p)
                    sc.activation(v2[:].rearrange("p c k -> p (c k)"), bank(4), ACT.Copy).then_inc(A["vr"], 1)

                    turns = (8, 4)[a]

                    def turned(x):
                        b = x % 4
                        act.wait_ge(A["tp"], turns * p + x + 1)
                        if b == 0:
                            act.wait_ge(A["pv"], (2, 1)[a] * p + x // 4)
                        sc.activation(PT2[:, 0:b + 1, b * P:(b + 1) * P],
                                      bank(4 + x % 2, (b + 1) * P).rearrange("p (c k) -> p c k", k=P),
                                      ACT.Copy).then_inc(A["te"], 1)

                    for n, (m, b) in enumerate(tiles):
                        w = (b + 1) * P
                        act.wait_ge(A["mx"], 8 * p + n + 1)
                        if a == 0:
                            act.wait_ge(A["tp"], 8 * p + max(n - 3, 0))
                        else:
                            act.wait_ge(A["tp"], 4 * p + max(n // 2 - 1, 0))
                        sc.activation(P2[n % 4][:, 0:w], ss[n % 2][:, 0:w], ACT.Exp,
                                      bias=nmax[:, n % 2:n % 2 + 1],
                                      accum_out=psum_row[:, n % 2:n % 2 + 1]).then_inc(A["ex"], 1)
                        if a == 0 and n >= 2:
                            turned(n - 2)
                        if a == 1 and n % 2 and n >= 3:
                            turned(n // 2 - 1)
                    if a == 0:
                        turned(6)
                    turned(turns - 1)
                    act.wait_ge(A["pv"], (2, 1)[a] * (p + 1))
                    if a == 0:
                        sc.activation(OH[:, p, :], bank(6), ACT.Copy).then_inc(A["oh"], 1)
                    else:
                        sc.activation(sq[0][:], bank(6), ACT.Square).then_inc(A["osq"], 1)
                        act.wait_ge(A["oss"], p + 1)
                        sc.activation(root[:], bank(7), ACT.Sqrt, bias=eps[:, 1:2],
                                      scale=1.0 / P).then_inc(A["rt"], 1)
                        act.wait_ge(A["oh"], p + 1)
                        act.wait_ge(A["ol"], p)
                        sc.activation(OH[:, p, :], t_sb[0][:], ACT.Copy, scale=lam[:, 5:6])
                        sc.activation(f_sb[0][:], t_sb[0][:], ACT.Copy, scale=lam[:, 5:6]).then_inc(A["ort"], 1)

        def act_mlp(act, tl, a, r0):
            sc, L = nc.scalar, mlp[a]
            act.drain().then_inc(L["free"], RING)
            with act.Fori(0, 2) as i:
                for n in range(16):
                    r, j = r0 + i * 8 + n // 4, n % 4
                    hi_ahead(act, r, j)
                    act.wait_ge(unit_done, RING * r + j + 1)
                    act.wait_ge(L["sq"], 16 * i + max(n - 1, 0))
                    sc.activation(t_sb[n % 2][:], bank(j), ACT.Relu).then_inc(L["free"], 1)
                    act.wait_ge(L["sq"], 16 * i + n + 1)
                    sc.activation(HH[:, n, :], f_sb[n % 2][:], ACT.Copy).then_inc(L["hh"], 1)
                for n in range(16):
                    hi_ahead(act, r0 + i * 8 + 4 + n // 4, n % 4)

        @block.scalar
        def _(act):
            tl = Tally()
            sc = nc.scalar
            act.wait_ge(consts_in, 32)
            sc.activation(cvec[:].rearrange("p a b -> p (a b)"), col("c", 0, 32), ACT.Silu).then_inc(cvec_done, 1)
            act.wait_ge(consts_made, 1)
            act.wait_ge(x_in, 16)
            act_squares(act, tl, xk, KC, T)
            act_root(act, tl, KC, T, 0)
            meet(act, "act", tl)
            act_affine(act, tl, KC, T, ACT.Identity, lambda k: gain[:, k, 0:1],
                       lambda k: MOD[:, k, 0:1], hi=rhk)
            act.wait_ge(ctx_in, 16)
            act_squares(act, tl, lambda k: CX[:, k, :], KC, TC)
            act_root(act, tl, KC, TC, 0)
            act_affine(act, tl, KC, TC, ACT.Identity, lambda k: gain[:, k, 1:2],
                       lambda k: MOD[:, k, 1:2], hi=lambda k: CH[:, k, :])
            for j in range(AHEAD):
                split_hi(act, 0, j)
            meet(act, "act", tl)
            for j in range(RING):
                hi_ahead(act, R_IN, j)
                if j < 2:
                    act.wait_ge(unit_done, j + 1)
                    sc.activation(cqT[:, j, :], bank(j), ACT.Copy).then_inc(in_evac_a, 1)
            with act.Fori(0, 4) as i:
                for j in range(RING):
                    hi_ahead(act, R_CONV + i, j)
                    if j % 2:
                        act.wait_ge(unit_done, RING * (R_CONV + i) + j + 1)
                        act.wait_ge(glu_done, 2 * i)
                        sc.activation(sig[j // 2][:], bank(j), ACT.Sigmoid).then_inc(sig_done, 1)
            act.wait_ge(glu_done, 8)
            act.drain().then_inc(gate_free, RING)
            with act.Fori(0, 4) as i:
                for j in range(RING):
                    hi_ahead(act, R_GATE + i, j)
                    act.wait_ge(unit_done, RING * (R_GATE + i) + j + 1)
                    act.wait_ge(gate_out[j % 2], 32 * i + 16 * (j // 2))
                    sc.activation(sig[j % 2][:], bank(j), ACT.Sigmoid).then_inc(gate_free, 1)
                    act.wait_ge(gate_free, RING * i + j + 1 + RING)
                    act.dma_start(gates_dram[i * 4 + j], sig[j % 2][:]).then_inc(gate_out[j % 2], 16)
            act_squares(act, tl, lambda k: cqT[:, k, :], 2, T)
            act_root(act, tl, 2, T, 0)
            act_affine(act, tl, 2, T, ACT.Identity, lambda k: col("q_norm_g", k),
                       lambda k: 0.0, hi=lambda k: CQH[:, k, :])
            for lo, w in ((0, T), (T, TC)):
                act_squares(act, tl, lambda k: ckvT[:, lo:lo + w], 1, w)
                act_root(act, tl, 1, w, 0)
                act_affine(act, tl, 1, w, ACT.Identity, lambda k: col("kv_norm_g"), lambda k: 0.0,
                           hi=lambda k: CKH[:, lo:lo + w])
            for j in range(2):
                act.wait_ge(gate_out[j], 16 * 8)
            meet(act, "act", tl)
            def keys_values(i, pp):
                p = i * 4 + pp
                act.wait_ge(gen_done, 4 * p + 1)
                act.wait_ge(s_done, 8 * p)
                sc.activation(KT[0][0:NOPE, :], psf[0:NOPE, 0:KEYS], ACT.Copy)
                sc.activation(KT[1][0:NOPE, :], psf[NOPE:P, 0:KEYS], ACT.Copy).then_inc(k_evac, 1)
                act.wait_ge(gen_done, 4 * p + 2)
                act.wait_ge(vt_done, p)
                sc.activation(VT[:], bank(2, KEYS), ACT.Copy).then_inc(v_evac, 1)

            with act.Fori(0, 2) as i:
                for pp in range(4):
                    p = i * 4 + pp
                    hi_ahead(act, R_MLA + i, pp)
                    if pp == 0:
                        keys_values(i, 0)
                    act.wait_ge(vt_done, p + 1)
                    act.wait_ge(pv_done, 2 * p)
                    sc.activation(Vk[:].rearrange("p c k -> p (c k)"), bank(4, KEYS),
                                  ACT.Copy).then_inc(v_ready, 1)

                    def turned(n):
                        act.wait_ge(tp_done, 8 * p + n + 1)
                        if n == 0 or n == 4:
                            act.wait_ge(pv_done, 2 * p + n // 4)
                        sc.activation(PT[:, :, (n % 4) * P:(n % 4 + 1) * P],
                                      bank(4, KEYS).rearrange("p (c k) -> p c k", c=6),
                                      ACT.Copy).then_inc(tp_evac, 1)

                    for n in range(8):
                        act.wait_ge(max_done, 8 * p + n + 1)
                        act.wait_ge(tp_done, 8 * p + max(n - 2, 0))
                        sc.activation(Pm[n % 3][:], bank(2 * (n % 2), KEYS), ACT.Exp,
                                      bias=nmax[:, n % 2:n % 2 + 1],
                                      accum_out=psum_row[:, n % 2:n % 2 + 1]).then_inc(exp_done, 1)
                        if n >= 2:
                            turned(n - 2)
                    turned(6)
                    turned(7)
                    if pp < 3:
                        keys_values(i, pp + 1)
                    act.wait_ge(pv_done, 2 * p + 2)
                    sc.activation(RH[:, p, :], bank(6), ACT.Copy).then_inc(o_hi, 1)
            meet(act, "act", tl)
            act.dma_start(gate_sb[:], gates_dram[0:8].rearrange("k p t -> p k t")).then_inc(gate_in, 16)
            for n in range(8):
                hi_ahead(act, R_WO + n // 4, n % 4)
            act_squares(act, tl, lambda k: ypad[:, k, 0:T], KC, T, act_centred(act, tl))
            act_root(act, tl, KC, T, 0)
            act.wait_ge(wo_evac, 8)
            act.dma_start(gate_sb[:], gates_dram[8:16].rearrange("k p t -> p k t")).then_inc(gate_in, 16)
            act_affine(act, tl, KC, T, ACT.Silu, lambda k: col("conv_ln_g", k),
                       lambda k: col("conv_ln_b", k), hi=lambda k: VH[:, k, :])
            meet(act, "act", tl)
            for n in range(8):
                hi_ahead(act, R_PW + n // 4, n % 4)
                act.wait_ge(pw_evac, n + 1)
                sc.activation(RH[:, n, :], Mg[:, n, :], ACT.Copy).then_inc(m_hi, 1)
            meet(act, "act", tl)
            for n in range(8):
                hi_ahead(act, R_OUT + n // 4, n % 4)
            meet(act, "act", tl)
            act_squares(act, tl, xk, KC, T)
            act_root(act, tl, KC, T, 0)
            act_affine(act, tl, KC, T, ACT.Identity, lambda k: gain[:, k, 0:1],
                       lambda k: MOD[:, 24 + k, 0:1], hi=rhk)
            meet(act, "act", tl)
            act.dma_start(SK[:], sub_keys).then_inc(keys_in, 16)
            with act.Fori(0, 4) as i:
                for j in range(RING):
                    hi_ahead(act, R_PQ + i, j)
                    act.wait_ge(unit_done, RING * (R_PQ + i) + j + 1)
                    act.wait_ge(sc_done, 4 * i + max(j - 1, 0))
                    sc.activation(qs[j % 2][:], bank(j), ACT.Copy).then_inc(q_ready, 1)
            act.wait_ge(z_ready, 1)
            ev = E[2][:].rearrange("p a b c -> p (a b c)")
            sc.activation(ev, ev, ACT.Exp).then_inc(z_exp, 1)
            meet(act, "act", tl)
            for m in range(3):
                act.wait_ge(e_tp, m + 1)
                sc.activation(ET[m][:], bank(m), ACT.Copy)
            act.drain().then_inc(e_tp, 1)
            with act.Fori(0, 8) as i:
                for b in range(2):
                    act.wait_ge(g_out[b], 16 * i)
                    for s in range(8):
                        act.wait_ge(g_mm, 16 * i + 8 * b + s + 3)
                        sc.activation(Gs[b][:, :, 4 * s:4 * s + 4],
                                      bank(s % 4).rearrange("p (t e) -> p e t", t=4),
                                      ACT.Copy).then_inc(g_evac, 1)
            meet(act, "act", tl)
            def act_up(r, par, n):
                for c in range(RING):
                    hi_ahead(act, r, c)
                    act.wait_ge(unit_done, RING * r + c + 1)
                    sc.activation(ge[c % 2][:], bank(c), ACT.Gelu).then_inc(ge_done, 1)
                    act.wait_ge(w_done, RING * n + c + 1)
                    sc.activation(WH[par][:, c, :], wf[c % 2][:], ACT.Copy).then_inc(wh_done, 1)

            def act_down(r):
                split_hi(act, r, 3)
                split_hi(act, r + 1, 0)
                split_hi(act, r + 1, 1)
                split_hi(act, r + 1, 2)

            act_up(R_UV, 0, 0)
            with act.Fori(0, 15) as i:
                for b in range(2):
                    act_up(R_UV + 1 + i * 4 + 2 * b, 1 - b, i * 2 + 1 + b)
                    act_down(R_UV + 2 + i * 4 + 2 * b)
            act_up(R_UV + 61, 1, 31)
            act_down(R_UV + 62)
            act_down(R_UV + 63)
            meet(act, "act", tl)
            act_squares(act, tl, xk, KC, T)
            act_root(act, tl, KC, T, 0)
            act_affine(act, tl, KC, T, ACT.Identity, lambda k: gain[:, k, 0:1],
                       lambda k: MOD2[:, k:k + 1], hi=rhk)
            meet(act, "act", tl)
            act.dma_start(hotz[:], bias_hot).then_inc(bias_tables, 16)
            act.dma_start(relb[0:BUCKETS, :], rel_bias).then_inc(bias_tables, 16)
            for n in range(8):
                hi_ahead(act, R_DSA_IN + n // 4, n % 4)
                act.wait_ge(unit_done, RING * R_DSA_IN + n + 1)
                dst = kvT[:, n, :] if n < 2 else iqT[:, n - 2, :] if n < 6 else ikT[:] if n == 6 else None
                if dst is not None:
                    sc.activation(dst, bank(n), ACT.Copy).then_inc(ix_evac, 1)
                else:
                    sc.activation(iwT[0:IDX_H, :], psf[0:IDX_H, n * T:(n + 1) * T], ACT.Copy,
                                  scale=IW_SCALE).then_inc(ix_evac, 1)
            act.drain()
            act_squares(act, tl, lambda k: kvT[:, k, :], 2, T)
            act_root(act, tl, 2, T, 1)
            act_affine(act, tl, 2, T, ACT.Identity, lambda k: col("a_kv_norm", k), lambda k: 0.0,
                       hi=lambda k: KVH[:, k, :])
            act.wait_ge(bias_mm, 1)
            sc.activation(brow[:], psf[0:HEADS, 6 * T:6 * T + BIAS_Z], ACT.Copy).then_inc(bias_ev, 1)
            act.wait_ge(bias_ev, 1)
            act.dma_start(bias_rows, brow[:].unsqueeze(1).to_broadcast([HEADS, P, BIAS_Z])).then_inc(bias_out, 16)
            meet(act, "act", tl)
            for b in range(1, TB):
                for h in range(IDX_H):
                    n = (b - 1) * IDX_H + h
                    act.wait_ge(ix_mm, n + 1)
                    if n >= 2:
                        act.wait_ge(ix_add, n - 1)
                    w = (b + 1) * P
                    sc.activation(sq[n % 2][:, 0:w], bank(n % 4, w), ACT.Relu).then_inc(ix_relu, 1)
            act.wait_ge(bias_out, 16)
            meet(act, "act", tl)
            act_attention(act, tl, 0)
            meet(act, "act", tl)
            act_residual_norm(act, tl, R_AWO, 0, 0)
            act_mlp(act, tl, 0, R_MLP1)
            act_post(act, tl, 0, 1)
            act.dma_start(lb_sb[:], bass.AP(b_lambda.tensor, 0, [[0, P], [1, 256]])).then_inc(lam_in, 16)
            act.wait_ge(lam_exp, 1)
            sc.activation(lam[:, 2:4], lam[:, 0:2], ACT.Exp).then_inc(lam_exp, 1)
            act_attention(act, tl, 1)
            meet(act, "act", tl)
            act_residual_norm(act, tl, R_BWO, 1, 0)
            act_mlp(act, tl, 1, R_MLP2)
            act_post(act, tl, 1, 1)

        def dve_retrieve(dve, tl):
            v = nc.vector
            dve.wait_ge(iota_made, 1)
            io16 = iota[:, 0:TOPK].unsqueeze(1).to_broadcast([P, TOPK, TOPK])
            with dve.Fori(0, 4) as i:
                for j in range(RING):
                    lo_ahead(dve, R_PQ + i, j)
                    m = j % 2
                    dve.wait_ge(sc_done, RING * i + j + 1)
                    v.memset(nmax[:, 0:1], 0.0)
                    src = ps[:, 4 + m, :].rearrange("p (b k) -> p b k", b=TB)
                    for b in range(TB):
                        v.max(top_v[m][:, b, 0:8], src[:, b, :])
                    dve.drain()
                    for b in range(TB):
                        v.max_index(top_i[m][:, b, 0:8], top_v[m][:, b, 0:8], src[:, b, :])
                        v.match_replace(left[:, b, :], top_v[m][:, b, 0:8], src[:, b, :], LOWEST)
                    dve.drain().then_inc(sc_used, 1)
                    for b in range(TB):
                        v.max(top_v[m][:, b, 8:16], left[:, b, :])
                    dve.drain()
                    for b in range(TB):
                        v.max_index(top_i[m][:, b, 8:16], top_v[m][:, b, 8:16], left[:, b, :])
                    dve.drain()
                    v.tensor_copy(top_f[m][:], top_i[m][:])
                    if m == 0:
                        continue
                    h = i * 2 + j // 2
                    for b in range(TB):
                        v.tensor_tensor(cand[:, b, :].rearrange("p (x y) -> p x y", x=TOPK),
                                        top_v[0][:, b, :].unsqueeze(2).to_broadcast([P, TOPK, TOPK]),
                                        top_v[1][:, b, :].unsqueeze(1).to_broadcast([P, TOPK, TOPK]), ALU.add)
                    dve.drain()
                    for b in range(TB):
                        v.max(best[:, b, 0:8], cand[:, b, :])
                    dve.drain()
                    for b in range(TB):
                        v.max_index(best_i[:, b, 0:8], best[:, b, 0:8], cand[:, b, :])
                        v.match_replace(cand2[:, b, :], best[:, b, 0:8], cand[:, b, :], LOWEST)
                    dve.drain()
                    for b in range(TB):
                        v.max(best[:, b, 8:16], cand2[:, b, :])
                    dve.drain()
                    for b in range(TB):
                        v.max_index(best_i[:, b, 8:16], best[:, b, 8:16], cand2[:, b, :])
                    dve.drain()
                    v.tensor_single_scalar(half_i[0][:], best_i[:], 4, ALU.logical_shift_right)
                    v.tensor_single_scalar(half_i[1][:], best_i[:], TOPK - 1, ALU.bitwise_and)
                    v.tensor_copy(E[2][:, :, h, :], best[:])
                    dve.drain()
                    for x in range(2):
                        v.tensor_copy(half_f[x][:], half_i[x][:])
                    dve.drain()
                    for x in range(2):
                        for b in range(TB):
                            v.tensor_tensor(hit[:, b, :].rearrange("p (x y) -> p x y", x=TOPK),
                                            half_f[x][:, b, :].unsqueeze(2).to_broadcast([P, TOPK, TOPK]),
                                            io16, ALU.is_equal)
                        dve.drain()
                        for b in range(TB):
                            hb = hit[:, b, :].rearrange("p (x y) -> p x y", x=TOPK)
                            v.tensor_tensor(hb, hb, top_f[x][:, b, :].unsqueeze(1).to_broadcast([P, TOPK, TOPK]),
                                            ALU.mult)
                        dve.drain()
                        v.tensor_reduce(E[x][:, :, h, :], hit[:].rearrange("p b (x y) -> p b x y", x=TOPK),
                                        AX.X, ALU.add)
                        dve.drain()
            bv = E[2][:].rearrange("p b h k -> p (b h) k")
            v.tensor_copy(zmax[:], bv[:, :, 0])
            dve.drain()
            v.tensor_tensor(bv, bv, zmax[:].unsqueeze(2).to_broadcast([P, TB * PEER_H, TOPK]), ALU.subtract)
            dve.drain().then_inc(z_ready, 1)
            dve.wait_ge(z_exp, 1)
            v.tensor_reduce(zsum[:], bv, AX.X, ALU.add)
            dve.drain()
            v.reciprocal(zsum[:], zsum[:])
            dve.drain()
            v.tensor_tensor(bv, bv, zsum[:].unsqueeze(2).to_broadcast([P, TB * PEER_H, TOPK]), ALU.mult)

        def dve_residual_norm(dve, tl, r0, layer, which, evac):
            v = nc.vector
            g0 = 48 * layer + 16
            v.tensor_scalar(gain[:, :, 1], MOD2[:, g0:g0 + 8], 1.0, None, ALU.add)
            dve.drain()
            for n in range(8):
                lo_ahead(dve, r0 + n // 4, n % 4)
                dve.wait_ge(unit_done, RING * r0 + n + 1)
                v.tensor_scalar(f_sb[0][:], bank(n % 4), gain[:, n, 1:2], None, ALU.mult).then_inc(evac, 1)
                dve.drain()
                v.scalar_tensor_tensor(X[:, n, :], X[:, n, :], ALPHA, f_sb[0][:], ALU.mult,
                                       ALU.add).then_inc(x_made, 1)
                dve.drain()
            dve_post(dve, tl, layer, which)

        def dve_post(dve, tl, layer, which):
            v = nc.vector
            last = (layer, which) == (1, 1)
            if which == 1:
                g0 = 48 * layer + 40
                v.tensor_scalar(gain[:, :, 1], MOD2[:, g0:g0 + 8], 1.0, None, ALU.add)
            c = (layer * 2 + which) * 8
            if not last:
                s0 = 48 * layer + 24 if which == 0 else 48
                g = gain[:, :, 0]
                v.tensor_scalar(g, MOD2[:, s0 + 8:s0 + 16], 1.0, None, ALU.add)
                dve.drain()
                v.tensor_tensor(shift[:], g, col("ln_b", c, 8), ALU.mult)
                dve.drain()
                v.tensor_tensor(g, g, col("ln_g", c, 8), ALU.mult)
                v.tensor_tensor(shift[:], shift[:], MOD2[:, s0:s0 + 8], ALU.add)
            meet(dve, "dve", tl)
            if which == 1:
                for k in range(KC):
                    v.scalar_tensor_tensor(X[:, k, :], Y2[:, k, :], gain[:, k, 1:2], X[:, k, :],
                                           ALU.mult, ALU.add).then_inc(x_made, 1)
            dve_centre(dve, tl, xk)
            dve_rinv(dve, tl, T)
            if last:
                dve_scaled(dve, tl, xk, KC, T)
            else:
                dve_scaled(dve, tl, xk, KC, T, rhk, rlk)
            meet(dve, "dve", tl)
            if not last:
                for k in range(KC):
                    v.scalar_tensor_tensor(X[:, k, :], X[:, k, :], col("ln_g", c + k), rinv[:],
                                           ALU.mult, ALU.mult)
                dve.drain()
                for k in range(KC):
                    v.tensor_scalar(X[:, k, :], X[:, k, :], col("ln_b", c + k),
                                    ALPHA if which == 0 else 1.0, ALU.add, ALU.mult)

        def dve_attention(dve, tl, a):
            v, A = nc.vector, att[a]
            r0, units = ((R_DSA, 2), (R_DIFF, 3))[a]
            body = 2 if a == 0 else 4
            turns = (8, 4)[a]
            with dve.Fori(0, PAIRS // body) as i:
                for pp in range(body):
                    p = i * body + pp
                    for x in range(units):
                        u = units * pp + x
                        lo_ahead(dve, r0 + i * (units * body // 4) + u // 4, u % 4)

                    def normalised(n):
                        m, b = order(a)[n]
                        w = (b + 1) * P
                        c = slice(n % 2, n % 2 + 1)
                        dve.wait_ge(A["ex"], 8 * p + n + 1)
                        v.reciprocal(rrow[:, c], psum_row[:, c])
                        dve.drain()
                        if a == 0:
                            v.tensor_scalar(P2[n % 4][:, 0:w], P2[n % 4][:, 0:w], rrow[:, c], None,
                                            ALU.mult).then_inc(A["pd"], 1)
                        elif m == 1:
                            p0, p1 = P2[(n - 1) % 4][:, 0:w], P2[n % 4][:, 0:w]
                            v.tensor_scalar(p1, p1, rrow[:, 1:2], lam[:, 4:5],
                                            ALU.mult, ALU.mult)
                            dve.drain()
                            v.scalar_tensor_tensor(p0, p0, rrow[:, 0:1], p1, ALU.mult, ALU.subtract).then_inc(A["pd"], 1)

                    for n, (m, b) in enumerate(order(a)):
                        w = (b + 1) * P
                        if b == 0:
                            dve.wait_ge(bias_in4[a][2 * (pp % 2) + m], 16 * (body // 2) * i + 16 * (pp // 2) + 16)
                        dve.wait_ge(A["s"], 8 * p + n + 1)
                        tb = Tb[2 * (pp % 2) + m][:, (TB - 1 - b) * P:TB * P]
                        s = ss[n % 2][:, 0:w]
                        v.tensor_tensor(s, bank(2 * (n % 2), w), tb, ALU.add)
                        dve.drain()
                        if a == 0 and b:
                            v.tensor_tensor(s, s, M[b][:, 0:w], ALU.add)
                            dve.drain()
                        v.tensor_reduce(nmax[:, n % 2:n % 2 + 1], s, AX.X, ALU.max,
                                        negate=True).then_inc(A["mx"], 1)
                        if n:
                            normalised(n - 1)
                    normalised(7)
                    if a == 0:
                        dve.wait_ge(A["oh"], p + 1)
                        v.tensor_tensor(OL[:, p, :], bank(6), OH[:, p, :].bitcast(F32),
                                        ALU.subtract).then_inc(A["ol"], 1)
                    else:
                        dve.wait_ge(A["rt"], p + 1)
                        v.reciprocal(rinv[:], root[:])
                        dve.drain()
                        v.tensor_tensor(t_sb[0][:], bank(6), rinv[:], ALU.mult).then_inc(A["oh"], 1)
                        dve.wait_ge(A["ort"], p + 1)
                        v.tensor_tensor(OL[:, p, :], f_sb[0][:], OH[:, p, :].bitcast(F32),
                                        ALU.subtract).then_inc(A["ol"], 1)

        def dve_mlp(dve, tl, a, r0):
            v, L = nc.vector, mlp[a]
            v.memset(Y2[:], 0.0)
            dve.drain()
            with dve.Fori(0, 2) as i:
                for n in range(16):
                    lo_ahead(dve, r0 + i * 8 + n // 4, n % 4)
                    dve.wait_ge(L["free"], RING + 16 * i + n + 1)
                    if n >= 2:
                        dve.wait_ge(L["hh"], 16 * i + n - 1)
                    v.tensor_tensor(f_sb[n % 2][:], t_sb[n % 2][:], t_sb[n % 2][:],
                                    ALU.mult).then_inc(L["sq"], 1)
                    dve.wait_ge(L["hh"], 16 * i + n + 1)
                    v.tensor_tensor(HL[:, n, :], f_sb[n % 2][:], HH[:, n, :].bitcast(F32),
                                    ALU.subtract).then_inc(L["hl"], 1)
                for n in range(16):
                    lo_ahead(dve, r0 + i * 8 + 4 + n // 4, n % 4)
                    if n % 2:
                        d = n // 2
                        dve.wait_ge(unit_done, RING * (r0 + i * 8 + 4 + n // 4) + n % 4 + 1)
                        v.tensor_tensor(Y2[:, d, :], Y2[:, d, :], bank(4 + d % 4), ALU.add).then_inc(L["acc"], 1)
            dve.drain()

        @block.vector
        def _(dve):
            tl = Tally()
            v = nc.vector
            dve.wait_ge(x_in, 16)
            dve.wait_ge(mod_used, MOD_UP)
            for c in range(2):
                v.tensor_tensor(MOD[:, 0:MOD_UP, c], bank(7, 2 * MOD_UP).rearrange("p (m c) -> p m c", c=2)[:, :, c],
                                col("b_mod", 0, MOD_UP), ALU.add)
            dve.drain()
            for c in range(2):
                v.scalar_tensor_tensor(gain[:, :, c], MOD[:, 8:16, c], 1.0, col("norm1_g", 0, 8),
                                       ALU.add, ALU.mult)
            dve_rinv(dve, tl, T)
            meet(dve, "dve", tl)
            dve_scaled(dve, tl, xk, KC, T, rhk, rlk)
            dve_rinv(dve, tl, TC)
            dve_scaled(dve, tl, lambda k: CX[:, k, :], KC, TC, lambda k: CH[:, k, :], lambda k: CL[:, k, :])
            for j in range(AHEAD):
                split_lo(dve, 0, j)
            meet(dve, "dve", tl)
            for j in range(RING):
                lo_ahead(dve, R_IN, j)
                if j == 2:
                    dve.wait_ge(unit_done, 3)
                    v.tensor_copy(ckvT[:, 0:T], bank(2))
                    v.tensor_copy(ckvT[:, T:KEYS], bank(5, TC))
                if j == 3:
                    dve.wait_ge(unit_done, 4)
                    v.tensor_tensor(t_sb[0][NOPE:QK], ps[NOPE:QK, 3, :], trig_sb[NOPE:QK], ALU.mult)
                    v.tensor_tensor(t_sb[1][NOPE:QK], ps[QK:P, 3, :], trig_sb[QK:P], ALU.mult)
                    dve.drain()
                    for m in range(2):
                        v.tensor_tensor(KT[m][NOPE:QK, 0:T], t_sb[0][NOPE:QK], t_sb[1][NOPE:QK], ALU.add)
                        v.tensor_copy(KT[m][NOPE:QK, T:KEYS], ps[NOPE:QK, 6, 0:TC])
                    dve.drain().then_inc(in_evac_d, 1)
            def taps(c, lo, hi):
                for t in range(lo, min(hi, CONV_W)):
                    w = pk[:, bass.ds(c * CONV_W + (_cols["conv_w"] + t), 1)]
                    y = ypad[:, c, t:t + T]
                    acc = f_sb[t % 2]
                    if t == 0:
                        dve.wait_ge(tap_done, 32 * c)
                        ins = v.tensor_scalar(acc[:], y, w, pk[:, bass.ds(c + _cols["conv_b"], 1)],
                                              ALU.mult, ALU.add)
                    elif t == 1:
                        ins = v.tensor_scalar(acc[:], y, w, None, ALU.mult)
                    else:
                        dve.wait_ge(tap_done, 32 * c + t - 1)
                        ins = v.scalar_tensor_tensor(acc[:], y, w, acc[:], ALU.mult, ALU.add)
                    ins.then_inc(tap_done, 1)

            def store_conv(c):
                dve.wait_ge(tap_done, 32 * c + CONV_W)
                v.tensor_tensor(ypad[:, c, 0:T], f_sb[0][:], f_sb[1][:], ALU.add).then_inc(tap_done, 1)

            def conv_round(i):
                for j in range(RING):
                    lo_ahead(dve, R_CONV + i, j)
                    if j % 2:
                        dve.wait_ge(sig_done, 2 * i + j // 2 + 1)
                        v.tensor_tensor(ypad[:, i * 2 + j // 2, HALF_W:HALF_W + T], bank(j - 1),
                                        sig[j // 2][:], ALU.mult).then_inc(glu_done, 1)
                    if not isinstance(i, int):
                        if j == 0:
                            dve.wait_ge(glu_done, i)
                        taps(i - 1, 8 * j, 8 * j + 8)
                if not isinstance(i, int):
                    store_conv(i - 1)

            conv_round(0)
            with dve.Fori(1, 4) as i:
                conv_round(i)
            dve.wait_ge(glu_done, KC)
            with dve.Fori(0, 3) as i:
                for j in range(RING):
                    lo_ahead(dve, R_GATE + i, j)
                    taps(i + 3, 8 * j, 8 * j + 8)
                store_conv(i + 3)
            for j in range(RING):
                lo_ahead(dve, R_GATE + 3, j)
            dve_rinv(dve, tl, T)
            dve_scaled(dve, tl, lambda k: cqT[:, k, :], 2, T, lambda k: CQH[:, k, :], lambda k: CQL[:, k, :])
            for lo, w in ((0, T), (T, TC)):
                dve_rinv(dve, tl, w)
                dve_scaled(dve, tl, lambda k: ckvT[:, lo:lo + w], 1, w, lambda k: CKH[:, lo:lo + w],
                           lambda k: CKL[:, lo:lo + w])
            meet(dve, "dve", tl)
            with dve.Fori(0, 2) as i:
                for pp in range(4):
                    p = i * 4 + pp
                    lo_ahead(dve, R_MLA + i, pp)

                    def queries(m):
                        dve.wait_ge(gen_done, 4 * p + 3 + m)
                        v.tensor_scalar(QT[m][0:NOPE], ps[0:NOPE, 7, :], SCALE1, None, ALU.mult)
                        v.scalar_tensor_tensor(t_sb[0][NOPE:QK], ps[NOPE:QK, 7, :], SCALE1,
                                               trig_sb[NOPE:QK], ALU.mult, ALU.mult)
                        v.scalar_tensor_tensor(t_sb[1][NOPE:QK], ps[QK:P, 7, :], SCALE1,
                                               trig_sb[QK:P], ALU.mult, ALU.mult)
                        dve.drain()
                        v.tensor_tensor(QT[m][NOPE:QK], t_sb[0][NOPE:QK], t_sb[1][NOPE:QK],
                                        ALU.add).then_inc(q_evac, 1)

                    def normalised(n):
                        dve.wait_ge(exp_done, 8 * p + n + 1)
                        v.reciprocal(rrow[:, n % 2:n % 2 + 1], psum_row[:, n % 2:n % 2 + 1])
                        dve.drain()
                        v.tensor_scalar(Pm[n % 3][:], Pm[n % 3][:], rrow[:, n % 2:n % 2 + 1], None,
                                        ALU.mult).then_inc(p_done, 1)

                    def low_part(p):
                        dve.wait_ge(o_hi, p + 1)
                        v.tensor_tensor(RL[:, p, :], bank(6), RH[:, p, :].bitcast(F32),
                                        ALU.subtract).then_inc(o_lo, 1)

                    dve.wait_ge(s_done, 8 * p)
                    queries(0)
                    if pp:
                        low_part(p - 1)
                    queries(1)
                    for n in range(8):
                        dve.wait_ge(s_done, 8 * p + n + 1)
                        v.tensor_reduce(nmax[:, n % 2:n % 2 + 1], bank(2 * (n % 2), KEYS), AX.X, ALU.max,
                                        negate=True).then_inc(max_done, 1)
                        if n:
                            normalised(n - 1)
                        taps(i + 6, 8 * pp + n, 8 * pp + n + 1)
                    normalised(7)
                    dve.wait_ge(mod_used, MOD_UP + 4 * p + 4)
                    for c in range(2):
                        ins = v.tensor_tensor(MOD[:, bass.ds(4 * p + MOD_UP, 4), c],
                                              bank(7, 8).rearrange("p (m c) -> p m c", c=2)[:, :, c],
                                              pk[:, bass.ds(4 * p + (_cols["b_mod"] + MOD_UP), 4)], ALU.add)
                    ins.then_inc(mod_evac, 1)
                    if pp == 3:
                        low_part(p)
                        store_conv(i + 6)
            meet(dve, "dve", tl)
            dve.wait_ge(gate_in, 16)
            for n in range(8):
                lo_ahead(dve, R_WO + n // 4, n % 4)
                dve.wait_ge(unit_done, RING * R_WO + n + 1)
                v.tensor_tensor(Mg[:, n, :], bank(n % 4), gate_sb[:, n, :], ALU.mult).then_inc(wo_evac, 1)
            yk = lambda k: ypad[:, k, 0:T]
            dve_centre(dve, tl, yk)
            dve_rinv(dve, tl, T)
            dve_scaled(dve, tl, yk, KC, T, lambda k: VH[:, k, :], lambda k: VL[:, k, :])
            meet(dve, "dve", tl)
            dve.wait_ge(gate_in, 32)
            for n in range(8):
                lo_ahead(dve, R_PW + n // 4, n % 4)
                dve.wait_ge(unit_done, RING * R_PW + n + 1)
                v.tensor_tensor(f_sb[0][:], bank(n % 4), gate_sb[:, n, :], ALU.mult)
                dve.drain()
                v.tensor_tensor(Mg[:, n, :], Mg[:, n, :], f_sb[0][:], ALU.add).then_inc(pw_evac, 1)
                dve.wait_ge(m_hi, n + 1)
                v.tensor_tensor(RL[:, n, :], Mg[:, n, :], RH[:, n, :].bitcast(F32), ALU.subtract)
            meet(dve, "dve", tl)
            for n in range(8):
                lo_ahead(dve, R_OUT + n // 4, n % 4)
                dve.wait_ge(unit_done, RING * R_OUT + n + 1)
                v.scalar_tensor_tensor(X[:, n, :], bank(n % 4), MOD[:, 16 + n, 0:1], X[:, n, :],
                                       ALU.mult, ALU.add).then_inc(out_evac, 1)
            v.scalar_tensor_tensor(gain[:, :, 0], MOD[:, 32:40, 0], 1.0, col("norm2_g", 0, 8), ALU.add, ALU.mult)
            meet(dve, "dve", tl)
            dve_rinv(dve, tl, T)
            dve_scaled(dve, tl, xk, KC, T, rhk, rlk)
            meet(dve, "dve", tl)
            dve_retrieve(dve, tl)
            meet(dve, "dve", tl)
            dve.wait_ge(e_tp, 4)
            iob = iota[:].unsqueeze(1).to_broadcast([P, 8, P])
            with dve.Fori(0, 16) as i:
                for s in range(4):
                    dve.wait_ge(g_mm, 8 * i + 2 * s)
                    for x in range(8):
                        t = 8 * s + x
                        v.tensor_scalar(A1[s % 2][:, x, :], iota[:], ET[0][:, bass.ds(i * 32 + t, 1)],
                                        ET[2][:, bass.ds(i * 32 + t, 1)], ALU.is_equal, ALU.mult)
                    e2 = ET[1][:, bass.ds(i * 32 + 8 * s, 8)].unsqueeze(2).to_broadcast([P, 8, P])
                    v.tensor_tensor(B1[s % 2][:], e2, iob, ALU.is_equal).then_inc(hot_done, 1)
            dve.wait_ge(mod_used, MODS)
            v.tensor_tensor(MOD2[:], bank(6, 96 * 2).rearrange("p (m c) -> p m c", c=2)[:, :, 0],
                            col("ada_b", 0, 96), ALU.add)
            meet(dve, "dve", tl)
            for b in range(2):
                dve.wait_ge(g_out[b], 16 * 8)
            v.memset(Y[:], 0.0)

            def dve_up(r, par, n, loads):
                dve.wait_ge(gl_in[par], 16 * loads)
                for c in range(RING):
                    lo_ahead(dve, r, c)
                    dve.wait_ge(ge_done, RING * n + c + 1)
                    gl = GL[par][:, :, 32 * c:32 * c + 32]
                    v.tensor_tensor(wf[c % 2][:].rearrange("p (b t) -> p b t", b=16),
                                    ge[c % 2][:].rearrange("p (b t) -> p b t", b=16), gl,
                                    ALU.mult).then_inc(w_done, 1)
                    dve.wait_ge(wh_done, RING * n + c + 1)
                    v.tensor_tensor(WL[par][:, c, :], wf[c % 2][:], WH[par][:, c, :].bitcast(F32),
                                    ALU.subtract).then_inc(wl_done, 1)

            def dve_down(r, n):
                split_lo(dve, r, 3)
                for h in range(2):
                    for d in range(8):
                        dve.wait_ge(acc_mm, 16 * n + 8 * h + d + 1)
                        dve.wait_ge(acc_done, 16 * n + h * (d + 1))
                        v.tensor_tensor(Y[:, d, :], Y[:, d, :], bank(4 + d % 4), ALU.add).then_inc(acc_done, 1)
                    if h == 0:
                        split_lo(dve, r + 1, 0)
                        split_lo(dve, r + 1, 1)
                split_lo(dve, r + 1, 2)

            dve_up(R_UV, 0, 0, 1)
            with dve.Fori(0, 15) as i:
                for b in range(2):
                    n = i * 2 + 1 + b
                    dve_up(R_UV + 1 + i * 4 + 2 * b, 1 - b, n, i + b + 1)
                    dve_down(R_UV + 2 + i * 4 + 2 * b, n - 1)
            dve_up(R_UV + 61, 1, 31, 16)
            dve_down(R_UV + 62, 30)
            dve_down(R_UV + 63, 31)
            dve.drain()
            for k in range(KC):
                v.scalar_tensor_tensor(X[:, k, :], Y[:, k, :], MOD[:, 40 + k, 0:1], X[:, k, :],
                                       ALU.mult, ALU.add)
            v.scalar_tensor_tensor(gain[:, :, 0], MOD2[:, 8:16], 1.0, col("final_g", 0, 8), ALU.add, ALU.mult)
            meet(dve, "dve", tl)
            dve_rinv(dve, tl, T)
            dve_scaled(dve, tl, xk, KC, T, rhk, rlk)
            meet(dve, "dve", tl)
            for k in range(KC):
                v.scalar_tensor_tensor(X[:, k, :], X[:, k, :], col("final_g", k), rinv[:],
                                       ALU.mult, ALU.mult)
            v.memset(relb[BUCKETS:BUCKETS + 1, :], NEG).then_inc(relb_made, 1)
            for n in range(8):
                lo_ahead(dve, R_DSA_IN + n // 4, n % 4)
            dve_rinv(dve, tl, T)
            dve_scaled(dve, tl, lambda k: kvT[:, k, :], 2, T, lambda k: KVH[:, k, :], lambda k: KVL[:, k, :])
            dve.wait_ge(iw_tp, 1)
            v.tensor_copy(IW[:].rearrange("p b h -> p (b h)"), bank(5, TB * IDX_H)).then_inc(iw_evac, 1)
            meet(dve, "dve", tl)
            for b in range(1, TB):
                w = (b + 1) * P
                for h in range(IDX_H):
                    n = (b - 1) * IDX_H + h
                    dve.wait_ge(ix_relu, n + 1)
                    if h == 0:
                        v.tensor_scalar(score[b][:, 0:w], sq[n % 2][:, 0:w], IW[:, b, h:h + 1], None,
                                        ALU.mult).then_inc(ix_add, 1)
                    else:
                        v.scalar_tensor_tensor(score[b][:, 0:w], sq[n % 2][:, 0:w], IW[:, b, h:h + 1],
                                               score[b][:, 0:w], ALU.mult, ALU.add).then_inc(ix_add, 1)
                    dve.wait_ge(ix_add, n + 1)
                dve.drain().then_inc(ix_scored, 1)
            dve.wait_ge(ix_masked, TB - 1)
            with dve.Fori(0, SEL // 8) as i:
                for b in range(1, TB):
                    v.max(top8[:, b, :], score[b][:, 0:(b + 1) * P])
                dve.drain()
                for b in range(1, TB):
                    v.match_replace(score[b][:, 0:(b + 1) * P], top8[:, b, :], score[b][:, 0:(b + 1) * P], TAKEN)
                dve.drain()
            for b in range(1, TB):
                v.tensor_scalar(M[b][:, 0:(b + 1) * P], score[b][:, 0:(b + 1) * P], TAKEN, NEG,
                                ALU.not_equal, ALU.mult)
            meet(dve, "dve", tl)
            dve_attention(dve, tl, 0)
            meet(dve, "dve", tl)
            dve_residual_norm(dve, tl, R_AWO, 0, 0, awo_evac)
            dve_mlp(dve, tl, 0, R_MLP1)
            dve_post(dve, tl, 0, 1)
            dve.wait_ge(lam_in, 16)
            for x in range(2):
                v.tensor_tensor(ss[0][:, 64 * x:64 * x + 64], lb_sb[:, 128 * x:128 * x + 64],
                                lb_sb[:, 128 * x + 64:128 * x + 128], ALU.mult)
            dve.drain()
            v.tensor_reduce(lam[:, 0:2], ss[0][:, 0:128].rearrange("p (a b) -> p a b", a=2), AX.X,
                            ALU.add).then_inc(lam_exp, 1)
            dve.wait_ge(lam_exp, 2)
            v.tensor_tensor(lam[:, 4:5], lam[:, 2:3], lam[:, 3:4], ALU.subtract)
            v.tensor_scalar(lam[:, 5:6], col("b_subln"), 1.0 - LAM_INIT, None, ALU.mult)
            dve.drain()
            v.tensor_scalar(lam[:, 4:5], lam[:, 4:5], LAM_INIT, None, ALU.add)
            dve.drain()
            dve_attention(dve, tl, 1)
            meet(dve, "dve", tl)
            dve_residual_norm(dve, tl, R_BWO, 1, 0, bwo_evac)
            dve_mlp(dve, tl, 1, R_MLP2)
            dve_post(dve, tl, 1, 1)

        def pe_post(pe, tl, layer, which):
            meet(pe, "pe", tl)
            if which == 1:
                for k in range(KC):
                    pe_mean(pe, tl, xk, k, made=True)
            pe_sums(pe, tl, KC, T)
            meet(pe, "pe", tl)

        def pe_attention(pe, tl, a):
            A, mm = att[a], nc.tensor.matmul
            r0, units = ((R_DSA, 2), (R_DIFF, 3))[a]
            body = 2 if a == 0 else 4
            turns, main = (8, 4)[a], slab(RH, RL)
            kv = slab(KVH, KVL, 0, 2)

            def unit(i, pp, x):
                return r0 + i * (units * body // 4) + (units * pp + x) // 4, (units * pp + x) % 4

            def first_units(i, pp):
                p = i * body + pp
                if a == 0:
                    if not (isinstance(p, int) and p == 0):
                        pe.wait_ge(A["q_ev"], p)
                    pe_unit(pe, *unit(i, pp, 0), 7, main).then_inc(unit_done, 1)
                else:
                    for x in range(2):
                        if not (isinstance(p, int) and p == 0):
                            pe.wait_ge(A["mx"], 8 * p - 1 + x)
                        pe_unit(pe, *unit(i, pp, x), 2 * x, main).then_inc(unit_done, 1)

            def pair(i, pp, last):
                p = i * body + pp
                if a == 0:
                    pe.wait_ge(A["mx"], 8 * p)
                    r, j = unit(i, pp, 1)
                    pe.wait_ge(lo_done, RING * r + j + 1)
                    product(j, (0, 1), bank(0), kv).then_inc(A["k_mm"], 1)
                    product(j, (2, 3), bank(2), kv).then_inc(unit_done, 1)
                else:
                    pe.wait_ge(A["rt"], p)
                    pe_unit(pe, *unit(i, pp, 2), 7, main).then_inc(unit_done, 1)
                pe.wait_ge(A["v_ev"], p + 1)
                pe.wait_ge(A["te"], turns * p)
                for c in range(TB):
                    ins = nc.tensor.transpose(bank(4)[:, c * P:(c + 1) * P],
                                              vT2[:, c * P:(c + 1) * P], ident[:])
                ins.then_inc(A["vt"], 1)

                def scores(n):
                    m, b = order(a)[n]
                    if n == 0:
                        pe.wait_ge(A["q_ev"], p + 1)
                        pe.wait_ge(A["k_ev"], p + 1)
                    if n >= 2:
                        pe.wait_ge(A["mx"], 8 * p + n - 1)
                    o, w = 64 * m, (b + 1) * P
                    mm(bank(2 * (n % 2), w), q2[o:o + 64, b * P:(b + 1) * P], k2[o:o + 64, 0:w],
                       start=True, stop=True).then_inc(A["s"], 1)

                def turn(x, src):
                    b = x % 4
                    pe.wait_ge(A["pd"], turns * p + x + 1)
                    if x == 0:
                        pe.wait_ge(A["vr"], p + 1)
                    if x >= 2:
                        pe.wait_ge(A["te"], turns * p + x - 1)
                    for c in range(b + 1):
                        ins = nc.tensor.transpose(bank(4 + x % 2)[:, c * P:(c + 1) * P],
                                                  src[:, c * P:(c + 1) * P], ident[:])
                    ins.then_inc(A["tp"], 1)

                def values(m):
                    pe.wait_ge(A["te"], turns * p + (4 * m + 4 if a == 0 else 4))
                    if m == 0:
                        pe.wait_ge(A["ol"] if a == 0 else A["oh"], p)
                        pe.wait_ge(A["vr"], p + 1)
                    rows = slice(64 * m, 64 * m + 64) if a == 0 else slice(0, P)
                    for c in range(TB):
                        ins = mm(ps[rows, 6, c * P:T], v2[:, c, rows], PT2[:, c, c * P:T],
                                 start=(c == 0), stop=(c == TB - 1))
                    ins.then_inc(A["pv"], 1)

                for n in range(8):
                    scores(n)
                    if a == 0 and n >= 2:
                        turn(n - 2, P2[(n - 2) % 4])
                    if a == 0 and n == 6:
                        values(0)
                    if a == 1 and n % 2 and n >= 3:
                        turn(n // 2 - 1, P2[(n - 3) % 4])
                if not last:
                    first_units(i, pp + 1)
                if a == 0:
                    turn(6, P2[2])
                    turn(7, P2[3])
                    values(1)
                else:
                    turn(3, P2[2])
                    values(0)
                    pe.wait_ge(A["osq"], p + 1)
                    mm(bank(7), ones[:], sq[0][:], start=True, stop=True).then_inc(A["oss"], 1)

            first_units(0, 0)
            with pe.Fori(0, PAIRS // body - 1) as i:
                for pp in range(body):
                    pair(i, pp, False)
            for pp in range(body):
                pair(PAIRS // body - 1, pp, pp == body - 1)

        def pe_mlp(pe, tl, a, r0):
            L, main = mlp[a], slab(RH, RL)
            with pe.Fori(0, 2) as i:
                for n in range(16):
                    pe.wait_ge(L["free"], 16 * i + n + 1)
                    pe_unit(pe, r0 + i * 8 + n // 4, n % 4, n % 4, main).then_inc(unit_done, 1)
                for n in range(16):
                    d, g = n // 2, n % 2
                    pe.wait_ge(L["hl"], 16 * i + 16) if n == 0 else None
                    if g == 0:
                        pe.wait_ge(L["acc"], 8 * i + max(d - 3, 0))
                    pe_unit(pe, r0 + i * 8 + 4 + n // 4, n % 4, 4 + d % 4, slab(HH, HL, 8 * g),
                            start=(g == 0), stop=(g == 1)).then_inc(unit_done, 1)

        @block.tensor
        def _(pe):
            tl = Tally()
            mm = nc.tensor.matmul
            pe.wait_ge(cvec_done, 1)
            for m in range(MOD_UP):
                if m % 4 == 0:
                    pe.wait_ge(up_in[m // 4], 16)
                pe_mod(pe, 0, 0, bank(7)[:, 2 * m:2 * m + 2], 0, mod_up[m // 8][:, m % 8])
                if m == 7:
                    pe.wait_ge(consts_made, 1)
                    pe_sums(pe, tl, KC, T)
            meet(pe, "pe", tl)
            pe_sums(pe, tl, KC, TC)
            meet(pe, "pe", tl)
            main = slab(RH, RL)
            for j in range(RING):
                u = pe_unit(pe, R_IN, j, j, main)
                if j >= 2:
                    u = product(j, range(8), bank(3 + j, TC), slab(CH, CL))
                u.then_inc(unit_done, 1)
            pe.wait_ge(in_evac_a, 2)
            pe.wait_ge(in_evac_d, 1)
            with pe.Fori(0, 4) as i:
                for j in range(RING):
                    pe.wait_ge(glu_done, 2 * i)
                    pe_unit(pe, R_CONV + i, j, j, main).then_inc(unit_done, 1)
            with pe.Fori(0, 4) as i:
                for j in range(RING):
                    pe.wait_ge(gate_free, RING * i + j + 1)
                    pe_unit(pe, R_GATE + i, j, j, main).then_inc(unit_done, 1)
            pe_sums(pe, tl, 2, T)
            pe_sums(pe, tl, 1, T)
            pe_sums(pe, tl, 1, TC)
            meet(pe, "pe", tl)
            cq = slab(CQH, CQL, 0, 2)

            def generated(i, pp):
                p = i * 4 + pp
                pe.wait_ge(lo_done, RING * (R_MLA + i) + pp + 1)
                for x in range(2):
                    b = 2 * x
                    pe.wait_ge(exp_done, 8 * p - 1 + x if pp else 8 * p)
                    product(pp, (4 + x,), bank(b), [(CKH[:, 0:T], CKL[:, 0:T])])
                    product(pp, (4 + x,), bank(b + 1, TC),
                            [(CKH[:, T:KEYS], CKL[:, T:KEYS])]).then_inc(gen_done, 1)

            def first_queries(i, pp):
                pe.wait_ge(mod_evac, i * 4 + pp)
                product(pp, (0, 1), bank(7), cq).then_inc(gen_done, 1)

            with pe.Fori(0, 2) as i:
                for pp in range(4):
                    p = i * 4 + pp
                    if pp == 0:
                        generated(i, 0)
                        first_queries(i, 0)
                    pe.wait_ge(q_evac, 2 * p + 1)
                    product(pp, (2, 3), bank(7), cq).then_inc(gen_done, 1)
                    pe.wait_ge(v_evac, p + 1)
                    pe.wait_ge(tp_evac, 8 * p)
                    for c in range(6):
                        ins = nc.tensor.transpose(bank(4, KEYS)[:, c * P:(c + 1) * P],
                                                  VT[:, c * P:(c + 1) * P], ident[:])
                        if c == 0:
                            ins.then_inc(unit_done, 1)
                    ins.then_inc(vt_done, 1)

                    def scores(n):
                        m, b = n // 4, n % 4
                        if n == 0:
                            pe.wait_ge(k_evac, p + 1)
                            pe.wait_ge(q_evac, 2 * p + 1)
                        elif n == 4:
                            pe.wait_ge(q_evac, 2 * p + 2)
                        if n >= 2:
                            pe.wait_ge(exp_done, 8 * p + n - 1)
                        q = QT[m][0:QK, b * P:(b + 1) * P]
                        o = 2 * (n % 2)
                        mm(bank(o), q, KT[m][0:QK, 0:T], start=True, stop=True)
                        mm(bank(o + 1, TC), q, KT[m][0:QK, T:KEYS], start=True, stop=True).then_inc(s_done, 1)

                    def turn(n):
                        pe.wait_ge(p_done, 8 * p + n + 1)
                        if n == 0:
                            pe.wait_ge(v_ready, p + 1)
                        else:
                            pe.wait_ge(tp_evac, 8 * p + n)
                        for c in range(6):
                            ins = nc.tensor.transpose(bank(4, KEYS)[:, c * P:(c + 1) * P],
                                                      Pm[n % 3][:, c * P:(c + 1) * P], ident[:])
                        ins.then_inc(tp_done, 1)

                    def values(m):
                        pe.wait_ge(tp_evac, 8 * p + 4 * m + 4)
                        if m == 0:
                            pe.wait_ge(o_lo, p)
                        for c in range(6):
                            ins = mm(ps[VD * m:VD * m + VD, 6, :], Vk[:, c, VD * m:VD * m + VD],
                                     PT[:, c, :], start=(c == 0), stop=(c == 5))
                        ins.then_inc(pv_done, 1)

                    for n in range(8):
                        scores(n)
                        if n >= 2:
                            turn(n - 2)
                        if 1 <= n <= 4:
                            pe.wait_ge(q_evac, 2 * p + 2)
                            pe_mod(pe, 2 * p + (n - 1) // 2 + 1, (n - 1) % 2,
                                   bank(7)[:, 2 * n - 2:2 * n], 0)
                        if n == 6:
                            values(0)
                    turn(6)
                    if pp < 3:
                        generated(i, pp + 1)
                    turn(7)
                    if pp < 3:
                        first_queries(i, pp + 1)
                    values(1)
            meet(pe, "pe", tl)
            pe_dense8(pe, R_WO, wo_evac, main)
            pe.wait_ge(wo_evac, 8)
            yk = lambda k: ypad[:, k, 0:T]
            pe_means(pe, tl, yk)
            pe_sums(pe, tl, KC, T)
            meet(pe, "pe", tl)
            pe_dense8(pe, R_PW, pw_evac, slab(VH, VL))
            meet(pe, "pe", tl)
            pe_dense8(pe, R_OUT, out_evac, main)
            meet(pe, "pe", tl)
            pe_sums(pe, tl, KC, T)
            meet(pe, "pe", tl)
            pe.wait_ge(keys_in, 16)
            with pe.Fori(0, 4) as i:
                for j in range(RING):
                    pe.wait_ge(q_ready, 4 * i + max(j - 3, 0))
                    pe_unit(pe, R_PQ + i, j, j, main).then_inc(unit_done, 1)
                    for x in range(3):
                        pe_mod(pe, 2 * i + ((3 * j + x) // 6 + 1), (3 * j + x) % 6,
                               ps[:, 6, bass.ds(24 * i + (6 * j + 2 * x), 2)], 2)
                    pe.wait_ge(q_ready, 4 * i + j + 1)
                    pe.wait_ge(sc_used, 4 * i + max(j - 1, 0))
                    for b in range(TB):
                        ins = mm(bank(4 + j % 2)[:, b * P:(b + 1) * P], qs[j % 2][:, b * P:(b + 1) * P],
                                 SK[:, i * 4 + j, :], start=True, stop=True)
                    ins.then_inc(sc_done, 1)
            meet(pe, "pe", tl)
            for m in range(3):
                for b in range(TB):
                    ins = nc.tensor.transpose(bank(m)[:, b * P:(b + 1) * P],
                                              E[m][:, b].rearrange("p h k -> p (h k)"), ident[:])
                ins.then_inc(e_tp, 1)
            pe.drain().then_inc(g_mm, 2)
            with pe.Fori(0, 8) as i:
                for s in range(16):
                    pe.wait_ge(hot_done, 8 * i + s // 2 + 1)
                    pe.wait_ge(g_evac, 16 * i + max(s - 3, 0))
                    for x in range(4):
                        k = 4 * (s % 2) + x
                        ins = mm(bank(s % 4)[:, x * P:(x + 1) * P], A1[s // 2 % 2][:, k, :],
                                 B1[s // 2 % 2][:, k, :], start=True, stop=True)
                    ins.then_inc(g_mm, 1)
                    if s % 2 and s < 12:
                        x = s // 2
                        pe_mod(pe, i + 9, x,
                               ps[:, 6, bass.ds(12 * i + (96 + 2 * x), 2)], 2)
            meet(pe, "pe", tl)

            def up(r, n):
                for c in range(RING):
                    pe.wait_ge(ge_done, RING * n + c - 3) if not isinstance(n, int) or n else None
                    pe_unit(pe, r, c, c, main).then_inc(unit_done, 1)

            def down(r, par, n):
                pe.wait_ge(wl_done, RING * n + RING)
                for h in range(2):
                    pe.wait_ge(lo_done, RING * r + 2 * h + 2)
                    for d in range(8):
                        x = 8 * h + d
                        if x >= 4:
                            pe.wait_ge(acc_done, 16 * n + x - 3)
                        else:
                            pe.wait_ge(acc_done, 16 * n)
                        for c in (2 * h, 2 * h + 1):
                            ins = product(c, (d,), bank(4 + d % 4), [(WH[par][:, c, :], WL[par][:, c, :])],
                                          start=(c == 2 * h), stop=(c == 2 * h + 1))
                        ins.then_inc(acc_mm, 1)
                    pe.drain().then_inc(unit_done, 2)

            up(R_UV, 0)
            with pe.Fori(0, 15) as i:
                for b in range(2):
                    up(R_UV + 1 + i * 4 + 2 * b, i * 2 + 1 + b)
                    down(R_UV + 2 + i * 4 + 2 * b, b, i * 2 + b)
            up(R_UV + 61, 31)
            down(R_UV + 62, 0, 30)
            down(R_UV + 63, 1, 31)
            meet(pe, "pe", tl)
            pe_sums(pe, tl, KC, T)
            meet(pe, "pe", tl)
            for n in range(8):
                pe_unit(pe, R_DSA_IN + n // 4, n % 4, n, main).then_inc(unit_done, 1)
            pe.wait_ge(ix_evac, 8)
            pe_sums(pe, tl, 2, T)
            for b in range(TB):
                ins = nc.tensor.transpose(bank(5)[:, b * IDX_H:(b + 1) * IDX_H],
                                          iwT[0:IDX_H, b * P:(b + 1) * P], ident[0:IDX_H, 0:IDX_H])
            ins.then_inc(iw_tp, 1)
            pe.wait_ge(bias_tables, 32)
            pe.wait_ge(relb_made, 1)
            mm(ps[0:HEADS, 6, :], relb[:], hotz[:, 0:T], start=True, stop=True)
            mm(ps[0:HEADS, 7, 0:BIAS_Z - T], relb[:], hotz[:, T:BIAS_Z], start=True,
               stop=True).then_inc(bias_mm, 1)
            meet(pe, "pe", tl)
            for b in range(1, TB):
                for h in range(IDX_H):
                    n = (b - 1) * IDX_H + h
                    if n >= 4:
                        pe.wait_ge(ix_relu, n - 3)
                    o = 64 * (h % 2)
                    mm(bank(n % 4, (b + 1) * P), iqT[o:o + 64, h // 2, b * P:(b + 1) * P],
                       ikT[o:o + 64, 0:(b + 1) * P], start=True, stop=True).then_inc(ix_mm, 1)
            meet(pe, "pe", tl)
            pe_attention(pe, tl, 0)
            meet(pe, "pe", tl)
            pe_dense8(pe, R_AWO, awo_evac, slab(OH, OL), tl)
            pe_post(pe, tl, 0, 0)
            pe_mlp(pe, tl, 0, R_MLP1)
            pe_post(pe, tl, 0, 1)
            pe_attention(pe, tl, 1)
            meet(pe, "pe", tl)
            pe_dense8(pe, R_BWO, bwo_evac, slab(OH, OL), tl)
            pe_post(pe, tl, 1, 0)
            pe_mlp(pe, tl, 1, R_MLP2)
            pe_post(pe, tl, 1, 1)

    return nc


def rope_tables():
    rows = T // GRID_W
    r = np.repeat(np.arange(rows), GRID_W)
    c = np.tile(np.arange(GRID_W), rows)
    n = ROPE // 4
    freq = np.float32(10000.0) ** (-np.arange(n, dtype=np.float32) / np.float32(n))
    table = np.zeros((P, T), np.float32)
    for d in range(ROPE):
        ang = (r if d < ROPE // 2 else c).astype(np.float32) * freq[d % n]
        table[NOPE + d] = np.cos(ang)
        table[QK + d] = np.sin(ang) * (-1.0 if d % (2 * n) < n else 1.0)
    return table


def bias_one_hot():
    d = T - 1 - np.arange(BIAS_Z)
    exact = BUCKETS // 2
    n = np.maximum(d, 0)
    large = exact + (np.log(np.maximum(n, 1).astype(np.float32) / np.float32(exact)).astype(np.float32)
                     / np.float32(np.log(128 / exact)) * np.float32(BUCKETS - exact)).astype(np.int32)
    b = np.where(n < exact, n, np.minimum(large, BUCKETS - 1))
    b = np.where(d < 0, BUCKETS, b)
    return (np.arange(BUCKETS + 1)[:, None] == b[None, :]).astype(np.float32)


def kernel(**inputs):
    import concourse.bacc as bacc
    from concourse.bass_utils import run_bass_kernel_spmd

    a = {k: np.asarray(v) for k, v in inputs.items()}

    def tiles(w):
        n = w.shape[1] // P
        return w.reshape(8, P, n, P).transpose(2, 1, 0, 3)

    def zeros(*shape):
        return np.zeros(shape, np.float32)

    w_in = a["w_in"][0]
    swap = np.arange(ROPE) ^ (ROPE // 4)
    kr = w_in[:, 384:384 + ROPE]
    stream = [tiles(w_in[:, 0:384]), tiles(np.concatenate([zeros(D, NOPE), kr, kr[:, swap]], 1))]
    conv = tiles(w_in[:, 416:416 + 2 * D])
    stream.append(np.stack([conv[0:8], conv[8:16]], 1).reshape(16, P, 8, P))
    stream.append(tiles(w_in[:, 416 + 2 * D:416 + 4 * D]))
    uq = a["w_uq"][0].reshape(2, P, HEADS, QK)
    uq = np.concatenate([uq, uq[..., NOPE:][..., swap]], -1)
    ukv = a["w_ukv"][0].reshape(P, PAIRS, 2, NOPE + VD)
    pair = [uq[:, :, 0::2].transpose(2, 1, 0, 3), uq[:, :, 1::2].transpose(2, 1, 0, 3),
            ukv[..., 0:NOPE].reshape(P, PAIRS, 1, P).transpose(1, 0, 2, 3),
            ukv[..., NOPE:].reshape(P, PAIRS, 1, P).transpose(1, 0, 2, 3), zeros(PAIRS, P, 2, P)]
    stream.append(np.concatenate(pair, 2))
    stream += [tiles(a[n][0]) for n in ("w_o_mla", "w_pw", "w_out", "w_pq")]
    up = a["u_experts"][0].reshape(P, P, 8, P).transpose(1, 3, 2, 0)
    down = a["v_experts"][0].reshape(P, P, 8, P).transpose(1, 0, 2, 3)
    up, down = (x.reshape(CHUNK_ROUNDS, RING, P, 8, P) for x in (up, down))
    stream.append(up[0])
    for n in range(1, CHUNK_ROUNDS):
        stream += [up[n], down[n - 1]]
    stream.append(down[-1])
    wa = a["a_w_in_2"][0]
    ik = wa[:, 1792:1856]
    stream.append(tiles(np.concatenate([wa[:, 1024:1792], ik, ik, wa[:, 1856:1864], zeros(D, P - 8)], 1)))
    uk = a["a_w_uk_2"][0].reshape(PAIRS, 2, 64, 2, P).transpose(0, 4, 3, 1, 2).reshape(PAIRS, P, 2, P)
    uv = a["a_w_uv_2"][0].reshape(PAIRS, 2, 2, P, 64).transpose(0, 3, 2, 1, 4).reshape(PAIRS, P, 2, P)
    ukuv = np.concatenate([uk, uv, zeros(PAIRS, P, 4, P)], 2)
    stream.append(np.stack([tiles(wa[:, 0:D]), ukuv], 1).reshape(16, P, 8, P))
    stream.append(tiles(a["a_w_o_2"][0]))

    def mlp_units(layer):
        w1, w2 = a["mlp_w1_2"][layer], a["mlp_w2_2"][layer]
        parts = []
        for half in range(2):
            h = slice(half * 2048, (half + 1) * 2048)
            parts.append(tiles(w1[:, h]))
            x = w2[h].reshape(2, 8, P, 8, P)
            parts.append(x.transpose(3, 0, 2, 1, 4).reshape(16, P, 8, P))
        return parts

    stream += mlp_units(0)
    wb = a["b_w_in_2"][0]
    stream.append(np.stack([tiles(wb[:, D * x:D * (x + 1)]) for x in (1, 2, 0)], 1).reshape(24, P, 8, P))
    stream.append(tiles(a["b_w_o_2"][0]))
    stream += mlp_units(1)
    stream.append(zeros(RING, P, 8, P))
    w_all = np.concatenate(stream, 0).reshape(-1, P, 8 * P)
    assert w_all.shape[0] == RING * (ROUNDS + 1), w_all.shape

    w_mods = np.concatenate([tiles(a["w_mod"][0]), tiles(a["ada_w_2"][0]), tiles(a["ada_w_2"][1])], 0)
    w_mods = w_mods.reshape(MODS, P, 8 * P)

    def cols(v):
        return np.ascontiguousarray(v.reshape(-1, P).T)

    cs = [a["c"].reshape(8, P), a["c_ctx"].reshape(8, P), a["c_2"].reshape(8, P), a["c_2"].reshape(8, P)]
    parts = [np.stack(cs, -1).transpose(1, 0, 2).reshape(P, 32), cols(a["b_mod"]), cols(a["ada_b_2"]),
             cols(a["norm1_g"]), cols(a["norm2_g"]), cols(a["q_norm_g"]), cols(a["kv_norm_g"]),
             a["conv_w"][0].reshape(CONV_W, 8, P).transpose(2, 1, 0).reshape(P, 8 * CONV_W),
             cols(a["conv_b"]), cols(a["conv_ln_g"]), cols(a["conv_ln_b"]), cols(a["final_g"]),
             cols(a["ln_g_2"]), cols(a["ln_b_2"]), cols(a["a_kv_norm_2"]), cols(a["b_subln_2"])]
    pack = np.concatenate(parts, 1)
    arrays = {
        "w_all": w_all, "w_mods": w_mods,
        "x_t": a["x"][0].T.reshape(8, P, T).transpose(1, 0, 2),
        "ctx_t": a["ctx"][0].T.reshape(8, P, TC).transpose(1, 0, 2),
        "pack": pack, "trig": rope_tables(),
        "sub_keys_t": a["sub_keys"][0].reshape(16, NK, P).transpose(2, 0, 1),
        "rel_bias": a["rel_bias_2"], "bias_hot": bias_one_hot(),
        "b_lambda": a["b_lambda_2"].reshape(1, 256),
    }
    arrays = {k: np.ascontiguousarray(v) for k, v in arrays.items()}
    nc = bacc.Bacc("TRN2", target_bir_lowering=False, num_devices=1)
    aps = [nc.dram_tensor(k, v.shape, F32, kind="ExternalInput").ap() for k, v in arrays.items()]
    out = nc.dram_tensor("out_t", [P, KC, T], F32, kind="ExternalOutput").ap()
    build(nc, *aps, out)
    r = run_bass_kernel_spmd(nc, [arrays], core_ids=[0])
    got = np.asarray(r.results[0]["out_t"])
    return np.ascontiguousarray(got.transpose(1, 0, 2).reshape(D, T).T).reshape(1, T, D)
```
